# Optimizing a Trainium2 kernel written in Bass

```python
import jax, jax.numpy as jnp
from jax import lax
import numpy as np

D_MODEL = 1024
BATCH = 1
SEQ = 512
DEPTH = 1

CHUNK = 64
Q_BLOCK = 128
NORM_EPS = 1e-6
MASK_VALUE = -1e30
TINY = 1e-30

MIX_WIDTH = D_MODEL
HGRN_HEADS = 4
HGRN_WIDTH = MIX_WIDTH // 4
HGRN_KEY_DIM = HGRN_WIDTH // HGRN_HEADS
HGRN_VAL_DIM = HGRN_WIDTH // HGRN_HEADS
POOL_WINDOWS = (2, 4, 8, 16)
POOL_GROUPS = len(POOL_WINDOWS)
POOL_WIDTH = MIX_WIDTH // 4
POOL_GROUP_DIM = POOL_WIDTH // POOL_GROUPS
FOX_HEADS = 8
FOX_WIDTH = MIX_WIDTH // 2
FOX_HEAD_DIM = FOX_WIDTH // FOX_HEADS

IN_WIDTHS = (HGRN_WIDTH, HGRN_WIDTH, HGRN_WIDTH, HGRN_WIDTH,
             POOL_WIDTH, POOL_WIDTH,
             FOX_WIDTH, FOX_WIDTH, FOX_WIDTH, FOX_WIDTH, FOX_HEADS)
IN_WIDTH = int(sum(IN_WIDTHS))
IN_SPLIT_POINTS = tuple(int(v) for v in np.cumsum(IN_WIDTHS)[:-1])


def _rmsnorm(x, g):
    xf = x.astype(jnp.float32)
    y = xf * lax.rsqrt(jnp.mean(xf * xf, axis=-1, keepdims=True) + NORM_EPS)
    return (y * g.astype(jnp.float32)).astype(x.dtype)

def _hgrn2_chunkwise(q, k, v, log_f):
    B, T, H, dk = q.shape
    dv = v.shape[-1]
    n = T // CHUNK

    def to_chunks(a):
        return a.astype(jnp.float32).reshape(B, n, CHUNK, H, a.shape[-1]).transpose(1, 0, 3, 2, 4)

    qc, kc, vc, gc = to_chunks(q), to_chunks(k), to_chunks(v), to_chunks(log_f)
    pos = jnp.arange(CHUNK)
    causal = (pos[:, None] >= pos[None, :])[:, :, None]
    causal_f = causal.astype(jnp.float32)

    def step(S, inp):
        qi, ki, vi, gi = inp
        b = jnp.cumsum(gi, axis=2)
        diff = b[:, :, :, None, :] - b[:, :, None, :, :]
        decay = jnp.exp(jnp.where(causal, diff, 0.0)) * causal_f
        attn = jnp.einsum('bhtd,bhsd,bhtsd->bhts', qi, ki, decay)
        o = (jnp.einsum('bhts,bhsv->bhtv', attn, vi)
             + jnp.einsum('bhtd,bhdv->bhtv', qi * jnp.exp(b), S))
        b_last = b[:, :, -1, :]
        S = (jnp.exp(b_last)[..., None] * S
             + jnp.einsum('bhsd,bhsv->bhdv', ki * jnp.exp(b_last[:, :, None, :] - b), vi))
        return S, o

    S0 = jnp.zeros((B, H, dk, dv), jnp.float32)
    _, o = lax.scan(step, S0, (qc, kc, vc, gc))
    return o.transpose(1, 0, 3, 2, 4).reshape(B, T, H, dv)

def _multiscale_pool(u):
    B, T, _ = u.shape
    uf = u.astype(jnp.float32).reshape(B, T, POOL_GROUPS, POOL_GROUP_DIM)
    cs = jnp.pad(jnp.cumsum(uf, axis=1), ((0, 0), (1, 0), (0, 0), (0, 0)))
    t = jnp.arange(T, dtype=jnp.float32)
    outs = []
    for g, w in enumerate(POOL_WINDOWS):
        c = cs[:, :, g]
        upper = c[:, 1:]
        lower = jnp.pad(c[:, :T + 1 - w], ((0, 0), (w - 1, 0), (0, 0)))
        count = jnp.minimum(t + 1.0, float(w))[None, :, None]
        outs.append((upper - lower) / count - uf[:, :, g])
    return jnp.stack(outs, axis=2)

def _forgetting_attention(q, k, v, log_f):
    B, T, H, D = q.shape
    c = jnp.cumsum(log_f, axis=1).transpose(0, 2, 1)
    scale = D ** -0.5
    outs = []
    for i in range(T // Q_BLOCK):
        q0, q1 = i * Q_BLOCK, (i + 1) * Q_BLOCK
        s = jnp.einsum('bqhd,bkhd->bhqk', q[:, q0:q1], k[:, :q1]).astype(jnp.float32) * scale
        mask = (q0 + jnp.arange(Q_BLOCK))[:, None] >= jnp.arange(q1)[None, :]
        bias = jnp.where(mask, c[:, :, q0:q1, None] - c[:, :, None, :q1], 0.0)
        p = jax.nn.softmax(jnp.where(mask, s + bias, MASK_VALUE), axis=-1)
        outs.append(jnp.einsum('bhqk,bkhd->bqhd', p.astype(v.dtype), v[:, :q1]))
    return jnp.concatenate(outs, axis=1)

def first_inputs(seed: int = 0) -> dict:
    key = jax.random.key(seed)
    ks = jax.random.split(key, 11)
    f32 = jnp.float32
    x = jax.random.normal(ks[0], (BATCH, SEQ, D_MODEL), f32)
    lower_bounds = jax.random.normal(ks[1], (DEPTH, HGRN_WIDTH), f32)
    pre_norm_g = 1.0 + 0.05 * jax.random.normal(ks[2], (DEPTH, D_MODEL), f32)
    w_in = jax.random.normal(ks[3], (DEPTH, D_MODEL, IN_WIDTH), f32) * D_MODEL ** -0.5
    hgrn_norm_g = 1.0 + 0.05 * jax.random.normal(ks[4], (DEPTH, HGRN_WIDTH), f32)
    fox_f_bias = jax.random.uniform(ks[5], (DEPTH, FOX_HEADS), f32, minval=1.0, maxval=4.0)
    pool_w = jax.random.normal(ks[6], (DEPTH, POOL_GROUPS, POOL_GROUP_DIM, POOL_GROUP_DIM), f32) * POOL_GROUP_DIM ** -0.5
    pool_scale = jax.random.uniform(ks[7], (DEPTH, POOL_WIDTH), f32, minval=0.5, maxval=1.5)
    w_out = jax.random.normal(ks[8], (DEPTH, MIX_WIDTH, D_MODEL), f32) * MIX_WIDTH ** -0.5
    post_norm_g = 1.0 + 0.05 * jax.random.normal(ks[9], (DEPTH, D_MODEL), f32)
    return {"x": x, "lower_bounds": lower_bounds, "pre_norm_g": pre_norm_g, "w_in": w_in,
            "hgrn_norm_g": hgrn_norm_g, "fox_f_bias": fox_f_bias, "pool_w": pool_w,
            "pool_scale": pool_scale, "w_out": w_out, "post_norm_g": post_norm_g}

def first_block(x, lower_bounds, pre_norm_g, w_in, hgrn_norm_g, fox_f_bias, pool_w, pool_scale, w_out, post_norm_g):
    B, T, _ = x.shape
    p = jax.nn.softmax(lower_bounds.astype(jnp.float32), axis=0)
    lbs = jnp.cumsum(p, axis=0) - p[0]
    for l in range(DEPTH):
        h = _rmsnorm(x, pre_norm_g[l])
        proj = jnp.einsum('btd,de->bte', h, w_in[l])
        q_a, f_a, i_a, g_a, u_b, g_b, q_c, k_c, v_c, g_c, f_c = jnp.split(proj, IN_SPLIT_POINTS, axis=-1)

        lb = lbs[l]
        z = f_a.astype(jnp.float32)
        f_gate = lb + (1.0 - lb) * jax.nn.sigmoid(z)
        log_f_a = jnp.log(jnp.maximum(f_gate, TINY))
        k_a = (1.0 - lb) * jax.nn.sigmoid(-z)
        hshape = (B, T, HGRN_HEADS, HGRN_KEY_DIM)
        o_a = _hgrn2_chunkwise(jax.nn.silu(q_a).reshape(hshape), k_a.reshape(hshape),
                               i_a.reshape(B, T, HGRN_HEADS, HGRN_VAL_DIM), log_f_a.reshape(hshape))
        o_a = _rmsnorm(o_a, hgrn_norm_g[l].reshape(HGRN_HEADS, HGRN_VAL_DIM)).reshape(B, T, HGRN_WIDTH)
        o_a = o_a.astype(x.dtype) * jax.nn.silu(g_a)

        pooled = _multiscale_pool(u_b)
        o_b = jnp.einsum('btgc,gcd->btgd', pooled, pool_w[l].astype(jnp.float32)).reshape(B, T, POOL_WIDTH)
        o_b = (o_b * pool_scale[l].astype(jnp.float32)).astype(x.dtype) * jax.nn.silu(g_b)

        log_f_c = jax.nn.log_sigmoid((f_c + fox_f_bias[l]).astype(jnp.float32))
        fshape = (B, T, FOX_HEADS, FOX_HEAD_DIM)
        o_c = _forgetting_attention(q_c.reshape(fshape), k_c.reshape(fshape), v_c.reshape(fshape), log_f_c)
        o_c = o_c.reshape(B, T, FOX_WIDTH).astype(x.dtype) * jax.nn.silu(g_c)

        mixed = jnp.concatenate([o_a, o_b, o_c], axis=-1)
        y = jnp.einsum('bte,ed->btd', mixed, w_out[l])
        x = x + _rmsnorm(y, post_norm_g[l])
    return x


RWKV_HEAD = 64
RWKV_HEADS = D_MODEL // RWKV_HEAD
RWKV_DIM = RWKV_HEADS * RWKV_HEAD
DECAY_LORA = 64
ICLR_LORA = 64
GATE_LORA = 160
GN_EPS = 64e-5
RWKV_SPLIT = (RWKV_DIM, RWKV_DIM, RWKV_DIM, DECAY_LORA, ICLR_LORA, GATE_LORA)
RWKV_COLS = sum(RWKV_SPLIT)

NSA_HEAD = 64
NSA_HEADS = D_MODEL // NSA_HEAD
NSA_GROUPS = 4
NSA_HPG = NSA_HEADS // NSA_GROUPS
NSA_KV = NSA_GROUPS * NSA_HEAD
CMP_BLOCK = 32
CMP_STRIDE = 16
CMP_HIDDEN = 128
SLC_BLOCK = 64
N_SELECT = 16
WINDOW = 512
NSA_SPLIT = (NSA_HEADS * NSA_HEAD,) + (NSA_KV,) * 6 + (3 * NSA_HEADS,)
NSA_COLS = sum(NSA_SPLIT)

GATE_COLS = 2 * D_MODEL
IN_COLS = RWKV_COLS + NSA_COLS + GATE_COLS

D_FF = ((8 * D_MODEL // 3 + 255) // 256) * 256
CONV_W = 3

NEG_INF = -1e30
FORCE = 1e9


def rms_norm(x, g):
    xf = x.astype(jnp.float32)
    y = xf * lax.rsqrt(jnp.mean(xf * xf, axis=-1, keepdims=True) + NORM_EPS)
    return (y * g.astype(jnp.float32)).astype(x.dtype)

def masked_softmax(s, mask, axis):
    s = jnp.where(mask, s, NEG_INF)
    e = jnp.where(mask, jnp.exp(s - jnp.max(s, axis=axis, keepdims=True)), 0.0)
    return e / jnp.maximum(jnp.sum(e, axis=axis, keepdims=True), TINY)

def alibi_slopes():
    h = jnp.arange(1, NSA_HEADS + 1, dtype=jnp.float32)
    return jnp.exp2(-8.0 * h / NSA_HEADS).reshape(NSA_GROUPS, NSA_HPG)

def split_cols(z, widths):
    return jnp.split(z, [int(c) for c in np.cumsum(widths)[:-1]], axis=-1)

def wkv7_scan(r, w, k, v, a, b):
    B, _, H, N = r.shape

    def step(state, inp):
        r_t, w_t, k_t, v_t, a_t, b_t = inp
        sa = jnp.einsum('bhvk,bhk->bhv', state, a_t)
        state = (state * w_t[:, :, None, :] + sa[..., None] * b_t[:, :, None, :]
                 + v_t[..., None] * k_t[:, :, None, :])
        return state, jnp.einsum('bhvk,bhk->bhv', state, r_t)

    tm = lambda t: jnp.moveaxis(t, 1, 0)
    state0 = jnp.zeros((B, H, N, N), jnp.float32)
    _, y = lax.scan(step, state0, (tm(r), tm(w), tm(k), tm(v), tm(a), tm(b)))
    return jnp.moveaxis(y, 0, 1)

def rwkv7_time_mix(z, mu, w0, w2, a0, a2, g2, k_k, k_a, r_k, ln_w, ln_b):
    B, S, _ = z.shape
    f32 = jnp.float32
    prev = jnp.pad(z, ((0, 0), (1, 0), (0, 0)))[:, :-1]
    z = z + (prev - z) * mu
    r, k, v, wd, ad, gd = split_cols(z, RWKV_SPLIT)
    w_log = -jax.nn.softplus(-(w0 + jnp.tanh(wd) @ w2)) - 0.5
    decay = jnp.exp(-jnp.exp(w_log.astype(f32)))
    a = jax.nn.sigmoid(a0 + ad @ a2)
    g = jax.nn.sigmoid(gd) @ g2
    heads = lambda t: t.reshape(B, S, RWKV_HEADS, RWKV_HEAD).astype(f32)
    kk = heads(k * k_k)
    kk = kk / jnp.maximum(jnp.sqrt(jnp.sum(kk * kk, axis=-1, keepdims=True)), 1e-12)
    k = k * (1.0 + (a - 1.0) * k_a)
    r_h, k_h, v_h, a_h = heads(r), heads(k), heads(v), heads(a)
    y = wkv7_scan(r_h, heads(decay), k_h, v_h, -kk, kk * a_h)
    mean = jnp.mean(y, axis=-1, keepdims=True)
    var = jnp.mean(jnp.square(y - mean), axis=-1, keepdims=True)
    y = ((y - mean) * lax.rsqrt(var + GN_EPS)).reshape(B, S, RWKV_DIM)
    y = y * ln_w.astype(f32) + ln_b.astype(f32)
    bonus = jnp.sum(r_h * k_h * r_k.astype(f32), axis=-1, keepdims=True) * v_h
    y = y + bonus.reshape(B, S, RWKV_DIM)
    return (y * g.astype(f32)).astype(z.dtype)

def nsa_attention(z, cmp_pos_k, cmp_w1_k, cmp_w2_k, cmp_pos_v, cmp_w1_v, cmp_w2_v):
    B, S, _ = z.shape
    f32 = jnp.float32
    G, HG, DH = NSA_GROUPS, NSA_HPG, NSA_HEAD
    q, kc, vc, ks, vs, kw, vw, gl = split_cols(z, NSA_SPLIT)
    q = (q.astype(f32) * DH ** -0.5).reshape(B, S, G, HG, DH).transpose(0, 2, 3, 1, 4)
    gates = jax.nn.sigmoid(gl.astype(f32)).reshape(B, S, G, HG, 3).transpose(0, 2, 3, 1, 4)
    kv = lambda t: t.astype(f32).reshape(B, S, G, DH).transpose(0, 2, 1, 3)

    n_cmp = (S - CMP_BLOCK) // CMP_STRIDE + 1
    cidx = np.arange(n_cmp)[:, None] * CMP_STRIDE + np.arange(CMP_BLOCK)[None, :]

    def compress(t, pos, w1, w2):
        blk = kv(t)[:, :, cidx] + pos.astype(f32)
        hid = jax.nn.gelu(blk.reshape(B, G, n_cmp, CMP_BLOCK * DH) @ w1.astype(f32))
        return hid @ w2.astype(f32)

    k_cmp = compress(kc, cmp_pos_k, cmp_w1_k, cmp_w2_k)
    v_cmp = compress(vc, cmp_pos_v, cmp_w1_v, cmp_w2_v)
    cmp_end = jnp.asarray(cidx[:, -1], jnp.int32)
    cmp_mid = jnp.asarray(cidx.mean(axis=1), jnp.float32)

    n_sel = S // SLC_BLOCK
    top = min(N_SELECT, n_sel)
    k_slc = kv(ks).reshape(B, G, n_sel, SLC_BLOCK, DH)
    v_slc = kv(vs).reshape(B, G, n_sel, SLC_BLOCK, DH)
    r1, r2 = SLC_BLOCK // CMP_STRIDE, CMP_BLOCK // CMP_STRIDE
    off = np.array([m - n for m in range(r1) for n in range(r2)])
    imap_np = np.arange(n_sel)[:, None] * r1 + off[None, :]
    imap_ok = jnp.asarray((imap_np >= 0) & (imap_np < n_cmp))
    imap = jnp.asarray(np.clip(imap_np, 0, n_cmp - 1), jnp.int32)
    bi = jnp.arange(B)[:, None, None, None]
    gi = jnp.arange(G)[None, :, None, None]

    k_win = jnp.pad(kv(kw), ((0, 0), (0, 0), (WINDOW, 0), (0, 0)))
    v_win = jnp.pad(kv(vw), ((0, 0), (0, 0), (WINDOW, 0), (0, 0)))

    slopes = alibi_slopes()[None, :, :, None, None]

    def block(i):
        t0 = i * Q_BLOCK
        qb = lax.dynamic_slice_in_dim(q, t0, Q_BLOCK, axis=3)
        gb = lax.dynamic_slice_in_dim(gates, t0, Q_BLOCK, axis=3)
        t = t0 + jnp.arange(Q_BLOCK, dtype=jnp.int32)
        tf = t.astype(f32)

        s_c = jnp.einsum('bghtd,bgnd->bghtn', qb, k_cmp) - slopes * (tf[:, None] - cmp_mid[None, :])
        p_c = masked_softmax(s_c, cmp_end[None, :] <= t[:, None], -1)
        o_c = jnp.einsum('bghtn,bgnd->bghtd', p_c, v_cmp)

        imp_c = jnp.sum(p_c, axis=2)
        imp = jnp.sum(jnp.where(imap_ok, imp_c[..., imap], 0.0), axis=-1)
        cur = (t // SLC_BLOCK)[:, None]
        jb = jnp.arange(n_sel, dtype=jnp.int32)[None, :]
        forced = (jb == 0) | (jb == cur) | (jb == cur - 1)
        score = jnp.where(jb <= cur, jnp.where(forced, FORCE, imp), NEG_INF)
        vals, idx = lax.top_k(score, top)
        kg = k_slc[bi, gi, idx]
        vg = v_slc[bi, gi, idx]
        pos = idx[..., None] * SLC_BLOCK + jnp.arange(SLC_BLOCK, dtype=jnp.int32)
        dist_s = t[:, None, None] - pos
        mask_s = ((vals > 0.5 * NEG_INF)[..., None] & (dist_s >= 0))[:, :, None]
        s_s = (jnp.einsum('bghtd,bgtnld->bghtnl', qb, kg)
               - slopes[..., None] * dist_s.astype(f32)[:, :, None])
        p_s = masked_softmax(s_s, mask_s, (-2, -1))
        o_s = jnp.einsum('bghtnl,bgtnld->bghtd', p_s, vg)

        kwb = lax.dynamic_slice_in_dim(k_win, t0, Q_BLOCK + WINDOW, axis=2)
        vwb = lax.dynamic_slice_in_dim(v_win, t0, Q_BLOCK + WINDOW, axis=2)
        spos = t0 - WINDOW + jnp.arange(Q_BLOCK + WINDOW, dtype=jnp.int32)
        dist_w = t[:, None] - spos[None, :]
        mask_w = (spos[None, :] >= 0) & (dist_w >= 0) & (dist_w < WINDOW)
        s_w = jnp.einsum('bghtd,bgsd->bghts', qb, kwb) - slopes * dist_w.astype(f32)
        p_w = masked_softmax(s_w, mask_w, -1)
        o_w = jnp.einsum('bghts,bgsd->bghtd', p_w, vwb)

        return gb[..., 0:1] * o_c + gb[..., 1:2] * o_s + gb[..., 2:3] * o_w

    out = lax.map(block, jnp.arange(S // Q_BLOCK, dtype=jnp.int32))
    out = out.transpose(1, 0, 4, 2, 3, 5).reshape(B, S, NSA_HEADS * DH)
    return out.astype(z.dtype)

def causal_dwconv(u, w, b):
    C = u.shape[-1]
    y = lax.conv_general_dilated(u, w[:, None, :].astype(u.dtype), window_strides=(1,),
                                 padding=[(CONV_W - 1, 0)],
                                 dimension_numbers=('NWC', 'WIO', 'NWC'),
                                 feature_group_count=C)
    return y + b

def second_inputs(seed: int = 0) -> dict:
    key = jax.random.key(seed)
    ks = jax.random.split(key, 32)
    f32 = jnp.float32
    L = DEPTH
    nrm = lambda k, shape, scale: jax.random.normal(k, shape, f32) * scale
    gain = lambda k, n: 1.0 + 0.05 * jax.random.normal(k, (L, n), f32)
    return {
        "x": jax.random.normal(ks[0], (BATCH, SEQ, D_MODEL), f32),
        "norm_mix_pre": gain(ks[1], D_MODEL),
        "norm_mix_post": gain(ks[2], D_MODEL),
        "norm_ffn_pre": gain(ks[3], D_MODEL),
        "norm_ffn_post": gain(ks[4], D_MODEL),
        "w_in": nrm(ks[5], (L, D_MODEL, IN_COLS), D_MODEL ** -0.5),
        "rwkv_mu": jax.random.uniform(ks[6], (L, RWKV_COLS), f32),
        "rwkv_w0": jax.random.uniform(ks[7], (L, RWKV_DIM), f32, minval=-6.0, maxval=0.0),
        "rwkv_w2": nrm(ks[8], (L, DECAY_LORA, RWKV_DIM), DECAY_LORA ** -0.5),
        "rwkv_a0": nrm(ks[9], (L, RWKV_DIM), 0.1),
        "rwkv_a2": nrm(ks[10], (L, ICLR_LORA, RWKV_DIM), ICLR_LORA ** -0.5),
        "rwkv_g2": nrm(ks[11], (L, GATE_LORA, RWKV_DIM), GATE_LORA ** -0.5),
        "rwkv_k_k": 0.85 + nrm(ks[12], (L, RWKV_DIM), 0.05),
        "rwkv_k_a": 1.0 + nrm(ks[13], (L, RWKV_DIM), 0.05),
        "rwkv_r_k": nrm(ks[14], (L, RWKV_HEADS, RWKV_HEAD), 0.1),
        "rwkv_ln_w": gain(ks[15], RWKV_DIM),
        "rwkv_ln_b": nrm(ks[16], (L, RWKV_DIM), 0.02),
        "cmp_pos_k": nrm(ks[17], (L, CMP_BLOCK, NSA_HEAD), 0.1),
        "cmp_w1_k": nrm(ks[18], (L, CMP_BLOCK * NSA_HEAD, CMP_HIDDEN), (CMP_BLOCK * NSA_HEAD) ** -0.5),
        "cmp_w2_k": nrm(ks[19], (L, CMP_HIDDEN, NSA_HEAD), CMP_HIDDEN ** -0.5),
        "cmp_pos_v": nrm(ks[20], (L, CMP_BLOCK, NSA_HEAD), 0.1),
        "cmp_w1_v": nrm(ks[21], (L, CMP_BLOCK * NSA_HEAD, CMP_HIDDEN), (CMP_BLOCK * NSA_HEAD) ** -0.5),
        "cmp_w2_v": nrm(ks[22], (L, CMP_HIDDEN, NSA_HEAD), CMP_HIDDEN ** -0.5),
        "w_branch_rwkv": nrm(ks[23], (L, RWKV_DIM, D_MODEL), RWKV_DIM ** -0.5),
        "w_branch_nsa": nrm(ks[24], (L, NSA_HEADS * NSA_HEAD, D_MODEL), (NSA_HEADS * NSA_HEAD) ** -0.5),
        "w_out": nrm(ks[25], (L, D_MODEL, D_MODEL), D_MODEL ** -0.5),
        "ffn_up": nrm(ks[26], (L, D_MODEL, 2 * D_FF), D_MODEL ** -0.5),
        "ffn_conv_w": nrm(ks[27], (L, CONV_W, 2 * D_FF), CONV_W ** -0.5),
        "ffn_conv_b": nrm(ks[28], (L, 2 * D_FF), 0.02),
        "ffn_down": nrm(ks[29], (L, D_FF, D_MODEL), D_FF ** -0.5),
    }

def second_block(x, norm_mix_pre, norm_mix_post, norm_ffn_pre, norm_ffn_post, w_in,
              rwkv_mu, rwkv_w0, rwkv_w2, rwkv_a0, rwkv_a2, rwkv_g2, rwkv_k_k, rwkv_k_a,
              rwkv_r_k, rwkv_ln_w, rwkv_ln_b,
              cmp_pos_k, cmp_w1_k, cmp_w2_k, cmp_pos_v, cmp_w1_v, cmp_w2_v,
              w_branch_rwkv, w_branch_nsa, w_out,
              ffn_up, ffn_conv_w, ffn_conv_b, ffn_down):
    for l in range(DEPTH):
        h = rms_norm(x, norm_mix_pre[l])
        z = h @ w_in[l]
        z_rwkv, z_nsa, z_gate = jnp.split(z, [RWKV_COLS, RWKV_COLS + NSA_COLS], axis=-1)
        o_a = rwkv7_time_mix(z_rwkv, rwkv_mu[l], rwkv_w0[l], rwkv_w2[l], rwkv_a0[l],
                             rwkv_a2[l], rwkv_g2[l], rwkv_k_k[l], rwkv_k_a[l],
                             rwkv_r_k[l], rwkv_ln_w[l], rwkv_ln_b[l])
        o_b = nsa_attention(z_nsa, cmp_pos_k[l], cmp_w1_k[l], cmp_w2_k[l],
                            cmp_pos_v[l], cmp_w1_v[l], cmp_w2_v[l])
        g_a, g_b = jnp.split(jax.nn.sigmoid(z_gate), 2, axis=-1)
        m = g_a * (o_a @ w_branch_rwkv[l]) + g_b * (o_b @ w_branch_nsa[l])
        x = x + rms_norm(m @ w_out[l], norm_mix_post[l])
        h = rms_norm(x, norm_ffn_pre[l])
        u = causal_dwconv(h @ ffn_up[l], ffn_conv_w[l], ffn_conv_b[l])
        u_gate, u_val = jnp.split(u, 2, axis=-1)
        x = x + rms_norm((jax.nn.silu(u_gate) * u_val) @ ffn_down[l], norm_ffn_post[l])
    return x


def setup_inputs(seed=0):
    out = dict(first_inputs(seed))
    for name, value in second_inputs(seed + 1).items():
        if name != "x":
            out[name + "_2"] = value
    return out


def reference(
    x, lower_bounds, pre_norm_g, w_in, hgrn_norm_g, fox_f_bias, pool_w, pool_scale, w_out,
    post_norm_g, norm_mix_pre_2, norm_mix_post_2, norm_ffn_pre_2, norm_ffn_post_2, w_in_2,
    rwkv_mu_2, rwkv_w0_2, rwkv_w2_2, rwkv_a0_2, rwkv_a2_2, rwkv_g2_2, rwkv_k_k_2, rwkv_k_a_2,
    rwkv_r_k_2, rwkv_ln_w_2, rwkv_ln_b_2, cmp_pos_k_2, cmp_w1_k_2, cmp_w2_k_2, cmp_pos_v_2,
    cmp_w1_v_2, cmp_w2_v_2, w_branch_rwkv_2, w_branch_nsa_2, w_out_2, ffn_up_2, ffn_conv_w_2,
    ffn_conv_b_2, ffn_down_2,
):
    x = first_block(
        x, lower_bounds, pre_norm_g, w_in, hgrn_norm_g, fox_f_bias, pool_w, pool_scale, w_out,
        post_norm_g,
    )
    return second_block(
        x, norm_mix_pre_2, norm_mix_post_2, norm_ffn_pre_2, norm_ffn_post_2, w_in_2, rwkv_mu_2,
        rwkv_w0_2, rwkv_w2_2, rwkv_a0_2, rwkv_a2_2, rwkv_g2_2, rwkv_k_k_2, rwkv_k_a_2,
        rwkv_r_k_2, rwkv_ln_w_2, rwkv_ln_b_2, cmp_pos_k_2, cmp_w1_k_2, cmp_w2_k_2, cmp_pos_v_2,
        cmp_w1_v_2, cmp_w2_v_2, w_branch_rwkv_2, w_branch_nsa_2, w_out_2, ffn_up_2,
        ffn_conv_w_2, ffn_conv_b_2, ffn_down_2,
    )


_drawn_inputs = setup_inputs


def setup_inputs(seed=0):
    import zlib

    import numpy as np

    out = dict(_drawn_inputs(seed))
    spreads = {}
    factors = {'rwkv_a0_2': 2.791, 'rwkv_ln_b_2': 4.801, 'cmp_pos_k_2': 8.0, 'ffn_conv_b_2': 4.124}
    for name, (base, spread) in spreads.items():
        noise = np.random.default_rng([zlib.crc32(name.encode()), seed]).standard_normal(out[name].shape)
        drawn = base * np.exp(spread * noise) if base else spread * noise
        out[name] = __import__('jax').numpy.asarray(drawn.astype(out[name].dtype))
    for name, factor in factors.items():
        out[name] = (out[name] * factor).astype(out[name].dtype)
    return out
```

```python
import concourse.bass as bass
from concourse import mybir
from contextlib import ExitStack

FP32 = mybir.dt.float32
ALU = mybir.AluOpType
ACT = mybir.ActivationFunctionType
AX = mybir.AxisListType

P = 128
T = 512
TT = T // P
D = 1024
KT = D // P
DH = 64
EPS = 1e-6
TINY = 1e-30
BIG_NEG = -1e30
BANKS = 6
FOX_HEADS = 8
RWKV_COLS = 3360
NSA_COLS = 2608
NSA_HEADS, NSA_GROUPS = 16, 4
D_FF = 2816
FF_TILES = D_FF // P
CMP_N = 31
LOG_DECAY = -0.6065306597126334
MID = 38.8
ARENA = 43200

PCOLS = {}


def _pack(names):
    at = 0
    for name, n in names:
        PCOLS[name] = (at, n)
        at += n
    return at


N_PCOLS = _pack([("pre_norm", KT), ("mix_pre", KT), ("ffn_pre", KT), ("hgrn_norm", 2), ("pool_scale", 2),
                 ("fox_bias", 1), ("mu_rkv", 24), ("mu_lora", 3), ("w0", KT), ("a0", KT), ("k_k", KT),
                 ("k_a", KT), ("r_k", KT), ("conv_w", 3 * 2 * FF_TILES), ("conv_b", 2 * FF_TILES)])
CCOLS = {"ident": (0, 128), "head_ones": (128, 128), "dist": (256, 512), "mask": (768, 512)}
N_CCOLS = 1280


def build_program(nc, d, x_saved, out):
    with ExitStack() as ctx:
        sems = {}

        def sem(name):
            if name not in sems:
                sems[name] = ctx.enter_context(nc.semaphore(name))
            return sems[name]

        def tensor(name, words):
            return ctx.enter_context(nc.sbuf_tensor(name, [P, words], FP32))

        const = tensor("const", N_CCOLS)
        par = tensor("par", N_PCOLS)
        stat = tensor("stat", 256)
        ring = tensor("ring", 2 * 4096)
        arena = tensor("arena", ARENA)
        bank = [ctx.enter_context(nc.psum_tensor(f"bank{b}", [P, 512], FP32)) for b in range(8)]

        def view(at, *dims):
            n = 1
            for x in dims:
                n *= x
            assert at + n <= ARENA, (at, dims)
            v = arena[:, at:at + n]
            if len(dims) == 2:
                v = v.rearrange("p (a b) -> p a b", a=dims[0])
            elif len(dims) == 3:
                v = v.rearrange("p (a b c) -> p a b c", a=dims[0], b=dims[1])
            elif len(dims) == 4:
                v = v.rearrange("p (a b c e) -> p a b c e", a=dims[0], b=dims[1], c=dims[2])
            return v

        def params(name, k=0, parts=P):
            at = PCOLS[name][0] + k
            return par[0:parts, at:at + 1]

        def cst(name):
            at, n = CCOLS[name]
            return const[:, at:at + n]

        def over(ap, n):
            return ap.unsqueeze(1).broadcast_to([P, n, ap.shape[1]])

        def along(ap, n):
            return ap.unsqueeze(2).broadcast_to([P, ap.shape[1], n])

        ident, head_ones = cst("ident"), cst("head_ones")
        dist, causal = cst("dist"), cst("mask")

        x_tok = view(0, TT, D)
        h_t = view(4096, KT, T)
        S0 = 8192
        mix_t = view(S0, KT, T)
        at = S0 + 4096
        q_a, f_a, k_a, i_a, silu_ga, u_b, silu_gb = (view(at + 1024 * n, 2, T) for n in range(7))
        y_tok1 = view(at, TT, D)
        gain1 = view(at + 4096, D)
        at += 7168
        q_c, k_c, silu_gc, v_c = (view(at + 2048 * n, *((4, T) if n < 3 else (TT, 512))) for n in range(4))
        at += 8192
        sig = view(at, 2, T)
        at += 1024
        fc_x = view(at, T)
        at += 512
        pool_w = view(at, 2, P)
        fc_w = view(at + 256, KT, 8)
        at += 320
        z_sel = view(at, 192)
        inv_count = view(at + 192, 2, T)
        at += 1216
        pool_pad = view(at, 2, 528)
        pool_s = view(at + 1056, 2, 528)
        at += 2112
        hg_u = view(at, 3, T)
        at += 1536
        norm_1 = view(at, TT, D)
        sel_b = view(at, DH, P)
        fox_o = view(at, TT, 512)
        fox_att = at + 2048
        sel8 = view(at + 5120, 8, P)
        fc_abs, fc_e, fc_ls, fc_neg = (view(at + 6144 + 512 * n, T) for n in range(4))
        at += 8192
        assert at <= ARENA, at
        hg_kv = view(4096, 3, T)
        hg_s = view(4096 + 1536, 2, T)
        hg_sq = view(4096 + 2560, 2, T)
        oa_t = view(S0, KT, T)
        norm_2 = view(S0 + 4096, TT, D)
        at = S0 + 4096
        lo_wa, lo_g1, lo_g2 = view(at, T), view(at + 512, T), view(at + 1024, T)
        at += 1536
        lora_w, g2_a, g2_b = view(at, D), view(at + 1024, D), view(at + 2048, D)
        at += 3072
        m_gram, m_low, m_blk = view(at, 512), view(at + 512, P), view(at + 640, P)
        m_e = view(at + 768, 3, P)
        m_reset, head_sel = view(at + 1152, T), view(at + 1664, 2)
        at += 1666 + 2
        a_r = view(at, 2, TT, 2, P)
        b_h, k_h = view(at + 2048, 2, T), view(at + 3072, 2, T)
        at += 4096
        v_tok, b_tok, k_tok = (view(at + 1024 * n, TT, 256) for n in range(3))
        at += 3072
        bonus, last_p = view(at, 16), view(at + 16, 8)
        state = view(at + 24, 2, P)
        rhs_b, sa_b = view(at + 280, 256), view(at + 536, 256)
        st_tmp = view(at + 792, 256)
        at += 1048
        gram = view(at, TT, 4, 512)
        inv, invt = (view(at + 8192 + 2048 * n, TT, 4, P) for n in range(2))
        low, pw = view(0, TT, 4, P), view(2048, TT, 4, P)
        pwt = gram[:, :, :, 0:P]
        r_q, k_q, v_q, lw_q, b_q, pm_q, pi_q, pp_q, av_q, kk_q, t1_q, t2_q = (
            view(1024 * n if n < 4 else at + 1024 * (n - 4), 2, T) for n in range(12))
        z_pad = view(at + 8192, 2, 514)
        z_d = view(at + 8192 + 1028, 2, T)
        y_q, g_q, t3_q = (view(1024 * n, TT, 256) for n in range(3))
        ln_q = view(3072, 2, 256)
        at = S0 + 4096
        q_n = view(at, KT, T)
        ob_t = q_n
        at += 4096
        k_s, k_w = view(at, 2, T), view(at + 1024, 2, T)
        v_s, v_w = view(at + 2048, TT, 256), view(at + 3072, TT, 256)
        at += 4096
        xk, xv = view(at, 4, T), view(at + 2048, 4, T)
        at += 4096
        gates, gl_w = view(at, TT, 48), view(at + 192, KT, 48)
        at += 576
        w1k, w1v = view(at, 16, P), view(at + 2048, 16, P)
        at += 4096
        w2k, w2v, pos_k, pos_v = view(at, DH), view(at + 64, DH), view(at + 128, 16), view(at + 144, 16)
        at += 160
        hb, hx, h2, hid_k, hid_v = (view(at, 2), view(at + 2, 124), view(at + 126, 124),
                                    view(at + 250, 4, 32), view(at + 378, 4, 32))
        hs = view(at + 506, 124)
        at += 630
        hid4 = view(at, 4, 4, 32)
        k_cmp = view(at + 512, 2, 32)
        at += 576
        v_bd = view(at, 4, 4, DH)
        at += 1024
        c_bias, c_01, v_mask = view(at, TT, 16 * 32), view(at + 2048, TT, 32), view(at + 2176, 4)
        at += 2180
        tab = view(at, 2, T)
        at += 1024
        nsa_att = at
        at += 3072
        c_sc, c_pt = view(at, 2, 512), view(at + 1024, 2, 512)
        at += 2048
        assert at <= ARENA, at
        nsa_o = view(0, TT, D)
        at = S0 + 8192
        sig_a, sig_b = view(at, 4, T), view(at + 2048, 4, T)
        m_t = view(at + 4096, KT, T)
        m_tmp = view(at + 8192, 2, T)
        y_tok2 = view(at + 9216, TT, D)
        gain2 = view(at + 9216 + 4096, D)
        assert at + 9216 + 5120 <= ARENA
        act_t = view(S0, FF_TILES, T)
        at = S0 + FF_TILES * T
        ff_pad = view(at, 4, 514)
        ff_c = view(at + 2056, 4, T)
        ff_s = view(at + 2056 + 2048, 2, T)
        at += 2056 + 3072
        norm_3 = view(at, TT, D)
        y_tok3 = norm_3
        gain3 = view(at + 4096, D)
        assert at + 5120 <= ARENA

        base = {}
        total = [0]

        def jobs(name, n):
            base[name] = total[0]
            total[0] += n

        def attention_jobs(name, units):
            order = {}
            for s in range(units + 2):
                for kind, u in (("S", s), ("T", s - 1), ("V", s - 2)):
                    if 0 <= u < units:
                        order[kind, u] = total[0]
                        total[0] += 1
            base[name] = order

        jobs("n1", KT)
        jobs("p1", 29)
        jobs("hg", 2 * DH)
        jobs("hn", 2)
        jobs("pool", 2)
        attention_jobs("fox", FOX_HEADS * TT)
        jobs("ft", 4)
        jobs("y1", 8)
        jobs("n2", KT)
        jobs("lora", 3)
        for q in range(4):
            jobs(("ra", q), 19)
            jobs(("rb", q), 104)
            jobs(("rc", q), 19)
        jobs("np", 25)
        jobs("cmp", 24)
        attention_jobs("nsa", NSA_HEADS * TT * 2)
        jobs("nt", KT)
        jobs("merge", 32)
        jobs("y2", 8)
        jobs("n3", KT)
        jobs("ff", 44)
        jobs("y3", 8)

        full = [sem(f"bank_full{b}") for b in range(BANKS)]
        free = [sem(f"bank_free{b}") for b in range(BANKS)]

        def ps(j):
            return bank[j % BANKS][:, :]

        def wait_full(eng, j):
            eng.wait_ge(full[j % BANKS], j // BANKS + 1)

        def wait_read(eng, j):
            eng.wait_ge(free[j % BANKS], j // BANKS + 1)

        def claim(pe, j):
            if j >= BANKS:
                pe.wait_ge(free[j % BANKS], j // BANKS)

        def cols(w, a, b):
            return w.rearrange("(k p) c -> p k c", p=P)[:, :, a:b]

        stream = []

        def slot(n):
            return ring[:, (n % 2) * 4096:(n % 2) * 4096 + 4096]

        def slot_k(n, width=512):
            return slot(n)[:, 0:KT * width].rearrange("p (k c) -> p k c", k=KT)

        w_at = {}

        def add_use(name, parts, last):
            n = len(stream)
            w_at[name] = n
            loads = []
            for a, src in parts:
                loads.append((slot_k(n)[:, 0:src.shape[1], a:a + src.shape[2]], src))
            stream.append((loads, last))

        for n in range(7):
            add_use(("p1", n), [(0, cols(d["w_in"], 512 * n, 512 * n + 512))], ("job", base["p1"] + 4 * n + 3))
        for n in range(2):
            add_use(("y1", n), [(0, cols(d["w_out"], 512 * n, 512 * n + 512))], ("job", base["y1"] + 7))
        w2 = d["w_in_2"]
        add_use("lora", [(0, cols(w2, 3072, RWKV_COLS))], ("job", base["lora"] + 2))
        for q in range(4):
            add_use(("rk", q), [(0, cols(w2, 256 * q, 256 * q + 256)),
                                (256, cols(w2, 1024 + 256 * q, 1280 + 256 * q))], ("job", base["ra", q] + 3))
            add_use(("v", q), [(0, cols(w2, 2048 + 256 * q, 2304 + 256 * q))], ("job", base["ra", q] + 5))
        nb = RWKV_COLS
        for n in range(2):
            parts = []
            for half in range(2):
                for hg in range(4):
                    a = nb + (2 * n + half) * 256 + hg * DH
                    parts.append((hg * P + half * DH, cols(w2, a, a + DH)))
            add_use(("q", n), parts, ("job", base["np"] + 4 * n + 3))
        for n in range(3):
            a = nb + 1024 + 512 * n
            add_use(("kv", n), [(0, cols(w2, a, a + 512))], ("job", base["np"] + (11, 17, 23)[n]))
        zg = RWKV_COLS + NSA_COLS
        for hf in range(2):
            for m, src in enumerate((cols(w2, zg + 512 * hf, zg + 512 * hf + 512),
                                     cols(w2, zg + D + 512 * hf, zg + D + 512 * hf + 512),
                                     cols(d["w_branch_rwkv_2"], 512 * hf, 512 * hf + 512),
                                     cols(d["w_branch_nsa_2"], 512 * hf, 512 * hf + 512))):
                add_use(("merge", hf, m), [(0, src)], ("job", base["merge"] + 16 * hf + 4 * m + 3))
        for n in range(2):
            add_use(("y2", n), [(0, cols(d["w_out_2"], 512 * n, 512 * n + 512))], ("job", base["y2"] + 7))
        for n in range(11):
            add_use(("ff", n), [(0, cols(d["ffn_up_2"], 256 * n, 256 * n + 256)),
                                (256, cols(d["ffn_up_2"], D_FF + 256 * n, D_FF + 256 * n + 256))],
                    ("job", base["ff"] + 4 * n + 3))
        DOWN = [(0, 8), (8, 16), (16, 22)]
        down_reads = 0
        for hf in range(2):
            for n, (a, b) in enumerate(DOWN):
                src = d["ffn_down_2"][a * P:b * P, 512 * hf:512 * hf + 512].rearrange("(k p) c -> p k c", p=P)
                if n < 2:
                    down_reads += 1
                add_use(("y3", hf, n), [(0, src)],
                        ("down", down_reads) if n < 2 else ("job", base["y3"] + 4 * hf + 3))
        slot_loads = []
        for n, (loads, _) in enumerate(stream):
            slot_loads.append(16 * len(loads) + (slot_loads[n - 2] if n >= 2 else 0))
        w_loaded = [sem("w_loaded0"), sem("w_loaded1")]
        down_read = sem("down_read")

        def weights(pe, name):
            n = w_at[name]
            pe.wait_ge(w_loaded[n % 2], slot_loads[n])
            return slot_k(n)

        phase_done = sem("phase_done")

        def counter():
            count = [0]

            def join(eng):
                count[0] += 1
                eng.drain().then_inc(phase_done, 1)
                eng.wait_ge(phase_done, 4 * count[0])
            return join

        x_in, x_out = sem("x_in"), sem("x_out")
        load_total = {}

        def phase_loads(act, name, pairs):
            for dst, src in pairs:
                act.dma_start(dst, src).then_inc(sem("loaded_" + name), 16)

        def plan_loads(name, pairs):
            load_total[name] = 16 * len(pairs)
            return pairs

        def have(eng, name, times=1):
            eng.wait_ge(sem("loaded_" + name), load_total[name] * times)

        L_START = plan_loads("start", [(const[:, :], d["c_stay"]), (par[:, :], d["c_par"]),
                                       (fc_w, cols(d["w_in"], 3584, 3592)), (pool_w, d["c_pool_w"]),
                                       (z_sel, d["c_z_sel"]), (inv_count, d["c_inv_count"])])
        L_SEL = plan_loads("sel", [(sel_b, d["c_sel_b"])])
        L_FOX = plan_loads("fox", [(sel8[0:8], d["c_sel8"])])
        L_Y1 = plan_loads("y1", [(gain1, d["g_post"])])
        L_RW = plan_loads("rwkv", [(lora_w, d["c_lora_w"]), (g2_a, d["rwkv_g2_2"][0:128, :]),
                                   (g2_b[0:32], d["rwkv_g2_2"][128:160, :]),
                                   (view(S0 + 4096 + 4608, 1666), d["c_rwkv"])])
        L_LN = [plan_loads("ln", [(ln_q[:, 0, :], d["g_ln_w"][:, 256 * q:256 * q + 256]),
                                       (ln_q[:, 1, :], d["g_ln_b"][:, 256 * q:256 * q + 256])])
                for q in range(4)]
        L_NSA = plan_loads("nsa", [(gl_w, cols(w2, RWKV_COLS + 2560, RWKV_COLS + 2608)),
                                   (w1k, d["cmp_w1_k_2"].rearrange("(j p) m -> p j m", p=P)),
                                   (w1v, d["cmp_w1_v_2"].rearrange("(j p) m -> p j m", p=P)),
                                   (w2k, d["cmp_w2_k_2"]), (w2v, d["cmp_w2_v_2"]),
                                   (pos_k, d["c_pos_k"]), (pos_v, d["c_pos_v"]),
                                   (c_bias, d["c_cmp_bias"]), (c_01, d["c_cmp_01"]), (v_mask, d["c_v_mask"])])
        L_Y2 = plan_loads("y2", [(x_tok, x_saved.rearrange("(i p) c -> p i c", p=P)), (gain2, d["g_mix_post"])])
        L_Y3 = plan_loads("y3", [(gain3, d["g_ffn_post"])])

        SILU = ([(n, q_a[:, n, :]) for n in (0, 1)] + [(6 + n, silu_ga[:, n, :]) for n in (0, 1)]
                + [(10 + n, silu_gb[:, n, :]) for n in (0, 1)] + [(24 + n, silu_gc[:, n, :]) for n in range(4)])
        SILU_NO = {n: s for s, (n, _) in enumerate(SILU)}
        SILU_OUT = dict(SILU)

        def nsa_place(h):
            g, hg = h // 4, h % 4
            return slice((g % 2) * DH, (g % 2) * DH + DH), (g // 2) * 4 + hg

        def fox_units():
            units = []
            for h in range(FOX_HEADS):
                half, tile = slice((h % 2) * DH, (h % 2) * DH + DH), h // 2
                for i in range(TT):
                    w = (i + 1) * P
                    units.append((q_c[half, tile, i * P:(i + 1) * P], k_c[half, tile, 0:w],
                                  (sel8[0:8, h, :], fc_neg[0:8, 0:w]),
                                  [v_c[:, x, h * DH:(h + 1) * DH] for x in range(i + 1)], fox_att))
            return units

        def nsa_units():
            units = []
            for h in range(NSA_HEADS):
                half, tile = nsa_place(h)
                g = h // 4
                for i in range(TT):
                    w = (i + 1) * P
                    for k, v in ((k_s, v_s), (k_w, v_w)):
                        units.append((q_n[half, tile, i * P:(i + 1) * P], k[half, g // 2, 0:w], None,
                                      [v[:, x, g * DH:(g + 1) * DH] for x in range(i + 1)], nsa_att))
            return units

        ATT = {"fox": 0, "nsa": FOX_HEADS * TT}

        block = ctx.enter_context(nc.Block())

        @block.sync
        def _(sp):
            for i in range(TT):
                sp.dma_start(x_tok[:, i, :], d["x"][i * P:(i + 1) * P, :]).then_inc(x_in, 16)
            for n, (loads, _) in enumerate(stream):
                if n >= 2:
                    kind, last = stream[n - 2][1]
                    if kind == "job":
                        wait_full(sp, last)
                    else:
                        sp.wait_ge(down_read, last)
                for dst, src in loads:
                    sp.dma_start(dst, src).then_inc(w_loaded[n % 2], 16)
            for i in range(TT):
                sp.wait_ge(sem("result_ready"), i + 1)
                sp.dma_start(out[i * P:(i + 1) * P, :], x_tok[:, i, :]).then_inc(sem("result_out"), 16)
            sp.wait_ge(sem("result_out"), 16 * TT)

        @block.tensor
        def _(pe):
            join = counter()

            def mm(o, w, x, first=True, last=True):
                return pe.matmul(o, w, x, start=first, stop=last)

            def fill(j, ins):
                ins.then_inc(full[j % BANKS], 1)

            def transposes(j, tiles, width=P):
                claim(pe, j)
                for i, t in enumerate(tiles):
                    ins = pe.transpose(ps(j)[:, i * P:(i + 1) * P], t, ident)
                fill(j, ins)

            def to_channels(j, w):
                claim(pe, j)
                for k in range(KT):
                    ins = mm(ps(j)[0:w.shape[2], :], w[:, k, :], h_t[:, k, :], k == 0, k == KT - 1)
                fill(j, ins)

            def to_tokens(j, i, src, w):
                claim(pe, j)
                for k in range(KT):
                    ins = mm(ps(j)[:, 0:w.shape[2]], src[:, k, i * P:(i + 1) * P], w[:, k, :], k == 0, k == KT - 1)
                fill(j, ins)

            def norm(n, xn):
                pe.wait_ge(sem("norm_scaled"), n + 1)
                for k in range(KT):
                    transposes(base["n%d" % (n + 1)] + k, [xn[:, i, k * P:(k + 1) * P] for i in range(TT)])

            def attend(name, units):
                order = base[name]
                off = ATT[name]
                for s in range(len(units) + 2):
                    if s < len(units):
                        q, k, extra, _, att = units[s]
                        j = order["S", s]
                        claim(pe, j)
                        w = k.shape[1]
                        ins = mm(ps(j)[:, 0:w], q, k, True, extra is None)
                        if extra is not None:
                            ins = mm(ps(j)[:, 0:w], extra[0], extra[1], False, True)
                        fill(j, ins)
                    if 0 <= s - 1 < len(units):
                        u = s - 1
                        _, k, _, _, att = units[u]
                        pe.wait_ge(sem("probs_ready"), off + u + 1)
                        prob = view(att, 3, T)[:, u % 3, :]
                        transposes(order["T", u], [prob[:, x * P:(x + 1) * P] for x in range(k.shape[1] // P)])
                    if 0 <= s - 2:
                        u = s - 2
                        _, k, _, vals, att = units[u]
                        j = order["V", u]
                        wait_read(pe, order["T", u])
                        claim(pe, j)
                        pt = view(att + 1536, 3, T)[:, u % 3, :]
                        for x, v in enumerate(vals):
                            ins = mm(ps(j)[:, 0:DH], pt[:, x * P:(x + 1) * P], v, x == 0, x == len(vals) - 1)
                        fill(j, ins)

            def project_out(name, src):
                w = [weights(pe, (name, n)) for n in range(2)]
                for i in range(TT):
                    for hf in range(2):
                        to_tokens(base[name] + 2 * i + hf, i, src, w[hf])

            have(pe, "start")
            norm(0, norm_1)
            join(pe)
            for n in range(7):
                w = weights(pe, ("p1", n))
                for m in range(4):
                    if n == 5:
                        to_tokens(base["p1"] + 4 * n + m, m, h_t, w)
                    else:
                        to_channels(base["p1"] + 4 * n + m, w[:, :, m * P:(m + 1) * P])
            to_channels(base["p1"] + 28, fc_w)
            join(pe)
            have(pe, "sel")
            for n in range(2 * DH + 2):
                if n < 2 * DH:
                    j = base["hg"] + n
                    claim(pe, j)
                    fill(j, mm(ps(j), sel_b[:, n % DH, :], i_a[:, n // DH, :]))
                if n >= 2:
                    m = n - 2
                    pe.wait_ge(sem("hg_qs"), m + 1)
                    v = m % DH
                    mm(bank[6 + m // DH][:, :], z_sel[:, 64 - v:192 - v], hg_u[:, m % 3, :],
                       v == 0, v == DH - 1).then_inc(sem("hg_summed"), 1)
            for c in range(2):
                j = base["hn"] + c
                pe.wait_ge(sem("hg_squares"), c + 1)
                claim(pe, j)
                fill(j, mm(ps(j), head_ones, hg_sq[:, c, :]))
            for c in range(2):
                j = base["pool"] + c
                pe.wait_ge(sem("pooled"), c + 1)
                claim(pe, j)
                fill(j, mm(ps(j), pool_w[:, c, :], pool_s[:, c, 16:528]))
            join(pe)
            have(pe, "fox")
            pe.wait_ge(sem("fox_decay"), 1)
            attend("fox", fox_units())
            pe.wait_ge(sem("fox_o_ready"), 1)
            for k in range(4):
                transposes(base["ft"] + k, [fox_o[:, i, k * P:(k + 1) * P] for i in range(TT)])
            for k in range(4):
                wait_read(pe, base["ft"] + k)
            project_out("y1", mix_t)
            join(pe)
            norm(1, norm_2)
            join(pe)
            w = weights(pe, "lora")
            for n, (a, b) in enumerate(((0, 128), (128, 256), (256, 288))):
                to_channels(base["lora"] + n, w[:, :, a:b])
            have(pe, "rwkv")
            pe.wait_ge(sem("lora_ready"), 1)
            for q in range(4):
                b0 = base["ra", q]
                w = weights(pe, ("rk", q))
                for n in range(4):
                    to_channels(b0 + n, w[:, :, n * P:(n + 1) * P])
                w = weights(pe, ("v", q))
                for n in range(2):
                    to_channels(b0 + 4 + n, w[:, :, n * P:(n + 1) * P])
                for n in range(2):
                    j = b0 + 6 + n
                    c0 = (2 * q + n) * P
                    claim(pe, j)
                    fill(j, mm(ps(j), lora_w[0:64, c0:c0 + P], lo_wa[0:64, :]))
                for n in range(2):
                    j = b0 + 8 + n
                    c0 = (2 * q + n) * P
                    claim(pe, j)
                    fill(j, mm(ps(j), lora_w[64:128, c0:c0 + P], lo_wa[64:128, :]))
                pe.wait_ge(sem("kk_squares"), q + 1)
                for n in range(2):
                    j = b0 + 10 + n
                    claim(pe, j)
                    fill(j, mm(ps(j), head_ones, t1_q[:, n, :]))
                pe.wait_ge(sem("rk_ready"), q + 1)
                j = b0 + 12
                claim(pe, j)
                for c in range(TT):
                    for n in range(2):
                        ins = mm(ps(j)[:, 4 * c + 2 * n:4 * c + 2 * n + 2], t1_q[:, n, c * P:(c + 1) * P], head_sel)
                fill(j, ins)
                pe.wait_ge(sem("operands_ready"), q + 1)
                for m, src in enumerate((v_q, b_h, k_h)):
                    for n in range(2):
                        transposes(b0 + 13 + 2 * m + n, [src[:, n, c * P:(c + 1) * P] for c in range(TT)])
                join(pe)
                b0 = base["rb", q]
                for c in range(TT):
                    for h in range(4):
                        j = b0 + 6 * c + h
                        half, n = slice((h % 2) * DH, (h % 2) * DH + DH), h // 2
                        tok = slice(c * P, (c + 1) * P)
                        claim(pe, j)
                        ar = a_r[half, n, c, :, :].rearrange("p a b -> p (a b)")
                        mm(ps(j)[:, 0:256], b_h[half, n, tok], ar)
                        fill(j, mm(ps(j)[:, 256:512], k_h[half, n, tok], ar))
                    for x in range(2):
                        j = b0 + 6 * c + 4 + x
                        half = slice(x * DH, x * DH + DH)
                        claim(pe, j)
                        for n in range(2):
                            ins = mm(ps(j)[:, n * P:(n + 1) * P], a_r[half, n, c, 0, :], b_h[half, n, tok])
                        fill(j, ins)

                def four(j, w, x):
                    claim(pe, j)
                    for h in range(4):
                        ins = mm(ps(j)[:, h * P:(h + 1) * P], w[:, h, :], x[:, h, :])
                    fill(j, ins)

                for lev in range(3):
                    b1 = b0 + 24 + 16 * lev
                    for c in range(TT):
                        if lev == 0:
                            pe.wait_ge(sem("inv_started"), 4 * (4 * q + c + 1))
                        else:
                            wait_read(pe, b1 - 16 + 2 * c)
                            wait_read(pe, b1 - 16 + 2 * c + 1)
                        four(b1 + 2 * c, pwt[:, c], pw[:, c])
                        four(b1 + 2 * c + 1, pw[:, c], pwt[:, c])
                    for c in range(TT):
                        wait_read(pe, b1 + 2 * c)
                        wait_read(pe, b1 + 2 * c + 1)
                        if lev:
                            wait_read(pe, b1 - 8 + 2 * c)
                            wait_read(pe, b1 - 8 + 2 * c + 1)
                        four(b1 + 8 + 2 * c, pwt[:, c], inv[:, c])
                        four(b1 + 8 + 2 * c + 1, pw[:, c], invt[:, c])
                for m in range(3):
                    b1 = b0 + 72 + 12 * m
                    for c in range(TT):
                        pe.wait_ge(sem("between_ready"), 12 * q + 4 * m + c + 1)
                        wait_read(pe, (b0 + 64 if m == 0 else b1 - 8) + 2 * c)
                        wait_read(pe, (b0 + 65 if m == 0 else b1 - 7) + 2 * c)
                        four(b1 + c, pw[:, c], invt[:, c])
                    for c in range(TT):
                        wait_read(pe, b1 + c)
                        if m < 2:
                            four(b1 + 4 + 2 * c, pwt[:, c], inv[:, c])
                            four(b1 + 5 + 2 * c, inv[:, c], pwt[:, c])
                        else:
                            four(b1 + 4 + c, inv[:, c], pwt[:, c])
                join(pe)
                b0 = base["rc", q]
                for n in range(2):
                    j = b0 + n
                    claim(pe, j)
                    for c in range(2):
                        tok = slice((2 * n + c) * P, (2 * n + c + 1) * P)
                        mm(ps(j)[:, c * 256:(c + 1) * 256], lo_g1[:, tok], g2_a[:, 256 * q:256 * q + 256], True, False)
                        ins = mm(ps(j)[:, c * 256:(c + 1) * 256], lo_g2[0:32, tok],
                                 g2_b[0:32, 256 * q:256 * q + 256], False, True)
                    fill(j, ins)
                for c in range(TT):
                    j = b0 + 2 + 4 * c
                    if c:
                        pe.wait_ge(sem("state_ready"), 3 * q + c)
                    claim(pe, j)
                    for n in range(2):
                        if c:
                            mm(ps(j)[:, n * P:(n + 1) * P], a_r[:, n, c, 0, :], state[:, n, :], True, False)
                        for h in (2 * n, 2 * n + 1):
                            ins = mm(ps(j)[:, h * DH:(h + 1) * DH], gram[:, c, h, 256:384],
                                     v_tok[:, c, h * DH:(h + 1) * DH], c == 0, c == 0 or h % 2 == 1)
                    fill(j, ins)
                    wait_read(pe, j)
                    j += 1
                    claim(pe, j)
                    for h in range(4):
                        ins = mm(ps(j)[:, h * DH:(h + 1) * DH], invt[:, c, h, :], rhs_b[:, h * DH:(h + 1) * DH])
                    fill(j, ins)
                    wait_read(pe, j)
                    j += 1
                    claim(pe, j)
                    for n in range(2):
                        if c:
                            mm(ps(j)[:, n * P:(n + 1) * P], a_r[:, n, c, 1, :], state[:, n, :], True, False)
                        for h in (2 * n, 2 * n + 1):
                            hv = slice(h * DH, (h + 1) * DH)
                            mm(ps(j)[:, hv], gram[:, c, h, 128:256], sa_b[:, hv], c == 0, False)
                            ins = mm(ps(j)[:, hv], gram[:, c, h, 384:512], v_tok[:, c, hv], False,
                                     c == 0 or h % 2 == 1)
                    fill(j, ins)
                    if c < TT - 1:
                        j += 1
                        claim(pe, j)
                        for n in range(2):
                            ch = slice(n * P, (n + 1) * P)
                            mm(ps(j)[:, ch], b_tok[:, c, ch], sa_b[:, ch], True, False)
                            ins = mm(ps(j)[:, ch], k_tok[:, c, ch], v_tok[:, c, ch], False, True)
                        fill(j, ins)
                pe.wait_ge(sem("rwkv_o_ready"), q + 1)
                for n in range(2):
                    transposes(b0 + 17 + n, [y_q[:, c, n * P:(n + 1) * P] for c in range(TT)])
                join(pe)
            b0 = base["np"]
            for n in range(2):
                w = weights(pe, ("q", n))
                for m in range(4):
                    to_channels(b0 + 4 * n + m, w[:, :, m * P:(m + 1) * P])
            w = weights(pe, ("kv", 0))
            for m in range(4):
                to_channels(b0 + 8 + m, w[:, :, m * P:(m + 1) * P])
            for x in range(2):
                w = weights(pe, ("kv", 1 + x))
                for m in range(2):
                    to_channels(b0 + 12 + 6 * x + m, w[:, :, m * P:(m + 1) * P])
                for i in range(TT):
                    to_tokens(b0 + 14 + 6 * x + i, i, h_t, w[:, :, 256:512])
            have(pe, "nsa")
            j = b0 + 24
            claim(pe, j)
            for i in range(TT):
                for k in range(KT):
                    ins = mm(ps(j)[:, 48 * i:48 * i + 48], h_t[:, k, i * P:(i + 1) * P], gl_w[:, k, :],
                             k == 0, k == KT - 1)
            fill(j, ins)
            b0 = base["cmp"]
            for m, (w1, x, pos) in enumerate(((w1k, xk, pos_k), (w1v, xv, pos_v))):
                j = b0 + m
                for n in range(2):
                    wait_read(pe, base["np"] + 8 + 2 * m + n)
                claim(pe, j)
                for t in range(16):
                    mm(ps(j)[:, 0:124], w1[:, t, :], x[:, :, 2 * t:2 * t + 16 * CMP_N - 15:16], t == 0, t == 15)
                for t in range(16):
                    ins = mm(ps(j)[:, 128:130], w1[:, t, :], pos[:, t:t + 1].broadcast_to([P, 2]), t == 0, t == 15)
                fill(j, ins)
            j = b0 + 2
            pe.wait_ge(sem("hidden_ready"), 1)
            claim(pe, j)
            fill(j, mm(ps(j)[0:64, 0:128], w2k, hid_k.rearrange("p g n -> p (g n)")))
            j = b0 + 3
            pe.wait_ge(sem("hidden_ready"), 2)
            claim(pe, j)
            for g in range(4):
                ins = mm(ps(j)[:, g * DH:(g + 1) * DH], hid4[:, g].rearrange("p h n -> p (h n)"), w2v)
            fill(j, ins)
            for n in range(8):
                wait_read(pe, base["np"] + n)
            wait_read(pe, b0 + 2)
            wait_read(pe, b0 + 3)
            for i in range(TT):
                for x in range(2):
                    j = b0 + 4 + 5 * i + x
                    claim(pe, j)
                    for n in range(8):
                        half, tile = nsa_place((n // 4) * 8 + x * 4 + n % 4)
                        ins = mm(ps(j)[:, n * 32:(n + 1) * 32], q_n[half, tile, i * P:(i + 1) * P],
                                 k_cmp[half, n // 4, :])
                    fill(j, ins)
                pe.wait_ge(sem("cmp_probs"), i + 1)
                transposes(j + 1, [c_sc[:, i % 2, x * P:(x + 1) * P] for x in range(4)])
                wait_read(pe, j + 1)
                for x in range(2):
                    claim(pe, j + 2 + x)
                    for g in (2 * x, 2 * x + 1):
                        ins = mm(ps(j + 2 + x)[:, (g % 2) * 256:(g % 2) * 256 + 256],
                                 c_pt[:, i % 2, g * P:(g + 1) * P], v_bd[:, g].rearrange("p h n -> p (h n)"))
                    fill(j + 2 + x, ins)
            join(pe)
            attend("nsa", nsa_units())
            pe.wait_ge(sem("nsa_o_ready"), 1)
            for k in range(KT):
                transposes(base["nt"] + k, [nsa_o[:, i, k * P:(k + 1) * P] for i in range(TT)])
            join(pe)
            for hf in range(2):
                for m, src in enumerate((h_t, h_t, oa_t, ob_t)):
                    w = weights(pe, ("merge", hf, m))
                    for c in range(4):
                        j = base["merge"] + 16 * hf + 4 * m + c
                        claim(pe, j)
                        for k in range(KT):
                            ins = mm(ps(j), w[:, k, c * P:(c + 1) * P], src[:, k, :], k == 0, k == KT - 1)
                        fill(j, ins)
            pe.wait_ge(sem("merged"), 8)
            project_out("y2", m_t)
            join(pe)
            norm(2, norm_3)
            join(pe)
            for n in range(11):
                w = weights(pe, ("ff", n))
                for m in range(4):
                    to_channels(base["ff"] + 4 * n + m, w[:, :, m * P:(m + 1) * P])
            pe.wait_ge(sem("act_ready"), FF_TILES)
            for hf in range(2):
                b0 = base["y3"] + 4 * hf
                for n, (a, b) in enumerate(DOWN):
                    w = weights(pe, ("y3", hf, n))
                    for i in range(TT):
                        if n == 0:
                            claim(pe, b0 + i)
                        for k in range(a, b):
                            ins = mm(ps(b0 + i), act_t[:, k, i * P:(i + 1) * P], w[:, k - a, :],
                                     k == 0, k == FF_TILES - 1)
                        if n == 2:
                            fill(b0 + i, ins)
                    if n < 2:
                        ins.then_inc(down_read, 1)
            join(pe)

        @block.scalar
        def _(act):
            join = counter()
            act_step = sem("act_step")
            steps = [0]

            def mark(ins):
                ins.then_inc(act_step, 1)
                steps[0] += 1
                return steps[0]

            def run(o, i, f, **kw):
                return act.activation(o, i, f, **kw)

            def read(j, ins):
                ins.then_inc(free[j % BANKS], 1)

            def copy_out(j, o, scale=1.0, width=512, parts=slice(0, P)):
                wait_full(act, j)
                read(j, run(o, ps(j)[parts, 0:width], ACT.Copy, scale=scale))

            def root(name, n, o, i):
                act.wait_ge(sem(name + "_ms"), n + 1)
                run(o, i, ACT.Sqrt).then_inc(sem(name + "_root"), 1)

            def attend(name, units):
                order = base[name]
                off = ATT[name]
                for s in range(len(units) + 1):
                    if s < len(units):
                        k, att = units[s][1], units[s][4]
                        w = k.shape[1]
                        act.wait_ge(sem("neg_max"), off + s + 1)
                        prob = view(att, 3, T)[:, s % 3, 0:w]
                        run(prob, prob, ACT.Exp, bias=stat[:, 20 + s % 4:21 + s % 4],
                            accum_out=stat[:, 24 + s % 4:25 + s % 4]).then_inc(sem("probs_ready"), 1)
                    if s >= 1:
                        u = s - 1
                        k, att = units[u][1], units[u][4]
                        if u >= 3:
                            wait_full(act, order["V", u - 3])
                        copy_out(order["T", u], view(att + 1536, 3, T)[:, u % 3, 0:k.shape[1]],
                                 width=k.shape[1])

            phase_loads(act, "start", L_START)
            root("norm", 0, stat[:, 8:12], stat[:, 4:8])
            join(act)
            phase_loads(act, "sel", L_SEL)
            for n in range(28):
                j = base["p1"] + n
                if n in SILU_NO:
                    s = SILU_NO[n]
                    if s >= 2:
                        wait_read(act, base["p1"] + SILU[s - 2][0])
                    wait_full(act, j)
                    run(sig[:, s % 2, :], ps(j), ACT.Sigmoid).then_inc(sem("silu_sig"), 1)
                elif n in (2, 3):
                    wait_full(act, j)
                    run(f_a[:, n - 2, :], ps(j), ACT.Sigmoid).then_inc(sem("forget_ready"), 1)
                    read(j, run(k_a[:, n - 2, :], ps(j), ACT.Sigmoid, scale=-1.0))
                elif n in (4, 5):
                    copy_out(j, i_a[:, n - 4, :])
                elif n in (8, 9):
                    copy_out(j, u_b[:, n - 8, :])
                elif n in range(12, 16):
                    copy_out(j, q_c[:, n - 12, :], scale=DH ** -0.5)
                elif n in range(16, 20):
                    copy_out(j, k_c[:, n - 16, :])
                else:
                    copy_out(j, v_c[:, n - 20, :])
            join(act)
            for c in range(2):
                act.wait_ge(sem("hg_summed"), DH * (c + 1))
                run(hg_sq[:, c, :], bank[6 + c][:, :], ACT.Square).then_inc(sem("hg_squares"), 1)
            root("hg", 0, hg_kv[:, 0:2, :], hg_kv[:, 0:2, :])
            join(act)
            phase_loads(act, "fox", L_FOX)
            phase_loads(act, "y1", L_Y1)
            act.wait_ge(sem("fox_abs"), 1)
            m = mark(run(fc_e[0:8, :], fc_abs[0:8, :], ACT.Exp, scale=-1.0))
            act.wait_ge(act_step, m)
            run(fc_e[0:8, :], fc_e[0:8, :], ACT.Ln, bias=1.0).then_inc(sem("fox_log"), 1)
            attend("fox", fox_units())

            def residual(name, n, y):
                for i in range(TT):
                    for hf in range(2):
                        copy_out(base[name] + 2 * i + hf, y[:, i, hf * 512:(hf + 1) * 512])
                root("post", n, stat[:, 8:12], stat[:, 4:8])

            residual("y1", 0, y_tok1)
            join(act)
            act.dma_start(x_saved.rearrange("(i p) c -> p i c", p=P), x_tok).then_inc(x_out, 16)
            root("norm", 1, stat[:, 8:12], stat[:, 4:8])
            act.wait_ge(x_out, 16)
            join(act)
            phase_loads(act, "rwkv", L_RW)
            mixes = [0]

            def to_mix(j, parts=P):
                m = mixes[0]
                mixes[0] += 1
                if m >= 2:
                    act.wait_ge(sem("mixed"), m - 1)
                copy_out(j, z_pad[0:parts, m % 2, 1:513], parts=slice(0, parts))

            act.wait_ge(sem("pads_zero"), 1)
            for n in range(3):
                to_mix(base["lora"] + n, (P, P, 32)[n])
            act.wait_ge(sem("mixed"), 3)
            run(lo_wa[0:64, :], lo_wa[0:64, :], ACT.Tanh)
            run(lo_g1, lo_g1, ACT.Sigmoid)
            run(lo_g2[0:32, :], lo_g2[0:32, :], ACT.Sigmoid).then_inc(sem("lora_ready"), 1)
            for q in range(4):
                b0 = base["ra", q]
                act.wait_ge(sem("pads_zero"), 1 + q)
                for n in range(6):
                    to_mix(b0 + n)
                for n in range(2):
                    wait_full(act, b0 + 6 + n)
                    read(b0 + 6 + n, run(lw_q[:, n, :], ps(b0 + 6 + n), ACT.Sigmoid, bias=params("w0", 2 * q + n)))
                for n in range(2):
                    wait_full(act, b0 + 8 + n)
                    read(b0 + 8 + n, run(av_q[:, n, :], ps(b0 + 8 + n), ACT.Sigmoid, bias=params("a0", 2 * q + n)))
                root("kk", q, t1_q, t1_q)
                act.wait_ge(sem("decay_sums"), q + 1)
                run(pm_q, b_q, ACT.Exp, bias=stat[:, 32:33])
                run(pp_q, pp_q, ACT.Exp, bias=stat[:, 32:33])
                run(last_p, b_q.rearrange("p n (c t) -> p (n c) t", t=P)[:, :, P - 1], ACT.Exp)
                run(pi_q, b_q, ACT.Exp, bias=stat[:, 33:34], scale=-1.0).then_inc(sem("decays_ready"), 1)
                for m, dst in enumerate((v_tok, b_tok, k_tok)):
                    for n in range(2):
                        j = b0 + 13 + 2 * m + n
                        wait_full(act, j)
                        read(j, run(dst[:, :, n * P:(n + 1) * P],
                                    ps(j).rearrange("p (c x) -> p c x", c=TT), ACT.Copy))
                join(act)
                b0 = base["rb", q]

                def flat(t, c):
                    return t[:, c].rearrange("p h x -> p (h x)")

                for lev in range(3):
                    for c in range(TT):
                        j = b0 + 24 + 16 * lev + 2 * c
                        wait_full(act, j + 1)
                        wait_full(act, j)
                        read(j, run(flat(pw, c), ps(j), ACT.Copy))
                        read(j + 1, run(pwt[:, c], ps(j + 1).rearrange("p (h x) -> p h x", h=4), ACT.Copy))
                for m in range(3):
                    for c in range(TT):
                        j = b0 + 72 + 12 * m + c
                        wait_full(act, j)
                        read(j, run(pwt[:, c], ps(j).rearrange("p (h x) -> p h x", h=4), ACT.Copy))
                join(act)
                phase_loads(act, "ln", L_LN[q])
                b0 = base["rc", q]
                for n in range(2):
                    copy_out(b0 + n, g_q[:, 2 * n:2 * n + 2, :].rearrange("p c x -> p (c x)"))
                for c in range(TT):
                    copy_out(b0 + 2 + 4 * c, rhs_b, width=256)
                    copy_out(b0 + 4 + 4 * c, y_q[:, c, :], width=256)
                root("gn", q, stat[:, 56:72], stat[:, 56:72])
                for n in range(2):
                    copy_out(b0 + 17 + n, oa_t[:, 2 * q + n, :])
                join(act)
            phase_loads(act, "nsa", L_NSA)
            b0 = base["np"]
            for n in range(8):
                copy_out(b0 + n, q_n[:, n, :], scale=DH ** -0.5)
            for m, dst in enumerate((xk, xv)):
                for n in range(2):
                    j = b0 + 8 + 2 * m + n
                    wait_full(act, j)
                    run(dst[0:64, 2 * n, :], ps(j)[0:64, :], ACT.Copy)
                    run(dst[64:128, 2 * n, 0:511], ps(j)[0:64, 1:512], ACT.Copy)
                    run(dst[0:64, 2 * n + 1, :], ps(j)[64:128, :], ACT.Copy)
                    read(j, run(dst[64:128, 2 * n + 1, 0:511], ps(j)[64:128, 1:512], ACT.Copy))
            for x, (k, v) in enumerate(((k_s, v_s), (k_w, v_w))):
                for m in range(2):
                    copy_out(b0 + 12 + 6 * x + m, k[:, m, :])
                for i in range(TT):
                    copy_out(b0 + 14 + 6 * x + i, v[:, i, :], width=256)
            wait_full(act, b0 + 24)
            read(b0 + 24, run(gates.rearrange("p i g -> p (i g)"), ps(b0 + 24)[:, 0:192], ACT.Sigmoid))
            b0 = base["cmp"]
            for m in range(2):
                act.wait_ge(sem("gelu_arg"), m + 1)
                run(hs, h2, ACT.Sigmoid, scale=1.5957691216057308).then_inc(sem("gelu_sig"), 1)
            wait_full(act, b0 + 2)
            for g in range(4):
                ins = run(k_cmp[(g % 2) * DH:(g % 2) * DH + DH, g // 2, :], ps(b0 + 2)[0:64, g * 32:(g + 1) * 32], ACT.Copy)
            read(b0 + 2, ins)
            for i in range(TT):
                j = b0 + 5 + 5 * i
                act.wait_ge(sem("cmp_shifted"), i + 1)
                run(c_sc[:, i % 2, :], c_sc[:, i % 2, :], ACT.Exp).then_inc(sem("cmp_exp"), 1)
                if i >= 2:
                    wait_full(act, j - 10 + 3)
                copy_out(j + 1, c_pt[:, i % 2, :])
                for x in range(2):
                    copy_out(j + 2 + x, nsa_o[:, i, 512 * x:512 * x + 512])
            join(act)
            attend("nsa", nsa_units())
            for k in range(KT):
                copy_out(base["nt"] + k, ob_t[:, k, :])
            join(act)
            phase_loads(act, "y2", L_Y2)
            for hf in range(2):
                b0 = base["merge"] + 16 * hf
                if hf:
                    act.wait_ge(sem("merged"), 4)
                for m, dst in enumerate((sig_a, sig_b)):
                    for c in range(4):
                        wait_full(act, b0 + 4 * m + c)
                        read(b0 + 4 * m + c, run(dst[:, c, :], ps(b0 + 4 * m + c), ACT.Sigmoid))
            residual("y2", 1, y_tok2)
            join(act)
            root("norm", 2, stat[:, 8:12], stat[:, 4:8])
            join(act)
            phase_loads(act, "y3", L_Y3)
            act.wait_ge(sem("ff_pads"), 1)
            for n in range(11):
                for m in range(4):
                    u = 4 * n + m
                    if u >= 4:
                        act.wait_ge(sem("conv_done"), u - 3)
                    copy_out(base["ff"] + u, ff_pad[:, u % 4, 2:514])
                for m in range(2):
                    act.wait_ge(sem("conv_done"), 4 * n + m + 1)
                    if n:
                        act.wait_ge(sem("act_ready"), 2 * n - 1 + m)
                    run(ff_s[:, m, :], ff_c[:, m, :], ACT.Sigmoid).then_inc(sem("ff_sig"), 1)
            for hf in range(2):
                for i in range(TT):
                    copy_out(base["y3"] + 4 * hf + i, y_tok3[:, i, hf * 512:(hf + 1) * 512])
            root("post", 2, stat[:, 8:12], stat[:, 4:8])
            join(act)

        @block.gpsimd
        def _(pool):
            join = counter()
            pool_step = sem("pool_step")
            steps = [0]

            def after(ins):
                ins.then_inc(pool_step, 1)
                steps[0] += 1
                pool.wait_ge(pool_step, steps[0])

            join(pool)
            join(pool)
            pool.memset(pool_pad[:, :, 0:16], 0.0)
            pool.memset(pool_s[:, :, 0:16], 0.0)
            for c in range(2):
                after(pool.tensor_copy(pool_pad[:, c, 16:528], u_b[:, c, :]))
            have(pool, "start")
            for c in range(2):
                a, b = pool_pad[:, c], pool_s[:, c]
                after(pool.tensor_tensor(b[:, 16:528], a[:, 16:528], a[:, 15:527], ALU.add))
                if c == 0:
                    up = slice(64, 128)
                    after(pool.tensor_tensor(a[up, 16:528], b[up, 16:528], b[up, 14:526], ALU.add))
                    after(pool.tensor_copy(b[up, 16:528], a[up, 16:528]))
                else:
                    after(pool.tensor_tensor(a[:, 16:528], b[:, 16:528], b[:, 14:526], ALU.add))
                    after(pool.tensor_tensor(b[:, 16:528], a[:, 16:528], a[:, 12:524], ALU.add))
                    after(pool.tensor_tensor(a[up, 16:528], b[up, 16:528], b[up, 8:520], ALU.add))
                    after(pool.tensor_copy(b[up, 16:528], a[up, 16:528]))
                after(pool.tensor_tensor(b[:, 16:528], b[:, 16:528], inv_count[:, c, :], ALU.mult))
                pool.tensor_tensor(b[:, 16:528], b[:, 16:528], u_b[:, c, :], ALU.subtract).then_inc(sem("pooled"), 1)
            for n in range(2 * DH):
                pool.wait_ge(sem("hg_scanned"), n + 1)
                if n >= 3:
                    pool.wait_ge(sem("hg_summed"), n - 2)
                pool.tensor_tensor(hg_u[:, n % 3, :], hg_s[:, n % 2, :], q_a[:, n // DH, :],
                                   ALU.mult).then_inc(sem("hg_qs"), 1)
            join(pool)
            join(pool)
            join(pool)
            for q in range(4):
                pool.memset(z_pad[:, :, 0:2], 0.0).then_inc(sem("pads_zero"), 1)
                join(pool)
                have(pool, "rwkv")
                for c in range(TT):
                    wait_read(pool, base["rb", q] + 6 * c + 4)
                    wait_read(pool, base["rb", q] + 6 * c + 5)
                    for h in range(4):
                        wait_read(pool, base["rb", q] + 6 * c + h)
                    blk = over(m_blk, 4)
                    after(pool.tensor_tensor(pw[:, c], low[:, c], blk, ALU.mult))
                    after(pool.tensor_tensor(pwt[:, c], gram[:, c, :, 0:128], blk, ALU.mult))
                    for dst, src in ((inv, pw), (invt, pwt)):
                        pool.tensor_tensor(dst[:, c], src[:, c], over(ident, 4), ALU.add).then_inc(
                            sem("inv_started"), 2)
                for m in range(3):
                    b0 = base["rb", q] + 72 + 12 * m
                    for c in range(TT):
                        wait_full(pool, base["rb", q] + 65 + 2 * c if m == 0 else b0 - 12 + c)
                        pool.tensor_tensor(pw[:, c], low[:, c], over(m_e[:, m, :], 4), ALU.mult).then_inc(
                            sem("between_ready"), 1)
                join(pool)
                join(pool)
            join(pool)
            for h in range(NSA_HEADS):
                if h >= 2:
                    wait_read(pool, base["nsa"]["S", 8 * (h - 1) - 1])
                after(pool.tensor_scalar(tab[:, h % 2, :], dist, 2.0 ** (-8.0 * (h + 1) / NSA_HEADS), None, ALU.mult))
                pool.tensor_tensor(tab[:, h % 2, :], tab[:, h % 2, :], causal, ALU.add).then_inc(sem("slopes_ready"), 1)
            join(pool)
            join(pool)
            join(pool)
            pool.memset(ff_pad[:, :, 0:2], 0.0).then_inc(sem("ff_pads"), 1)
            join(pool)

        @block.vector
        def _(dve):
            join = counter()
            dve_step = sem("dve_step")
            steps = [0]

            def mark(ins):
                ins.then_inc(dve_step, 1)
                steps[0] += 1
                return steps[0]

            def after(step):
                dve.wait_ge(dve_step, step)

            def then(ins):
                after(mark(ins))

            def read(j, ins):
                ins.then_inc(free[j % BANKS], 1)

            def tt(o, a, b, op):
                return dve.tensor_tensor(o, a, b, op)

            def stt(o, a, s, b, op0, op1):
                return dve.scalar_tensor_tensor(o, a, s, b, op0, op1)

            def ts(o, a, s1, s2=None, op0=ALU.mult, op1=None):
                if op1 is None:
                    return dve.tensor_scalar(o, a, s1, None, op0)
                return dve.tensor_scalar(o, a, s1, s2, op0, op1)

            def inverse_root(name, n, ins, o, i):
                ins.then_inc(sem(name + "_ms"), 1)
                dve.wait_ge(sem(name + "_root"), n + 1)
                return dve.reciprocal(o, i)

            def sum_squares(junk, x, n):
                return dve.tensor_tensor_reduce(out=junk, in0=x, in1=x, scale=1.0, scalar=0.0, op0=ALU.mult,
                                                op1=ALU.add, accum_out=stat[:, n:n + 1])

            def norm(n, xn, gain):
                for i in range(TT):
                    m = mark(sum_squares(xn[:, i, :], x_tok[:, i, :], i))
                after(m)
                then(inverse_root("norm", n, ts(stat[:, 4:8], stat[:, 0:4], 1.0 / D, EPS, ALU.mult, ALU.add),
                                  stat[:, 12:16], stat[:, 8:12]))
                for i in range(TT):
                    ins = ts(xn[:, i, :], x_tok[:, i, :], stat[:, 12 + i:13 + i])
                ins.then_inc(sem("norm_scaled"), 1)
                for k in range(KT):
                    j = base["n%d" % (n + 1)] + k
                    wait_full(dve, j)
                    read(j, ts(h_t[:, k, :], ps(j), params(gain, k)))

            def residual(name, n, y, gain, done):
                for i in range(TT):
                    for hf in range(2):
                        wait_read(dve, base[name] + ((4 * hf + i) if name == "y3" else (2 * i + hf)))
                    m = mark(sum_squares(view(4096 + 1024 * i, D), y[:, i, :], i))
                after(m)
                then(inverse_root("post", n, ts(stat[:, 4:8], stat[:, 0:4], 1.0 / D, EPS, ALU.mult, ALU.add),
                                  stat[:, 12:16], stat[:, 8:12]))
                marks = [mark(stt(y[:, i, :], y[:, i, :], stat[:, 12 + i:13 + i], gain, ALU.mult, ALU.mult))
                         for i in range(TT)]
                for i in range(TT):
                    after(marks[i])
                    tt(x_tok[:, i, :], x_tok[:, i, :], y[:, i, :], ALU.add).then_inc(done, 1)

            def attend(name, units, bias, finish):
                order = base[name]
                for s in range(len(units) + 2):
                    if s < len(units):
                        k, att = units[s][1], units[s][4]
                        w = k.shape[1]
                        j = order["S", s]
                        wait_full(dve, j)
                        if s >= 3:
                            wait_full(dve, order["T", s - 3])
                        read(j, dve.tensor_tensor_reduce(
                            out=view(att, 3, T)[:, s % 3, 0:w], in0=ps(j)[:, 0:w], in1=bias(s), scale=1.0,
                            scalar=-3.0e38, op0=ALU.add, op1=ALU.max, accum_out=stat[:, 16 + s % 4:17 + s % 4]))
                        wait_read(dve, j)
                        ts(stat[:, 20 + s % 4:21 + s % 4], stat[:, 16 + s % 4:17 + s % 4], -1.0).then_inc(
                            sem("neg_max"), 1)
                    if s >= 2:
                        u = s - 2
                        j = order["V", u]
                        wait_full(dve, j)
                        then(dve.reciprocal(stat[:, 28:29], stat[:, 24 + u % 4:25 + u % 4]))
                        finish(u, j)

            have(dve, "start")
            dve.wait_ge(x_in, 16 * TT)
            norm(0, norm_1, "pre_norm")
            join(dve)
            m = None
            for n in range(29):
                j = base["p1"] + n
                if n in SILU_NO:
                    s = SILU_NO[n]
                    wait_full(dve, j)
                    dve.wait_ge(sem("silu_sig"), s + 1)
                    read(j, tt(SILU_OUT[n], ps(j), sig[:, s % 2, :], ALU.mult))
                elif n == 2:
                    dve.wait_ge(sem("forget_ready"), 2)
                    ts(f_a, f_a, TINY, None, ALU.max)
            wait_full(dve, base["p1"] + 28)
            read(base["p1"] + 28, ts(fc_x[0:8, :], ps(base["p1"] + 28)[0:8, :], params("fox_bias", 0, 8), None, ALU.add))
            join(dve)
            def key_value(n):
                j = base["hg"] + n
                wait_full(dve, j)
                read(j, tt(hg_kv[:, n % 3, :], ps(j), k_a[:, n // DH, :], ALU.mult))

            key_value(0)
            for n in range(2 * DH):
                if n + 1 < 2 * DH:
                    key_value(n + 1)
                wait_read(dve, base["hg"] + n)
                if n >= 2:
                    dve.wait_ge(sem("hg_qs"), n - 1)
                dve.tensor_tensor_scan(hg_s[:, n % 2, :], f_a[:, n // DH, :], hg_kv[:, n % 3, :], 0.0,
                                       ALU.mult, ALU.add).then_inc(sem("hg_scanned"), 1)
            for c in range(2):
                j = base["hn"] + c
                wait_full(dve, j)
                if c == 0:
                    dve.wait_ge(sem("hg_scanned"), 2 * DH)
                m = ts(hg_kv[:, c, :], ps(j), 1.0 / DH, EPS, ALU.mult, ALU.add)
                read(j, m)
            for c in range(2):
                wait_read(dve, base["hn"] + c)
            then(ts(hg_kv[:, 2, 0:2], hg_kv[:, 0, 0:2], 1.0))
            then(inverse_root("hg", 0, ts(hg_kv[:, 2, 0:2], hg_kv[:, 0, 0:2], 1.0),
                              hg_kv[:, 0:2, :], hg_kv[:, 0:2, :]))
            for c in range(2):
                m = mark(stt(hg_sq[:, c, :], bank[6 + c][:, :], params("hgrn_norm", c), hg_kv[:, c, :],
                             ALU.mult, ALU.mult))
            after(m)
            for c in range(2):
                tt(mix_t[:, c, :], hg_sq[:, c, :], silu_ga[:, c, :], ALU.mult)
            for c in range(2):
                j = base["pool"] + c
                wait_full(dve, j)
                read(j, stt(mix_t[:, 2 + c, :], ps(j), params("pool_scale", c), silu_gb[:, c, :], ALU.mult, ALU.mult))
            join(dve)
            x8, a8, e8, l8, n8 = (v[0:8, :] for v in (fc_x, fc_abs, fc_e, fc_ls, fc_neg))
            stt(a8, x8, -1.0, x8, ALU.mult, ALU.max).then_inc(sem("fox_abs"), 1)
            dve.wait_ge(sem("fox_log"), 1)
            then(stt(l8, x8, 0.0, e8, ALU.min, ALU.subtract))
            then(ts(a8, x8, 0.0, 1.0, ALU.mult, ALU.add))
            dve.tensor_tensor_scan(n8, a8, l8, 0.0, ALU.mult, ALU.subtract).then_inc(sem("fox_decay"), 1)

            def fox_finish(u, j):
                ins = ts(fox_o[:, u % TT, (u // TT) * DH:(u // TT + 1) * DH], ps(j)[:, 0:DH], stat[:, 28:29])
                read(j, ins)
                wait_read(dve, j)

            attend("fox", fox_units(), lambda u: causal[:, 384 - P * (u % TT):512], fox_finish)
            ts(stat[:, 29:30], stat[:, 28:29], 1.0).then_inc(sem("fox_o_ready"), 1)
            for k in range(4):
                j = base["ft"] + k
                wait_full(dve, j)
                read(j, tt(mix_t[:, 4 + k, :], ps(j), silu_gc[:, k, :], ALU.mult))
            have(dve, "y1")
            residual("y1", 0, y_tok1, gain1, sem("x_ready"))
            join(dve)
            norm(1, norm_2, "mix_pre")
            dve.memset(stat[:, 32:33], MID)
            dve.memset(stat[:, 33:34], -MID)
            join(dve)
            have(dve, "rwkv")
            mixes = [0]

            def mix(j, o, mu, parts=P):
                m = mixes[0]
                mixes[0] += 1
                wait_read(dve, j)
                z = z_pad[0:parts, m % 2, :]
                then(tt(z_d[0:parts, m % 2, :], z[:, 0:512], z[:, 1:513], ALU.subtract))
                stt(o, z_d[0:parts, m % 2, :], mu, z[:, 1:513], ALU.mult, ALU.add).then_inc(sem("mixed"), 1)

            for n, (o, parts) in enumerate(((lo_wa, P), (lo_g1, P), (lo_g2, 32))):
                mix(base["lora"] + n, o[0:parts, :], params("mu_lora", n, parts), parts)
            for q in range(4):
                b0 = base["ra", q]
                for n in range(2):
                    mix(b0 + n, r_q[:, n, :], params("mu_rkv", 2 * q + n))
                for n in range(2):
                    mix(b0 + 2 + n, k_q[:, n, :], params("mu_rkv", 8 + 2 * q + n))
                for n in range(2):
                    mix(b0 + 4 + n, v_q[:, n, :], params("mu_rkv", 16 + 2 * q + n))
                dve.wait_ge(sem("mixed"), 3 + 6 * (q + 1))
                for n in range(2):
                    m = mark(ts(kk_q[:, n, :], k_q[:, n, :], params("k_k", 2 * q + n)))
                after(m)
                tt(t1_q, kk_q, kk_q, ALU.mult).then_inc(sem("kk_squares"), 1)
                for n in range(2):
                    wait_read(dve, b0 + 6 + n)
                then(ts(lw_q, lw_q, LOG_DECAY))
                for n in range(2):
                    m = mark(dve.tensor_tensor_scan(b_q[:, n, :], m_reset, lw_q[:, n, :], 0.0, ALU.mult, ALU.add))
                after(m)
                tt(pp_q, b_q, lw_q, ALU.subtract).then_inc(sem("decay_sums"), 1)
                for n in range(2):
                    j = b0 + 10 + n
                    wait_full(dve, j)
                    if n == 1:
                        wait_full(dve, b0 + 11)
                    wait_full(dve, b0 + 11)
                    ins = ts(t1_q[:, n, :], ps(j), 1e-24, None, ALU.max)
                    read(j, ins)
                for n in range(2):
                    wait_read(dve, b0 + 10 + n)
                then(inverse_root("kk", q, ts(z_d[:, 0, 0:2], t1_q[:, 0, 0:2], 1.0), t1_q, t1_q))
                m1 = mark(tt(kk_q, kk_q, t1_q, ALU.mult))
                for n in range(2):
                    wait_read(dve, b0 + 8 + n)
                    m = mark(ts(t2_q[:, n, :], av_q[:, n, :], 1.0, params("k_a", 2 * q + n), ALU.subtract, ALU.mult))
                after(m)
                then(stt(k_q, t2_q, 1.0, k_q, ALU.add, ALU.mult))
                for n in range(2):
                    m = mark(ts(t1_q[:, n, :], r_q[:, n, :], params("r_k", 2 * q + n)))
                after(m)
                tt(t1_q, t1_q, k_q, ALU.mult).then_inc(sem("rk_ready"), 1)
                m = mark(tt(t2_q, kk_q, av_q, ALU.mult))
                dve.wait_ge(sem("decays_ready"), q + 1)
                for n in range(2):
                    stt(a_r[:, n, :, 0, :], kk_q[:, n, :].rearrange("p (c t) -> p c t", c=TT), -1.0,
                        pp_q[:, n, :].rearrange("p (c t) -> p c t", c=TT), ALU.mult, ALU.mult)
                    tt(a_r[:, n, :, 1, :], r_q[:, n, :].rearrange("p (c t) -> p c t", c=TT),
                       pm_q[:, n, :].rearrange("p (c t) -> p c t", c=TT), ALU.mult)
                after(m)
                tt(b_h, t2_q, pi_q, ALU.mult)
                tt(k_h, k_q, pi_q, ALU.mult).then_inc(sem("operands_ready"), 1)
                j = b0 + 12
                wait_full(dve, j)
                read(j, dve.tensor_copy(bonus, ps(j)[:, 0:16]))
                join(dve)
                b0 = base["rb", q]
                for c in range(TT):
                    for h in range(4):
                        j = b0 + 6 * c + h
                        wait_full(dve, j)
                        read(j, tt(gram[:, c, h, :], ps(j), m_gram, ALU.mult))
                    for x in range(2):
                        j = b0 + 6 * c + 4 + x
                        wait_full(dve, j)
                        read(j, tt(low[:, c, x:4:2, :], ps(j)[:, 0:256].rearrange("p (h x) -> p h x", h=2),
                                   over(m_low, 2), ALU.mult))

                def add(j, t, c):
                    o = t[:, c].rearrange("p h x -> p (h x)")
                    read(j, tt(o, o, ps(j), ALU.add))

                for lev in range(3):
                    for c in range(TT):
                        j = b0 + 24 + 16 * lev + 8 + 2 * c
                        if lev == 0:
                            dve.wait_ge(sem("inv_started"), 4 * (4 * q + c + 1))
                        else:
                            wait_read(dve, j - 16)
                            wait_read(dve, j - 15)
                        wait_full(dve, j)
                        add(j, inv, c)
                        wait_full(dve, j + 1)
                        add(j + 1, invt, c)
                for m in range(3):
                    for c in range(TT):
                        j = b0 + 72 + 12 * m + (4 + 2 * c if m < 2 else 4 + c)
                        if m < 2:
                            wait_full(dve, j + 1)
                            wait_full(dve, j)
                            add(j, inv, c)
                            add(j + 1, invt, c)
                        else:
                            wait_full(dve, j)
                            add(j, invt, c)
                join(dve)
                b0 = base["rc", q]
                for c in range(TT):
                    j = b0 + 3 + 4 * c
                    wait_full(dve, j)
                    read(j, dve.tensor_copy(sa_b, ps(j)[:, 0:256]))
                    if c < TT - 1:
                        j += 2
                        wait_full(dve, j)
                        for n in range(2):
                            decay = last_p[:, 4 * n + c:4 * n + c + 1]
                            if c == 0:
                                ins = stt(state[:, n, :], ps(j)[:, n * P:(n + 1) * P], decay, head_ones,
                                          ALU.mult, ALU.mult)
                        if c == 0:
                            ins.then_inc(sem("state_ready"), 1)
                            dve.wait_ge(sem("state_ready"), 3 * q + 1)
                            read(j, ts(stat[:, 34:35], stat[:, 32:33], 1.0))
                        else:
                            read(j, tt(st_tmp, ps(j)[:, 0:256], state.rearrange("p n v -> p (n v)"), ALU.add))
                            wait_read(dve, j)
                            for n in range(2):
                                decay = last_p[:, 4 * n + c:4 * n + c + 1]
                                ins = stt(state[:, n, :], st_tmp[:, n * P:(n + 1) * P], decay, head_ones,
                                          ALU.mult, ALU.mult)
                            ins.then_inc(sem("state_ready"), 1)
                for c in range(TT):
                    wait_read(dve, b0 + 4 + 4 * c)
                have(dve, "ln", q + 1)
                y16 = y_q.rearrange("p c (h v) -> p (c h) v", v=DH)
                t16 = t3_q.rearrange("p c (h v) -> p (c h) v", v=DH)
                v16 = v_tok.rearrange("p c (h v) -> p (c h) v", v=DH)
                s16 = stat[:, 40:56]
                then(dve.reduce_sum(s16, y16, axis=AX.X))
                then(ts(s16, s16, -1.0 / DH))
                then(tt(y16, y16, along(s16, DH), ALU.add))
                then(tt(t16, y16, y16, ALU.mult))
                then(dve.reduce_sum(stat[:, 56:72], t16, axis=AX.X))
                then(inverse_root("gn", q, ts(stat[:, 56:72], stat[:, 56:72], 1.0 / DH, 64e-5, ALU.mult, ALU.add),
                                  stat[:, 72:88], stat[:, 56:72]))
                then(tt(y16, y16, along(stat[:, 72:88], DH), ALU.mult))
                then(tt(y_q, y_q, over(ln_q[:, 0, :], TT), ALU.mult))
                tt(t16, v16, along(bonus, DH), ALU.mult)
                then(tt(y_q, y_q, over(ln_q[:, 1, :], TT), ALU.add))
                then(tt(y16, y16, t16, ALU.add))
                for n in range(2):
                    wait_read(dve, b0 + n)
                tt(y_q, y_q, g_q, ALU.mult).then_inc(sem("rwkv_o_ready"), 1)
                join(dve)
            have(dve, "nsa")
            b0 = base["cmp"]
            for hid in (hid_k, hid_v):
                dve.memset(hid[:, :, 31:32], 0.0)
            for n, hid in enumerate((hid_k, hid_v)):
                j = b0 + n
                wait_full(dve, j)
                then(dve.tensor_copy(hb, ps(j)[:, 128:130]))
                read(j, ts(hx, ps(j)[:, 0:124], hb[:, 0:1], None, ALU.add))
                wait_read(dve, j)
                then(tt(h2, hx, hx, ALU.mult))
                then(ts(h2, h2, 0.044715, 1.0, ALU.mult, ALU.add))
                tt(h2, h2, hx, ALU.mult).then_inc(sem("gelu_arg"), 1)
                dve.wait_ge(sem("gelu_sig"), n + 1)
                ins = tt(hid[:, :, 0:31], hx.rearrange("p (g n) -> p g n", g=4), hs.rearrange("p (g n) -> p g n", g=4),
                         ALU.mult)
                if n == 0:
                    ins.then_inc(sem("hidden_ready"), 1)
                    dve.wait_ge(sem("hidden_ready"), 1)
                else:
                    then(ins)
                    for g in range(4):
                        ins = dve.tensor_copy(hid4[:, g], over(hid[:, g, :], 4))
                    ins.then_inc(sem("hidden_ready"), 1)
            j = b0 + 3
            wait_full(dve, j)
            for g in range(4):
                ins = tt(v_bd[:, g], over(ps(j)[:, g * DH:(g + 1) * DH], 4), along(v_mask, DH), ALU.mult)
            read(j, ins)
            wait_read(dve, base["np"] + 24)
            for i in range(TT):
                j = b0 + 4 + 5 * i
                sc = c_sc[:, i % 2, :]
                s3 = sc.rearrange("p (h n) -> p h n", n=32)
                s4 = sc.rearrange("p (g x n) -> p g x n", x=2, n=P)
                bias4 = c_bias[:, i, :].rearrange("p (g x n) -> p g x n", x=2, n=P)
                if i >= 2:
                    wait_full(dve, j - 10 + 2)
                for x in range(2):
                    wait_full(dve, j + x)
                    read(j + x, tt(s4[:, :, x, :], ps(j + x)[:, 0:256].rearrange("p (g n) -> p g n", g=2),
                                   bias4[:, :, x, :], ALU.add))
                for x in range(2):
                    wait_read(dve, j + x)
                then(dve.reduce_max(stat[:, 104:120], s3, axis=AX.X))
                tt(s3, s3, along(stat[:, 104:120], 32), ALU.subtract).then_inc(sem("cmp_shifted"), 1)
                dve.wait_ge(sem("cmp_exp"), i + 1)
                then(tt(s3, s3, over(c_01[:, i, :], 16), ALU.mult))
                then(dve.reduce_sum(stat[:, 120:136], s3, axis=AX.X))
                then(ts(stat[:, 120:136], stat[:, 120:136], TINY, None, ALU.max))
                then(dve.reciprocal(stat[:, 136:152], stat[:, 120:136]))
                then(tt(stat[:, 136:152], stat[:, 136:152], gates[:, i, :].rearrange("p (h b) -> p h b", b=3)[:, :, 0],
                        ALU.mult))
                tt(s3, s3, along(stat[:, 136:152], 32), ALU.mult).then_inc(sem("cmp_probs"), 1)
            join(dve)
            def nsa_bias(u):
                h, i = u // 8, u // 2 % TT
                dve.wait_ge(sem("slopes_ready"), h + 1)
                return tab[:, h % 2, 384 - P * i:512]

            def nsa_finish(u, j):
                h, i, br = u // 8, u // 2 % TT, 1 + u % 2
                then(tt(stat[:, 36:37], stat[:, 28:29], gates[:, i, 3 * h + br:3 * h + br + 1], ALU.mult))
                o = nsa_o[:, i, h * DH:(h + 1) * DH]
                read(j, stt(o, ps(j)[:, 0:DH], stat[:, 36:37], o, ALU.mult, ALU.add))
                wait_read(dve, j)

            attend("nsa", nsa_units(), nsa_bias, nsa_finish)
            ts(stat[:, 29:30], stat[:, 28:29], 1.0).then_inc(sem("nsa_o_ready"), 1)
            join(dve)
            for hf in range(2):
                b0 = base["merge"] + 16 * hf
                for c in range(4):
                    j = b0 + 8 + c
                    wait_read(dve, b0 + c)
                    wait_full(dve, j)
                    read(j, tt(m_t[:, 4 * hf + c, :], ps(j), sig_a[:, c, :], ALU.mult))
                for c in range(4):
                    j = b0 + 12 + c
                    wait_read(dve, b0 + 4 + c)
                    wait_full(dve, j)
                    if 4 * hf + c >= 2:
                        dve.wait_ge(sem("merged"), 4 * hf + c - 1)
                    read(j, tt(m_tmp[:, c % 2, :], ps(j), sig_b[:, c, :], ALU.mult))
                    wait_read(dve, j)
                    wait_read(dve, b0 + 8 + c)
                    m = m_t[:, 4 * hf + c, :]
                    tt(m, m, m_tmp[:, c % 2, :], ALU.add).then_inc(sem("merged"), 1)
            have(dve, "y2")
            residual("y2", 1, y_tok2, gain2, sem("x_ready"))
            join(dve)
            norm(2, norm_3, "ffn_pre")
            join(dve)
            for n in range(11):
                for m in range(4):
                    u = 4 * n + m
                    tile = 2 * n + m if m < 2 else FF_TILES + 2 * n + m - 2
                    if n and m >= 2:
                        dve.wait_ge(sem("act_ready"), 2 * n)
                    if n and m < 2:
                        dve.wait_ge(sem("act_ready"), 2 * n)
                    z, o = ff_pad[:, u % 4, :], ff_c[:, m, :]
                    cw = 3 * tile
                    wait_read(dve, base["ff"] + u)
                    then(ts(o, z[:, 2:514], params("conv_w", cw + 2), params("conv_b", tile), ALU.mult, ALU.add))
                    then(stt(o, z[:, 1:513], params("conv_w", cw + 1), o, ALU.mult, ALU.add))
                    stt(o, z[:, 0:512], params("conv_w", cw), o, ALU.mult, ALU.add).then_inc(sem("conv_done"), 1)
                for m in range(2):
                    dve.wait_ge(sem("ff_sig"), 2 * n + m + 1)
                    then(tt(ff_c[:, m, :], ff_c[:, m, :], ff_s[:, m, :], ALU.mult))
                    if m == 0:
                        dve.wait_ge(sem("conv_done"), 4 * n + 4)
                    tt(act_t[:, 2 * n + m, :], ff_c[:, m, :], ff_c[:, 2 + m, :], ALU.mult).then_inc(sem("act_ready"), 1)
            have(dve, "y3")
            residual("y3", 2, y_tok3, gain3, sem("result_ready"))
            join(dve)


def _constants():
    import numpy as np

    f = np.float32
    p, t = np.arange(P)[:, None], np.arange(512)[None, :]
    c = t[:, :P]
    same = lambda n: (p // n == c // n)
    stay = np.zeros((P, N_CCOLS), f)
    stay[:, 0:128] = p == c
    stay[:, 128:256] = same(DH)
    stay[:, 256:768] = t - 384 - p
    stay[:, 768:1280] = np.where(t - 384 > p, BIG_NEG, 0.0)
    z_sel = np.zeros((P, 192), f)
    z_sel[:DH, 64] = 1
    z_sel[DH:, 128] = 1
    sel_b = np.zeros((P, DH, P), f)
    for v in range(DH):
        sel_b[v, v, :DH] = 1
        sel_b[DH + v, v, DH:] = 1
    inv_count = np.zeros((P, 2, 512), f)
    for g, w in enumerate((2, 4, 8, 16)):
        inv_count[(g % 2) * DH:(g % 2) * DH + DH, g // 2] = 1.0 / np.minimum(t + 1.0, w)
    sel8 = np.zeros((8, 8, P), f)
    for h in range(8):
        sel8[h, h] = 1
    rwkv = np.zeros((P, 1666), f)
    rwkv[:, 0:512] = np.concatenate([p < c, p <= c, p < c, p <= c], 1)
    rwkv[:, 512:640] = c < p
    rwkv[:, 640:768] = same(16)
    for m, n in enumerate((32, 64, 128)):
        rwkv[:, 768 + P * m:896 + P * m] = same(n) & ~same(n // 2)
    rwkv[:, 1152:1664] = t % P != 0
    rwkv[:DH, 1664] = 1
    rwkv[DH:, 1665] = 1
    n = np.arange(32)
    tok = (np.arange(TT)[None, :, None] * P + np.arange(P)[:, None, None]).astype(f)
    seen = (16 * n + 31 <= tok) & (n < CMP_N)
    slopes = 2.0 ** (-8.0 * np.arange(1, 17) / 16)
    bias = -slopes.astype(f)[None, None, :, None] * (tok - (16 * n + 15.5).astype(f))[:, :, None, :]
    bias = np.where(seen[:, :, None, :], bias, BIG_NEG).astype(f)
    v_mask = (p // 32 == np.arange(4)[None, :]).astype(f)
    return {"c_stay": stay, "c_z_sel": z_sel, "c_sel_b": sel_b, "c_inv_count": inv_count, "c_sel8": sel8,
            "c_rwkv": rwkv, "c_cmp_bias": bias.reshape(P, TT, 512), "c_cmp_01": seen.astype(f),
            "c_v_mask": v_mask}


def _layouts(a):
    import numpy as np

    par = np.zeros((P, N_PCOLS), np.float32)

    def put(name, x, parts=P):
        at, n = PCOLS[name]
        par[0:parts, at:at + n] = x

    def by_tile(v):
        return v.reshape(-1, P).T

    mu = a["rwkv_mu_2"][0]
    put("pre_norm", by_tile(a["pre_norm_g"][0]))
    put("mix_pre", by_tile(a["norm_mix_pre_2"][0]))
    put("ffn_pre", by_tile(a["norm_ffn_pre_2"][0]))
    put("hgrn_norm", by_tile(a["hgrn_norm_g"][0]))
    put("pool_scale", by_tile(a["pool_scale"][0]))
    put("fox_bias", a["fox_f_bias"][0][:, None], 8)
    put("mu_rkv", by_tile(mu[:3072]))
    at = PCOLS["mu_lora"][0]
    par[:, at:at + 2] = by_tile(mu[3072:3328])
    par[0:32, at + 2] = mu[3328:]
    for name in ("w0", "a0", "k_k", "k_a"):
        put(name, by_tile(a[f"rwkv_{name}_2"][0]))
    put("r_k", by_tile(a["rwkv_r_k_2"][0].reshape(-1)))
    put("conv_w", a["ffn_conv_w_2"][0].reshape(3, 2 * FF_TILES, P).transpose(2, 1, 0).reshape(P, -1))
    put("conv_b", by_tile(a["ffn_conv_b_2"][0]))
    pool_w = np.zeros((P, 2, P), np.float32)
    for g in range(4):
        s = slice((g % 2) * DH, (g % 2) * DH + DH)
        pool_w[s, g // 2, s] = a["pool_w"][0, g]
    return {"c_par": par, "c_pool_w": pool_w,
            "c_lora_w": np.concatenate([a["rwkv_w2_2"][0], a["rwkv_a2_2"][0]], 0),
            "c_pos_k": a["cmp_pos_k_2"][0].reshape(16, 2, DH).transpose(1, 2, 0).reshape(P, 16),
            "c_pos_v": a["cmp_pos_v_2"][0].reshape(16, 2, DH).transpose(1, 2, 0).reshape(P, 16)}


_WHOLE = ["w_in", "w_out", "w_in_2", "rwkv_g2_2", "cmp_w1_k_2", "cmp_w2_k_2", "cmp_w1_v_2", "cmp_w2_v_2",
          "w_branch_rwkv_2", "w_branch_nsa_2", "w_out_2", "ffn_up_2", "ffn_down_2"]
_ROWS = {"g_post": "post_norm_g", "g_mix_post": "norm_mix_post_2", "g_ffn_post": "norm_ffn_post_2",
         "g_ln_w": "rwkv_ln_w_2", "g_ln_b": "rwkv_ln_b_2"}


def kernel(**inputs):
    import numpy as np
    import concourse.bacc as bacc
    from concourse.bass_utils import run_bass_kernel_spmd

    a = {name: np.asarray(v) for name, v in inputs.items()}
    arrays = {"x": a["x"][0], **{name: a[name][0] for name in _WHOLE}, **_layouts(a), **_constants(),
              **{name: a[src] for name, src in _ROWS.items()}}
    arrays = {name: np.ascontiguousarray(v) for name, v in arrays.items()}
    nc = bacc.Bacc("TRN2", target_bir_lowering=False, num_devices=1)
    d = {name: nc.dram_tensor(f"in_{name}", v.shape, FP32, kind="ExternalInput").ap() for name, v in arrays.items()}
    for name in _ROWS:
        d[name] = d[name].broadcast_to([P, D])
    x_saved = nc.dram_tensor("x_saved", [T, D], FP32).ap()
    out = nc.dram_tensor("out_x", [T, D], FP32, kind="ExternalOutput").ap()
    build_program(nc, d, x_saved, out)
    r = run_bass_kernel_spmd(nc, [{f"in_{name}": v for name, v in arrays.items()}], core_ids=[0])
    return np.asarray(r.results[0]["out_x"]).reshape(1, T, D)
```

```python
import concourse.bass as bass
from concourse import mybir
from contextlib import ExitStack

FP32 = mybir.dt.float32
FP32R = mybir.dt.float32r
ALU = mybir.AluOpType
ACT = mybir.ActivationFunctionType
AX = mybir.AxisListType

P = 128
T = 512
TT = T // P
D = 1024
KT = D // P
DH = 64
EPS = 1e-6
TINY = 1e-30
BIG_NEG = -1e30
BANKS = 6
FOX_HEADS = 8
RWKV_COLS = 3360
NSA_COLS = 2608
NSA_HEADS, NSA_GROUPS = 16, 4
D_FF = 2816
FF_TILES = D_FF // P
CMP_N = 31
LOG_DECAY = -0.6065306597126334
MID = 38.8
ARENA = 43200

PCOLS = {}


def _pack(names):
    at = 0
    for name, n in names:
        PCOLS[name] = (at, n)
        at += n
    return at


RAW_SLOTS = 3
SLOT = 2048
PIECE = 1024
RAW_AT = ARENA
HI_AT = RAW_AT + RAW_SLOTS * SLOT
MEMORY = HI_AT + 2 * PIECE

N_PCOLS = _pack([("pre_norm", KT), ("mix_pre", KT), ("ffn_pre", KT), ("hgrn_norm", 2), ("pool_scale", 2),
                 ("fox_bias", 1), ("mu_rkv", 24), ("mu_lora", 3), ("w0", KT), ("a0", KT), ("k_k", KT),
                 ("k_a", KT), ("r_k", KT), ("conv_w", 3 * 2 * FF_TILES), ("conv_b", 2 * FF_TILES)])
CCOLS = {"ident": (0, 128), "head_ones": (128, 128), "dist": (256, 512), "mask": (768, 512)}
N_CCOLS = 1280
LAG_H = 4
LAG_T, LAG_V = 2, 4


def build_program(nc, d, x_saved, out):
    with ExitStack() as ctx:
        sems = {}

        def sem(name):
            if name not in sems:
                sems[name] = ctx.enter_context(nc.semaphore(name))
            return sems[name]

        def tensor(name, words):
            return ctx.enter_context(nc.sbuf_tensor(name, [P, words], FP32))

        const = tensor("const", N_CCOLS)
        par = tensor("par", N_PCOLS)
        stat = tensor("stat", 256)
        start = (nc.sbuf_base + 31) // 32 * 32
        tensor("memory", MEMORY)
        arena = nc.alloc_sbuf_tensor_at("arena", [P, ARENA], FP32, offset=start)
        bank = [ctx.enter_context(nc.psum_tensor(f"bank{b}", [P, 512], FP32)) for b in range(8)]

        def words(dims):
            n = 1
            for x in dims:
                n *= x
            return n

        def view(at, *dims, of=arena):
            n = words(dims)
            v = of[:, at:at + n]
            if len(dims) == 2:
                v = v.rearrange("p (a b) -> p a b", a=dims[0])
            elif len(dims) == 3:
                v = v.rearrange("p (a b c) -> p a b c", a=dims[0], b=dims[1])
            elif len(dims) == 4:
                v = v.rearrange("p (a b c e) -> p a b c e", a=dims[0], b=dims[1], c=dims[2])
            return v

        def named(name, at, *dims, dtype=FP32R):
            return view(0, *dims, of=nc.alloc_sbuf_tensor_at(name, [P, words(dims)], dtype, offset=start + 4 * at))

        raw_ring, raw_ring_r = (nc.alloc_sbuf_tensor_at(name, [P, RAW_SLOTS * SLOT], dtype, offset=start + 4 * RAW_AT)
                                for name, dtype in (("weights", FP32), ("weights_lo", FP32R)))
        hi_ring = nc.alloc_sbuf_tensor_at("weights_hi", [P, 2 * PIECE], FP32R, offset=start + 4 * HI_AT)

        def params(name, k=0, parts=P):
            at = PCOLS[name][0] + k
            return par[0:parts, at:at + 1]

        def cst(name):
            at, n = CCOLS[name]
            return const[:, at:at + n]

        def over(ap, n):
            return ap.unsqueeze(1).broadcast_to([P, n, ap.shape[1]])

        def along(ap, n):
            return ap.unsqueeze(2).broadcast_to([P, ap.shape[1], n])

        ident, head_ones = cst("ident"), cst("head_ones")
        dist, causal = cst("dist"), cst("mask")

        x_tok = view(0, TT, D)
        h_hi, h_lo = named("h_hi", 4096, KT, T), named("h_lo", 8192, KT, T)
        S0 = 12288
        mix_t = named("mix_t", S0, KT, T, dtype=FP32)
        mix_lo, mix_hi = named("mix_lo", S0, KT, T), named("mix_hi", 4096, KT, T)
        at = S0 + 4096
        q_a, f_a, k_a, _, silu_ga, u_b, silu_gb = (view(at + 1024 * n, 2, T) for n in range(7))
        i_a = named("i_a", at + 3072, 2, T, dtype=FP32)
        i_lo = named("i_lo", at + 3072, 2, T)
        y_tok1 = view(at, TT, D)
        gain1 = view(at + 4096, D)
        at += 7168
        q_c, k_c, silu_gc, v_c = (view(at + 2048 * n, *((4, T) if n < 3 else (TT, 512))) for n in range(4))
        at += 8192
        sig = view(at, 2, T)
        i_hi = named("i_hi", at, 2, T)
        at += 1024
        fc_x = view(at, T)
        at += 512
        pool_w = view(at, 2, P)
        z_sel = view(at + 256, 192)
        inv_count = view(at + 448, 2, T)
        at += 1472
        pool_pad = view(4096, 2, 528)
        pool_s = view(4096 + 1056, 2, 528)
        hg_u = view(4096 + 2112, 3, T)
        hg_kv = view(4096 + 3648, 3, T)
        hg_s = view(4096 + 5184, 3, T)
        hg_sq = view(4096 + 6720, 2, T)
        norm_1 = view(at, TT, D)
        sel_b, sel_r = named("sel_b", at, DH, P, dtype=FP32), named("sel_r", at, DH, P)
        fox_o = view(at, TT, 512)
        fox_att = at + 2048
        sel8 = view(at + 5632, 8, P)
        fc_abs, fc_ls, fc_neg = (view(at + 6656 + 512 * n, T) for n in range(3))
        fc_e = fc_abs
        k_p = view(S0 + 4096, 8, T)
        fc_tab = view(8192, 8, T)
        at += 8192
        assert at <= ARENA, at
        oa_t = named("oa_t", S0, KT, T, dtype=FP32)
        norm_2 = view(S0 + 16384, TT, D)
        at = S0 + 4096
        lo_wa, lo_g1, lo_g2 = view(at, T), view(at + 512, T), view(at + 1024, T)
        at += 1536
        lora_w, g2_a, g2_b = view(at, D), view(at + 1024, D), view(at + 2048, D)
        at += 3072
        masks_at = at
        m_gram, m_low, m_blk = view(at, 512), view(at + 512, P), view(at + 640, P)
        m_e = view(at + 768, 3, P)
        m_reset, head_sel = view(at + 1152, T), view(at + 1664, 2)
        at += 1666 + 2
        a_r = view(at, 2, TT, 2, P)
        b_h, k_h = view(at + 2048, 2, T), view(at + 3072, 2, T)
        at += 4096
        v_tok, b_tok, k_tok = (view(at + 1024 * n, TT, 256) for n in range(3))
        at += 3072
        bonus, last_p = view(at, 16), view(at + 16, 8)
        state = view(at + 24, 2, P)
        rhs_b, sa_b = view(at + 280, 256), view(at + 536, 256)
        st_tmp = view(at + 792, 256)
        at += 1048
        gram = view(at, TT, 4, 512)
        inv, invt = (view(at + 8192 + 2048 * n, TT, 4, P) for n in range(2))
        low, pw = view(0, TT, 4, P), view(2048, TT, 4, P)
        pwt = gram[:, :, :, 0:P]
        r_q, k_q, v_q, lw_q, b_q, pm_q, pi_q, pp_q, av_q, kk_q, t1_q, t2_q = (
            view(1024 * n if n < 4 else at + 1024 * (n - 4), 2, T) for n in range(12))
        z_pad = view(at + 8192, 2, 514)
        z_d = view(at + 8192 + 1028, 2, T)
        y_q, g_q, t3_q = (view(1024 * n, TT, 256) for n in range(3))
        ln_q = view(3072, 2, 256)
        sq_c = view(3584, 256)
        at = S0 + 4096
        q_n = view(at, KT, T)
        ob_hi, ob_lo = named("ob_hi", at, KT, T), named("ob_lo", at + 4096, KT, T)
        at += 4096
        k_s, k_w = view(at, 4, T), view(at + 2048, 4, T)
        v_s, v_w = view(at + 4096, TT, 256), view(at + 5120, TT, 256)
        at += 6144
        xk, xv = view(at, 4, T), view(at + 2048, 4, T)
        nsa_att = at
        at += 4096
        gates, gl_w = view(at, TT, 48), named("gate_w", at + 192, KT, 48, dtype=FP32)
        gl_hi, gl_lo = named("gate_w_hi", at + 576, KT, 48), named("gate_w_lo", at + 192, KT, 48)
        at += 960
        w1k, w1v = view(at, 16, P), view(at + 2048, 16, P)
        tab = view(at, 2, T)
        at += 4096
        w2k, w2v, pos_k, pos_v = view(at, DH), view(at + 64, DH), view(at + 128, 16), view(at + 144, 16)
        at += 160
        hb, hx, h2, hid_k, hid_v = (view(at, 2), view(at + 2, 124), view(at + 126, 124),
                                    view(at + 250, 4, 32), view(at + 378, 4, 32))
        hs = view(at + 506, 124)
        at += 630
        hid4 = view(at, 4, 4, 32)
        k_cmp = view(at + 512, 2, 32)
        at += 576
        v_bd = view(at, 4, 4, DH)
        at += 1024
        c_bias, c_01, v_mask = view(at, TT, 16 * 32), view(at + 2048, TT, 32), view(at + 2176, 4)
        at += 2180
        c_sc, c_pt = view(at, 2, 512), view(at + 1024, 2, 512)
        at += 2048
        assert at <= ARENA, at
        nsa_o = view(0, TT, D)
        oa_hi, oa_lo = named("oa_hi", 0, KT, T), named("oa_lo", S0, KT, T)
        at = S0 + 12288
        sig_a, sig_b = view(at, 4, T), view(at + 2048, 4, T)
        m_t = named("m_t", at + 4096, KT, T, dtype=FP32)
        m_lo, m_hi = named("m_lo", at + 4096, KT, T), named("m_hi", at + 8192, KT, T)
        m_tmp = view(at + 12288, 2, T)
        y_tok2 = view(at + 13312, TT, D)
        gain2 = view(at + 17408, D)
        act_t = named("act_t", S0 + FF_TILES * T, FF_TILES, T, dtype=FP32)
        act_hi, act_lo = named("act_hi", S0, FF_TILES, T), named("act_lo", S0 + FF_TILES * T, FF_TILES, T)
        norm_3 = view(S0, TT, D)
        at = S0 + 2 * FF_TILES * T
        ff_pad = view(at, 4, 514)
        ff_c = named("ff_c", at + 2056, 4, T, dtype=FP32)
        ff_s = named("ff_s", at + 2056 + 2048, 2, T, dtype=FP32)
        gain3 = view(at + 2056 + 3072, D)
        y_tok3 = view(8192, TT, D)

        base = {}
        total = [0]

        def jobs(name, n):
            base[name] = total[0]
            total[0] += n

        def attention_jobs(name, units, tables=False):
            order = {}
            for s in range(units + LAG_V):
                for h in table_heads(s) if tables else ():
                    order["B", h] = total[0]
                    total[0] += 1
                for kind, u in (("S", s), ("T", s - LAG_T), ("V", s - LAG_V)):
                    if 0 <= u < units:
                        order[kind, u] = total[0]
                        total[0] += 1
            base[name] = order

        def table_heads(s):
            return [0, 1] if s == 0 else [s // TT + 1] if s % TT == 0 and s // TT + 1 < FOX_HEADS else []

        jobs("n1", KT)
        jobs("p1", 29)
        jobs("hg", 2 * DH)
        jobs("hn", 2)
        jobs("pool", 2)
        attention_jobs("fox", FOX_HEADS * TT, True)
        jobs("ft", 4)
        jobs("y1", 8)
        jobs("n2", KT)
        jobs("lora", 3)
        for q in range(4):
            jobs(("ra", q), 19)
            jobs(("rb", q), 92)
            jobs(("rc", q), 19)
        jobs("np", 25)
        jobs("cmp", 24)
        attention_jobs("nsa", NSA_HEADS * TT * 2)
        jobs("nt", KT)
        jobs("merge", 32)
        jobs("y2", 8)
        jobs("n3", KT)
        jobs("ff", 44)
        jobs("y3", 8)

        def powers(q, kind, lev, c):
            b1 = base["rb", q] + 24 + 12 * lev
            return b1 + {"a": c, "b": 4 + 2 * c, "d": (5 + 2 * c) if lev < 2 else 4 + c}[kind]

        def merges(q, kind, m, c):
            b1 = base["rb", q] + 60 + 12 * m
            return base["rb", q] + 56 + c if m < 0 else b1 + {"u": 0, "y": 4, "x": 8}[kind] + c

        def later_half(t, m):
            return t.rearrange("p h (n two b) -> p h n two b", two=2, b=16 << m)[:, :, :, 1, :]

        full = [sem(f"bank_full{b}") for b in range(BANKS)]
        free = [sem(f"bank_free{b}") for b in range(BANKS)]

        def ps(j):
            return bank[j % BANKS][:, :]

        def wait_full(eng, j):
            eng.wait_ge(full[j % BANKS], j // BANKS + 1)

        def wait_read(eng, j):
            eng.wait_ge(free[j % BANKS], j // BANKS + 1)

        def claim(pe, j):
            if j >= BANKS:
                pe.wait_ge(free[j % BANKS], j // BANKS)

        def cols(w, a, b):
            return w.rearrange("(k p) c -> p k c", p=P)[:, :, a:b]

        uses = []
        pieces = []
        released = []
        piece_of = {}
        token_reads = [0]

        def add_use(loads, k, width, cuts, releases):
            n = len(uses)
            at = (n % RAW_SLOTS) * SLOT
            raw, raw_r = view(at, k, width, of=raw_ring), view(at, k, width, of=raw_ring_r)
            uses.append([(raw[:, :, a:a + src.shape[2]], src) for a, src in loads])
            for (ks, cs), (how, value) in zip(cuts, releases):
                p = len(pieces)
                nk, nc_ = ks.stop - ks.start, cs.stop - cs.start
                hi = view((p % 2) * PIECE, nk, nc_, of=hi_ring)
                pieces.append((n, raw[:, ks, cs], raw_r[:, ks, cs], hi))
                released.append((how, value))
                if how == "job":
                    piece_of[value] = p

        def channels(job, *loads):
            width = sum(src.shape[2] for _, src in loads)
            cuts = [(slice(0, KT), slice(a, min(a + P, width))) for a in range(0, width, P)]
            add_use(loads, KT, width, cuts, [("job", job + n) for n in range(len(cuts))])

        def tokens(job, w, a, width, rows=D):
            per_piece = PIECE // width
            k = 0
            while k < rows // P:
                nk = min(2 * per_piece, rows // P - k)
                src = w[k * P:(k + nk) * P, a:a + width].rearrange("(k p) c -> p k c", p=P)
                cuts = [(slice(x, x + per_piece), slice(0, width)) for x in range(0, nk, per_piece)]
                last = k + nk == rows // P
                ends = []
                for n in range(len(cuts)):
                    if last and n == len(cuts) - 1:
                        ends.append(("job", job + TT - 1))
                    else:
                        token_reads[0] += 1
                        ends.append(("read", token_reads[0]))
                add_use([(0, src)], nk, width, cuts, ends)
                k += nk
            for i in range(TT - 1):
                piece_of[job + i] = piece_of[job + TT - 1]

        w1, w2 = d["w_in"], d["w_in_2"]
        b0 = base["p1"]
        for n in range(10):
            channels(b0 + 2 * n, (0, cols(w1, 256 * n, 256 * n + 256)))
        tokens(b0 + 20, w1, 2560, 512)
        for n in range(2):
            channels(b0 + 24 + 2 * n, (0, cols(w1, 3072 + 256 * n, 3328 + 256 * n)))
        channels(b0 + 28, (0, cols(w1, 3592 - 104, 3592)))
        for hf in range(2):
            tokens(base["y1"] + 4 * hf, d["w_out"], 512 * hf, 512)
        channels(base["lora"], (0, cols(w2, 3072, 3328)))
        channels(base["lora"] + 2, (0, cols(w2, RWKV_COLS - P, RWKV_COLS)))
        for q in range(4):
            for n in range(3):
                channels(base["ra", q] + 2 * n, (0, cols(w2, 1024 * n + 256 * q, 1024 * n + 256 * q + 256)))
        nb = RWKV_COLS
        b0 = base["np"]
        for n in range(4):
            loads = []
            for x in range(2):
                for half in range(2):
                    a = nb + (2 * (n // 2) + half) * 256 + (2 * (n % 2) + x) * DH
                    loads.append((x * P + half * DH, cols(w2, a, a + DH)))
            channels(b0 + 2 * n, *loads)
        for n in range(3):
            channels(b0 + (8, 10, 12)[n], (0, cols(w2, nb + 1024 + 256 * n, nb + 1280 + 256 * n)))
        tokens(b0 + 14, w2, nb + 1792, 256)
        channels(b0 + 18, (0, cols(w2, nb + 2048, nb + 2304)))
        tokens(b0 + 20, w2, nb + 2304, 256)
        zg = RWKV_COLS + NSA_COLS
        for hf in range(2):
            for m, (w, a) in enumerate(((w2, zg), (w2, zg + D), (d["w_branch_rwkv_2"], 0), (d["w_branch_nsa_2"], 0))):
                for n in range(2):
                    c0 = a + 512 * hf + 256 * n
                    channels(base["merge"] + 16 * hf + 4 * m + 2 * n, (0, cols(w, c0, c0 + 256)))
        for hf in range(2):
            tokens(base["y2"] + 4 * hf, d["w_out_2"], 512 * hf, 512)
        for n in range(11):
            for m in range(2):
                channels(base["ff"] + 4 * n + 2 * m,
                         (0, cols(d["ffn_up_2"], D_FF * m + 256 * n, D_FF * m + 256 * n + 256)))
        for hf in range(2):
            tokens(base["y3"] + 4 * hf, d["ffn_down_2"], 512 * hf, 512, rows=D_FF)

        loaded_at = []
        for n, loads in enumerate(uses):
            loaded_at.append(16 * len(loads) + (loaded_at[n - RAW_SLOTS] if n >= RAW_SLOTS else 0))
        w_loaded = [sem(f"w_loaded{n}") for n in range(RAW_SLOTS)]
        w_hi, w_lo, w_read = sem("w_hi"), sem("w_lo"), sem("w_read")

        def wait_released(eng, p):
            how, value = released[p]
            if how == "job":
                wait_full(eng, value)
            else:
                eng.wait_ge(w_read, value)

        phase_done = sem("phase_done")

        def counter():
            count = [0]

            def join(eng):
                count[0] += 1
                eng.drain().then_inc(phase_done, 1)
                eng.wait_ge(phase_done, 4 * count[0])
            return join

        x_in, x_out = sem("x_in"), sem("x_out")
        load_total = {}

        def phase_loads(act, name, pairs):
            for dst, src in pairs:
                act.dma_start(dst, src).then_inc(sem("loaded_" + name), 16)

        def plan_loads(name, pairs):
            load_total[name] = 16 * len(pairs)
            return pairs

        def have(eng, name, times=1):
            eng.wait_ge(sem("loaded_" + name), load_total[name] * times)

        L_START = plan_loads("start", [(const[:, :], d["c_stay"]), (par[:, :], d["c_par"]),
                                       (pool_w, d["c_pool_w"]),
                                       (z_sel, d["c_z_sel"]), (inv_count, d["c_inv_count"])])
        L_SEL = plan_loads("sel", [(sel_b, d["c_sel_b"])])
        L_FOX = plan_loads("fox", [(sel8[0:8], d["c_sel8"])])
        L_Y1 = plan_loads("y1", [(gain1, d["g_post"])])
        L_RW = plan_loads("rwkv", [(lora_w, d["c_lora_w"]), (g2_a, d["rwkv_g2_2"][0:128, :]),
                                   (g2_b[96:128], d["rwkv_g2_2"][128:160, :]),
                                   (view(masks_at, 1666), d["c_rwkv"])])
        L_LN = [plan_loads("ln", [(ln_q[:, 0, :], d["g_ln_w"][:, 256 * q:256 * q + 256]),
                                       (ln_q[:, 1, :], d["g_ln_b"][:, 256 * q:256 * q + 256])])
                for q in range(4)]
        L_NSA = plan_loads("nsa", [(gl_w, cols(w2, RWKV_COLS + 2560, RWKV_COLS + 2608)),
                                   (w1k, d["cmp_w1_k_2"].rearrange("(j p) m -> p j m", p=P)),
                                   (w1v, d["cmp_w1_v_2"].rearrange("(j p) m -> p j m", p=P)),
                                   (w2k, d["cmp_w2_k_2"]), (w2v, d["cmp_w2_v_2"]),
                                   (pos_k, d["c_pos_k"]), (pos_v, d["c_pos_v"]),
                                   (c_bias, d["c_cmp_bias"]), (c_01, d["c_cmp_01"]), (v_mask, d["c_v_mask"])])
        L_Y2 = plan_loads("y2", [(x_tok, x_saved.rearrange("(i p) c -> p i c", p=P))])
        L_G2 = plan_loads("gain2", [(gain2, d["g_mix_post"])])
        L_Y3 = plan_loads("y3", [(gain3, d["g_ffn_post"])])

        SILU = ([(n, q_a[:, n, :]) for n in (0, 1)] + [(6 + n, silu_ga[:, n, :]) for n in (0, 1)]
                + [(10 + n, silu_gb[:, n, :]) for n in (0, 1)] + [(24 + n, silu_gc[:, n, :]) for n in range(4)])
        SILU_NO = {n: s for s, (n, _) in enumerate(SILU)}
        SILU_OUT = dict(SILU)

        def nsa_place(h):
            g, hg = h // 4, h % 4
            return slice((g % 2) * DH, (g % 2) * DH + DH), (g // 2) * 4 + hg

        def fox_units():
            units = []
            for h in range(FOX_HEADS):
                tile = h // 2
                for i in range(TT):
                    w = (i + 1) * P
                    units.append((q_c[:, tile, i * P:(i + 1) * P], k_p[:, h, 0:w], (ident, causal[:, 384:512]),
                                  [v_c[:, x, h * DH:(h + 1) * DH] for x in range(i + 1)], fox_att))
            return units

        def nsa_units():
            units = []
            for h in range(NSA_HEADS):
                half, tile = nsa_place(h)
                g = h // 4
                for i in range(TT):
                    w = (i + 1) * P
                    for k, v in ((k_s, v_s), (k_w, v_w)):
                        units.append((q_n[:, tile, i * P:(i + 1) * P], k[:, g, 0:w], None,
                                      [v[:, x, g * DH:(g + 1) * DH] for x in range(i + 1)], nsa_att))
            return units

        ATT = {"fox": 0, "nsa": FOX_HEADS * TT}

        block = ctx.enter_context(nc.Block())

        @block.sync
        def _(sp):
            for i in range(TT):
                sp.dma_start(x_tok[:, i, :], d["x"][i * P:(i + 1) * P, :]).then_inc(x_in, 16)
            for n, loads in enumerate(uses):
                if n >= RAW_SLOTS:
                    wait_released(sp, [p for p in range(len(pieces)) if pieces[p][0] == n - RAW_SLOTS][-1])
                for dst, src in loads:
                    sp.dma_start(dst, src).then_inc(w_loaded[n % RAW_SLOTS], 16)
            for i in range(TT):
                sp.wait_ge(sem("result_ready"), i + 1)
                sp.dma_start(out[i * P:(i + 1) * P, :], x_tok[:, i, :]).then_inc(sem("result_out"), 16)
            sp.wait_ge(sem("result_out"), 16 * TT)

        @block.tensor
        def _(pe):
            join = counter()

            def mm(o, w, x, first=True, last=True):
                return pe.matmul(o, w, x, start=first, stop=last)

            def fill(j, ins):
                ins.then_inc(full[j % BANKS], 1)

            def transposes(j, tiles, width=P):
                claim(pe, j)
                for i, t in enumerate(tiles):
                    ins = pe.transpose(ps(j)[:, i * P:(i + 1) * P], t, ident)
                fill(j, ins)

            def mm3(o, w, x, first, last):
                mm(o, w[0], x[0], first, False)
                mm(o, w[0], x[1], False, False)
                return mm(o, w[1], x[0], False, last)

            taken = [0]

            def take_piece():
                _, _, lo, hi = pieces[taken[0]]
                taken[0] += 1
                pe.wait_ge(w_lo, taken[0])
                return hi, lo

            def to_channels(j, x):
                w = take_piece()
                claim(pe, j)
                for k in range(KT):
                    ins = mm3(ps(j)[0:w[0].shape[2], :], [v[:, k, :] for v in w], [v[:, k, :] for v in x],
                              k == 0, k == KT - 1)
                fill(j, ins)

            def to_tokens(j0, x, width, ready=None):
                k0, kt = 0, x[0].shape[1]
                while k0 < kt:
                    w = take_piece()
                    k1 = k0 + w[0].shape[1]
                    if ready:
                        pe.wait_ge(sem(ready), k1)
                    for i in range(TT):
                        if k0 == 0:
                            claim(pe, j0 + i)
                        for k in range(k0, k1):
                            ins = mm3(ps(j0 + i)[:, 0:width], [v[:, k, i * P:(i + 1) * P] for v in x],
                                      [v[:, k - k0, :] for v in w], k == 0, k == kt - 1)
                        if k1 == kt:
                            fill(j0 + i, ins)
                    if k1 < kt:
                        ins.then_inc(w_read, 1)
                    k0 = k1

            def norm(n, xn):
                pe.wait_ge(sem("norm_scaled"), n + 1)
                for k in range(KT):
                    transposes(base["n%d" % (n + 1)] + k, [xn[:, i, k * P:(k + 1) * P] for i in range(TT)])

            def attend(name, units):
                order = base[name]
                off = ATT[name]
                for s in range(len(units) + LAG_V):
                    for h in table_heads(s) if name == "fox" else ():
                        claim(pe, order["B", h])
                        fill(order["B", h], mm(ps(order["B", h]), sel8[0:8, h, :], fc_neg[0:8, :]))
                    if name == "fox" and s % TT == 0 and s < len(units):
                        pe.wait_ge(sem("fox_zeros"), s // TT + 1)
                        pe.wait_ge(sem("fox_keys"), s // TT + 1)
                    if s < len(units):
                        q, k, extra, _, att = units[s]
                        j = order["S", s]
                        claim(pe, j)
                        w = k.shape[1]
                        ins = mm(ps(j)[:, 0:w], q, k, True, extra is None)
                        if extra is not None:
                            ins = mm(ps(j)[:, w - P:w], extra[0], extra[1], False, True)
                        fill(j, ins)
                    if 0 <= s - LAG_T < len(units):
                        u = s - LAG_T
                        _, k, _, _, att = units[u]
                        pe.wait_ge(sem("probs_ready"), off + u + 1)
                        prob = view(att, 4, T)[:, u % 4, :]
                        transposes(order["T", u], [prob[:, x * P:(x + 1) * P] for x in range(k.shape[1] // P)])
                    if 0 <= s - LAG_V:
                        u = s - LAG_V
                        _, k, _, vals, att = units[u]
                        j = order["V", u]
                        wait_read(pe, order["T", u])
                        claim(pe, j)
                        pt = view(att + 2048, 3, T)[:, u % 3, :]
                        for x, v in enumerate(vals):
                            ins = mm(ps(j)[:, 0:DH], pt[:, x * P:(x + 1) * P], v, x == 0, x == len(vals) - 1)
                        fill(j, ins)

            def project_out(name, x, ready):
                for hf in range(2):
                    to_tokens(base[name] + 4 * hf, x, 512, ready)

            h_both = (h_hi, h_lo)

            have(pe, "start")
            norm(0, norm_1)
            join(pe)
            for n in range(29):
                if n == 20:
                    to_tokens(base["p1"] + n, h_both, 512)
                elif n < 20 or n >= 24:
                    to_channels(base["p1"] + n, h_both)
            join(pe)
            pe.wait_ge(sem("i_lo"), 2)
            for n in range(2 * DH + LAG_H):
                if n < 2 * DH:
                    j = base["hg"] + n
                    claim(pe, j)
                    mm(ps(j), sel_r[:, n % DH, :], i_hi[:, n // DH, :], True, False)
                    fill(j, mm(ps(j), sel_r[:, n % DH, :], i_lo[:, n // DH, :], False, True))
                if n >= LAG_H:
                    m = n - LAG_H
                    pe.wait_ge(sem("hg_qs"), m + 1)
                    v = m % DH
                    mm(bank[6 + m // DH][:, :], z_sel[:, 64 - v:192 - v], hg_u[:, m % 3, :],
                       v == 0, v == DH - 1).then_inc(sem("hg_summed"), 1)
            for c in range(2):
                j = base["hn"] + c
                pe.wait_ge(sem("hg_squares"), c + 1)
                claim(pe, j)
                fill(j, mm(ps(j), head_ones, hg_sq[:, c, :]))
            for c in range(2):
                j = base["pool"] + c
                pe.wait_ge(sem("pooled"), c + 1)
                claim(pe, j)
                fill(j, mm(ps(j), pool_w[:, c, :], pool_s[:, c, 16:528]))
            join(pe)
            have(pe, "fox")
            pe.wait_ge(sem("fox_decay"), 1)
            attend("fox", fox_units())
            pe.wait_ge(sem("fox_o_ready"), 1)
            for k in range(4):
                transposes(base["ft"] + k, [fox_o[:, i, k * P:(k + 1) * P] for i in range(TT)])
            project_out("y1", (mix_hi, mix_lo), "mix_lo")
            join(pe)
            norm(1, norm_2)
            join(pe)
            for n in range(3):
                to_channels(base["lora"] + n, h_both)
            have(pe, "rwkv")
            pe.wait_ge(sem("lora_ready"), 1)
            for q in range(4):
                b0 = base["ra", q]
                for n in range(6):
                    to_channels(b0 + n, h_both)
                for n in range(2):
                    j = b0 + 6 + n
                    c0 = (2 * q + n) * P
                    claim(pe, j)
                    fill(j, mm(ps(j), lora_w[0:64, c0:c0 + P], lo_wa[0:64, :]))
                for n in range(2):
                    j = b0 + 8 + n
                    c0 = (2 * q + n) * P
                    claim(pe, j)
                    fill(j, mm(ps(j), lora_w[64:128, c0:c0 + P], lo_wa[64:128, :]))
                pe.wait_ge(sem("kk_squares"), q + 1)
                for n in range(2):
                    j = b0 + 10 + n
                    claim(pe, j)
                    fill(j, mm(ps(j), head_ones, t1_q[:, n, :]))
                pe.wait_ge(sem("rk_ready"), q + 1)
                j = b0 + 12
                claim(pe, j)
                for c in range(TT):
                    for n in range(2):
                        ins = mm(ps(j)[:, 4 * c + 2 * n:4 * c + 2 * n + 2], t1_q[:, n, c * P:(c + 1) * P], head_sel)
                fill(j, ins)
                pe.wait_ge(sem("operands_ready"), q + 1)
                for m, src in enumerate((v_q, b_h, k_h)):
                    for n in range(2):
                        transposes(b0 + 13 + 2 * m + n, [src[:, n, c * P:(c + 1) * P] for c in range(TT)])
                join(pe)
                b0 = base["rb", q]
                for c in range(TT):
                    for h in range(4):
                        j = b0 + 6 * c + h
                        half, n = slice((h % 2) * DH, (h % 2) * DH + DH), h // 2
                        tok = slice(c * P, (c + 1) * P)
                        claim(pe, j)
                        ar = a_r[half, n, c, :, :].rearrange("p a b -> p (a b)")
                        mm(ps(j)[:, 0:256], b_h[half, n, tok], ar)
                        fill(j, mm(ps(j)[:, 256:512], k_h[half, n, tok], ar))
                    for x in range(2):
                        j = b0 + 6 * c + 4 + x
                        half = slice(x * DH, x * DH + DH)
                        claim(pe, j)
                        for n in range(2):
                            ins = mm(ps(j)[:, n * P:(n + 1) * P], a_r[half, n, c, 0, :], b_h[half, n, tok])
                        fill(j, ins)

                def four(j, w, x, n=P):
                    claim(pe, j)
                    for h in range(4):
                        ins = mm(ps(j)[:, h * n:(h + 1) * n], w[:, h, :], x[:, h])
                    fill(j, ins)

                for lev in range(3):
                    for c in range(TT):
                        if lev == 0:
                            pe.wait_ge(sem("inv_started"), 4 * q + c + 1)
                        else:
                            wait_read(pe, powers(q, "b", lev - 1, c))
                        four(powers(q, "a", lev, c), pwt[:, c], pw[:, c])
                    for c in range(TT):
                        wait_read(pe, powers(q, "a", lev, c))
                        if lev < 2:
                            transposes(powers(q, "b", lev, c), [pw[:, c, h, :] for h in range(4)])
                        if lev:
                            wait_read(pe, powers(q, "d", lev - 1, c))
                        four(powers(q, "d", lev, c), pw[:, c], invt[:, c])
                for c in range(TT):
                    wait_read(pe, powers(q, "d", 2, c))
                    transposes(merges(q, "x", -1, c), [invt[:, c, h, :] for h in range(4)])
                for m in range(3):
                    for c in range(TT):
                        pe.wait_ge(sem("between_ready"), 12 * q + 4 * m + c + 1)
                        if m:
                            wait_read(pe, merges(q, "y", m - 1, c))
                        four(merges(q, "u", m, c), pw[:, c], later_half(invt[:, c], m), 64)
                    for c in range(TT):
                        wait_read(pe, merges(q, "u", m, c))
                        wait_read(pe, merges(q, "x", m - 1, c))
                        four(merges(q, "y", m, c), inv[:, c], pwt[:, c, :, 0:64], 64)
                    if m < 2:
                        for c in range(TT):
                            wait_read(pe, merges(q, "y", m, c))
                            transposes(merges(q, "x", m, c), [invt[:, c, h, :] for h in range(4)])
                join(pe)
                b0 = base["rc", q]
                for n in range(2):
                    j = b0 + n
                    claim(pe, j)
                    for c in range(2):
                        tok = slice((2 * n + c) * P, (2 * n + c + 1) * P)
                        mm(ps(j)[:, c * 256:(c + 1) * 256], lo_g1[:, tok], g2_a[:, 256 * q:256 * q + 256], True, False)
                        ins = mm(ps(j)[:, c * 256:(c + 1) * 256], lo_g2[:, tok],
                                 g2_b[:, 256 * q:256 * q + 256], False, True)
                    fill(j, ins)
                for c in range(TT):
                    j = b0 + 2 + 4 * c
                    if c:
                        pe.wait_ge(sem("state_ready"), 3 * q + c)
                    claim(pe, j)
                    for n in range(2):
                        if c:
                            mm(ps(j)[:, n * P:(n + 1) * P], a_r[:, n, c, 0, :], state[:, n, :], True, False)
                        for h in (2 * n, 2 * n + 1):
                            ins = mm(ps(j)[:, h * DH:(h + 1) * DH], gram[:, c, h, 256:384],
                                     v_tok[:, c, h * DH:(h + 1) * DH], c == 0, c == 0 or h % 2 == 1)
                    fill(j, ins)
                    wait_read(pe, j)
                    j += 1
                    claim(pe, j)
                    for h in range(4):
                        ins = mm(ps(j)[:, h * DH:(h + 1) * DH], invt[:, c, h, :], rhs_b[:, h * DH:(h + 1) * DH])
                    fill(j, ins)
                    wait_read(pe, j)
                    j += 1
                    claim(pe, j)
                    for n in range(2):
                        if c:
                            mm(ps(j)[:, n * P:(n + 1) * P], a_r[:, n, c, 1, :], state[:, n, :], True, False)
                        for h in (2 * n, 2 * n + 1):
                            hv = slice(h * DH, (h + 1) * DH)
                            mm(ps(j)[:, hv], gram[:, c, h, 128:256], sa_b[:, hv], c == 0, False)
                            ins = mm(ps(j)[:, hv], gram[:, c, h, 384:512], v_tok[:, c, hv], False,
                                     c == 0 or h % 2 == 1)
                    fill(j, ins)
                    if c < TT - 1:
                        j += 1
                        claim(pe, j)
                        for n in range(2):
                            ch = slice(n * P, (n + 1) * P)
                            mm(ps(j)[:, ch], b_tok[:, c, ch], sa_b[:, ch], True, False)
                            ins = mm(ps(j)[:, ch], k_tok[:, c, ch], v_tok[:, c, ch], False, True)
                        fill(j, ins)
                pe.wait_ge(sem("rwkv_o_ready"), q + 1)
                for n in range(2):
                    transposes(b0 + 17 + n, [y_q[:, c, n * P:(n + 1) * P] for c in range(TT)])
                join(pe)
            b0 = base["np"]
            for n in range(24):
                if n in (14, 20):
                    to_tokens(b0 + n, h_both, 256)
                elif n < 14 or n in (18, 19):
                    to_channels(b0 + n, h_both)
            have(pe, "nsa")
            pe.wait_ge(sem("gate_lo"), 1)
            j = b0 + 24
            claim(pe, j)
            for i in range(TT):
                for k in range(KT):
                    ins = mm3(ps(j)[:, 48 * i:48 * i + 48], [v[:, k, i * P:(i + 1) * P] for v in h_both],
                              (gl_hi[:, k, :], gl_lo[:, k, :]), k == 0, k == KT - 1)
            fill(j, ins)
            b0 = base["cmp"]
            for m, (w1, x, pos) in enumerate(((w1k, xk, pos_k), (w1v, xv, pos_v))):
                j = b0 + m
                for n in range(2):
                    wait_read(pe, base["np"] + 8 + 2 * m + n)
                claim(pe, j)
                for t in range(16):
                    mm(ps(j)[:, 0:124], w1[:, t, :], x[:, :, 2 * t:2 * t + 16 * CMP_N - 15:16], t == 0, t == 15)
                for t in range(16):
                    ins = mm(ps(j)[:, 128:130], w1[:, t, :], pos[:, t:t + 1].broadcast_to([P, 2]), t == 0, t == 15)
                fill(j, ins)
            j = b0 + 2
            pe.wait_ge(sem("hidden_ready"), 1)
            claim(pe, j)
            fill(j, mm(ps(j)[0:64, 0:128], w2k, hid_k.rearrange("p g n -> p (g n)")))
            j = b0 + 3
            pe.wait_ge(sem("hidden_ready"), 2)
            claim(pe, j)
            for g in range(4):
                ins = mm(ps(j)[:, g * DH:(g + 1) * DH], hid4[:, g].rearrange("p h n -> p (h n)"), w2v)
            fill(j, ins)
            for n in range(8):
                wait_read(pe, base["np"] + n)
            wait_read(pe, b0 + 2)
            wait_read(pe, b0 + 3)
            for i in range(TT):
                for x in range(2):
                    j = b0 + 4 + 5 * i + x
                    claim(pe, j)
                    for n in range(8):
                        half, tile = nsa_place((n // 4) * 8 + x * 4 + n % 4)
                        ins = mm(ps(j)[:, n * 32:(n + 1) * 32], q_n[half, tile, i * P:(i + 1) * P],
                                 k_cmp[half, n // 4, :])
                    fill(j, ins)
                pe.wait_ge(sem("cmp_probs"), i + 1)
                transposes(j + 1, [c_sc[:, i % 2, x * P:(x + 1) * P] for x in range(4)])
                wait_read(pe, j + 1)
                for x in range(2):
                    claim(pe, j + 2 + x)
                    for g in (2 * x, 2 * x + 1):
                        ins = mm(ps(j + 2 + x)[:, (g % 2) * 256:(g % 2) * 256 + 256],
                                 c_pt[:, i % 2, g * P:(g + 1) * P], v_bd[:, g].rearrange("p h n -> p (h n)"))
                    fill(j + 2 + x, ins)
            join(pe)
            attend("nsa", nsa_units())
            pe.wait_ge(sem("nsa_o_ready"), 1)
            for k in range(KT):
                transposes(base["nt"] + k, [nsa_o[:, i, k * P:(k + 1) * P] for i in range(TT)])
            join(pe)
            for hf in range(2):
                for m, x in enumerate((h_both, h_both, (oa_hi, oa_lo), (ob_hi, ob_lo))):
                    if hf == 0 and m == 2:
                        pe.wait_ge(sem("oa_lo"), KT)
                    for c in range(4):
                        to_channels(base["merge"] + 16 * hf + 4 * m + c, x)
            project_out("y2", (m_hi, m_lo), "m_lo")
            join(pe)
            norm(2, norm_3)
            join(pe)
            for n in range(4 * 11):
                to_channels(base["ff"] + n, h_both)
            project_out("y3", (act_hi, act_lo), "act_lo")
            join(pe)


        @block.scalar
        def _(act):
            join = counter()
            act_step = sem("act_step")
            steps = [0]

            def mark(ins):
                ins.then_inc(act_step, 1)
                steps[0] += 1
                return steps[0]

            def run(o, i, f, **kw):
                return act.activation(o, i, f, **kw)

            def read(j, ins):
                ins.then_inc(free[j % BANKS], 1)

            def copy_out(j, o, scale=1.0, width=512, parts=slice(0, P)):
                wait_full(act, j)
                read(j, run(o, ps(j)[parts, 0:width], ACT.Copy, scale=scale))

            next_piece = [0]

            def stream_to(j):
                while next_piece[0] < min(piece_of[j] + 2, len(pieces)):
                    p = next_piece[0]
                    next_piece[0] += 1
                    n, raw, _, hi = pieces[p]
                    act.wait_ge(w_loaded[n % RAW_SLOTS], loaded_at[n])
                    if p >= 2:
                        wait_released(act, p - 2)
                    run(hi, raw, ACT.Copy).then_inc(w_hi, 1)

            def hi_of(name, o, i):
                run(o, i, ACT.Copy).then_inc(sem(name + "_hi"), 1)

            def norm_hi(n, gain):
                for k in range(KT):
                    j = base["n%d" % (n + 1)] + k
                    wait_full(act, j)
                    run(h_hi[:, k, :], ps(j), ACT.Copy, scale=params(gain, k)).then_inc(sem("h_hi"), 1)

            def root(name, n, o, i):
                act.wait_ge(sem(name + "_ms"), n + 1)
                run(o, i, ACT.Sqrt).then_inc(sem(name + "_root"), 1)

            def attend(name, units):
                order = base[name]
                off = ATT[name]
                for s in range(len(units) + LAG_T):
                    for h in table_heads(s) if name == "fox" else ():
                        copy_out(order["B", h], fc_tab[:, h, :])
                    if s < len(units):
                        k, att = units[s][1], units[s][4]
                        w = k.shape[1]
                        act.wait_ge(sem("neg_max"), off + s + 1)
                        prob = view(att, 4, T)[:, s % 4, 0:w]
                        run(prob, prob, ACT.Exp, bias=stat[:, 24 + s % 8:25 + s % 8],
                            accum_out=stat[:, 152 + s % 8:153 + s % 8]).then_inc(sem("probs_ready"), 1)
                    if s >= LAG_T:
                        u = s - LAG_T
                        k, att = units[u][1], units[u][4]
                        if u >= 3:
                            wait_full(act, order["V", u - 3])
                        copy_out(order["T", u], view(att + 2048, 3, T)[:, u % 3, 0:k.shape[1]],
                                 width=k.shape[1])

            phase_loads(act, "start", L_START)
            root("norm", 0, stat[:, 8:12], stat[:, 4:8])
            stream_to(base["p1"])
            norm_hi(0, "pre_norm")
            join(act)
            phase_loads(act, "sel", L_SEL)
            for n in range(29):
                j = base["p1"] + n
                stream_to(j)
                if n in SILU_NO:
                    s = SILU_NO[n]
                    if s >= 2:
                        wait_read(act, base["p1"] + SILU[s - 2][0])
                    wait_full(act, j)
                    run(sig[:, s % 2, :], ps(j), ACT.Sigmoid).then_inc(sem("silu_sig"), 1)
                elif n in (2, 3):
                    wait_full(act, j)
                    run(f_a[:, n - 2, :], ps(j), ACT.Sigmoid).then_inc(sem("forget_ready"), 1)
                    read(j, run(k_a[:, n - 2, :], ps(j), ACT.Sigmoid, scale=-1.0))
                elif n in (4, 5):
                    copy_out(j, i_a[:, n - 4, :])
                elif n in (8, 9):
                    copy_out(j, u_b[:, n - 8, :])
                elif n in range(12, 16):
                    copy_out(j, q_c[:, n - 12, :], scale=DH ** -0.5)
                elif n in range(16, 20):
                    copy_out(j, k_c[:, n - 16, :])
                elif n == 28:
                    wait_full(act, j)
                    read(j, run(fc_x[0:8, :], ps(j)[96:104, :], ACT.Identity, bias=params("fox_bias")[96:104]))
                else:
                    copy_out(j, v_c[:, n - 20, :])
                if 8 <= n < 24:
                    have(act, "sel")
                    run(sel_r[:, 4 * n - 32:4 * n - 28, :], sel_b[:, 4 * n - 32:4 * n - 28, :], ACT.Copy)
            join(act)
            for c in range(2):
                hi_of("i", i_hi[:, c, :], i_a[:, c, :])
            for c in range(2):
                act.wait_ge(sem("hg_summed"), DH * (c + 1))
                run(hg_sq[:, c, :], bank[6 + c][:, :], ACT.Square).then_inc(sem("hg_squares"), 1)
            root("hg", 0, hg_kv[:, 0:2, :], hg_kv[:, 0:2, :])
            join(act)
            phase_loads(act, "fox", L_FOX)
            phase_loads(act, "y1", L_Y1)
            act.wait_ge(sem("fox_abs"), 1)
            m = mark(run(fc_e[0:8, :], fc_abs[0:8, :], ACT.Exp, scale=-1.0))
            act.wait_ge(act_step, m)
            run(fc_e[0:8, :], fc_e[0:8, :], ACT.Ln, bias=1.0).then_inc(sem("fox_log"), 1)
            for h in range(FOX_HEADS):
                half = slice((h % 2) * DH, (h % 2) * DH + DH)
                run(k_p[half, h, :], k_c[half, h // 2, :], ACT.Copy).then_inc(sem("fox_keys"), 1)
                if h % 2:
                    hi_of("mix", mix_hi[:, h // 2, :], mix_t[:, h // 2, :])
            attend("fox", fox_units())
            for k in range(4):
                wait_read(act, base["ft"] + k)
                hi_of("mix", mix_hi[:, 4 + k, :], mix_t[:, 4 + k, :])

            def residual(name, n, y):
                for hf in range(2):
                    for i in range(TT):
                        stream_to(base[name] + 4 * hf + i)
                        copy_out(base[name] + 4 * hf + i, y[:, i, hf * 512:(hf + 1) * 512])
                root("post", n, stat[:, 8:12], stat[:, 4:8])

            residual("y1", 0, y_tok1)
            join(act)
            act.dma_start(x_saved.rearrange("(i p) c -> p i c", p=P), x_tok).then_inc(x_out, 16)
            phase_loads(act, "rwkv", L_RW)
            root("norm", 1, stat[:, 8:12], stat[:, 4:8])
            norm_hi(1, "mix_pre")
            act.wait_ge(x_out, 16)
            join(act)
            mixes = [0]

            def to_mix(j):
                m = mixes[0]
                mixes[0] += 1
                if m >= 2:
                    act.wait_ge(sem("mixed"), m - 1)
                stream_to(j)
                copy_out(j, z_pad[:, m % 2, 1:513])

            act.wait_ge(sem("pads_zero"), 1)
            for n in range(3):
                to_mix(base["lora"] + n)
            act.wait_ge(sem("mixed"), 3)
            run(lo_wa[0:64, :], lo_wa[0:64, :], ACT.Tanh)
            run(lo_g1, lo_g1, ACT.Sigmoid)
            run(lo_g2, lo_g2, ACT.Sigmoid).then_inc(sem("lora_ready"), 1)
            for q in range(4):
                b0 = base["ra", q]
                act.wait_ge(sem("pads_zero"), 1 + q)
                for n in range(6):
                    to_mix(b0 + n)
                for n in range(2):
                    wait_full(act, b0 + 6 + n)
                    read(b0 + 6 + n, run(lw_q[:, n, :], ps(b0 + 6 + n), ACT.Sigmoid, bias=params("w0", 2 * q + n)))
                for n in range(2):
                    wait_full(act, b0 + 8 + n)
                    read(b0 + 8 + n, run(av_q[:, n, :], ps(b0 + 8 + n), ACT.Sigmoid, bias=params("a0", 2 * q + n)))
                root("kk", q, t1_q, t1_q)
                act.wait_ge(sem("decay_sums"), q + 1)
                run(pm_q, b_q, ACT.Exp, bias=stat[:, 32:33])
                run(pp_q, pp_q, ACT.Exp, bias=stat[:, 32:33])
                run(last_p, b_q.rearrange("p n (c t) -> p (n c) t", t=P)[:, :, P - 1], ACT.Exp)
                run(pi_q, b_q, ACT.Exp, bias=stat[:, 33:34], scale=-1.0).then_inc(sem("decays_ready"), 1)
                for m, dst in enumerate((v_tok, b_tok, k_tok)):
                    for n in range(2):
                        j = b0 + 13 + 2 * m + n
                        wait_full(act, j)
                        read(j, run(dst[:, :, n * P:(n + 1) * P],
                                    ps(j).rearrange("p (c x) -> p c x", c=TT), ACT.Copy))
                join(act)
                b0 = base["rb", q]

                def to_heads(j, o, n=P):
                    wait_full(act, j)
                    read(j, run(o, ps(j)[:, 0:4 * n].rearrange("p (h x) -> p h x", h=4), ACT.Copy))

                for lev in range(3):
                    for c in range(TT):
                        to_heads(powers(q, "a", lev, c), pw[:, c])
                for m in range(3):
                    for c in range(TT):
                        to_heads(merges(q, "x", m - 1, c), inv[:, c])
                    for c in range(TT):
                        to_heads(merges(q, "u", m, c), pwt[:, c, :, 0:64], 64)
                join(act)
                phase_loads(act, "ln", L_LN[q])
                b0 = base["rc", q]
                for n in range(2):
                    copy_out(b0 + n, g_q[:, 2 * n:2 * n + 2, :].rearrange("p c x -> p (c x)"))
                for c in range(TT + 1):
                    if c < TT:
                        copy_out(b0 + 2 + 4 * c, rhs_b, width=256)
                    if c:
                        root("gn", TT * q + c - 1, stat[:, 52 + 4 * c:56 + 4 * c], stat[:, 52 + 4 * c:56 + 4 * c])
                    if c < TT:
                        copy_out(b0 + 4 + 4 * c, y_q[:, c, :], width=256)
                for n in range(2):
                    copy_out(b0 + 17 + n, oa_t[:, 2 * q + n, :])
                join(act)
            phase_loads(act, "nsa", L_NSA)
            b0 = base["np"]
            for n in range(8):
                stream_to(b0 + n)
                copy_out(b0 + n, q_n[:, n, :], scale=DH ** -0.5)
            have(act, "nsa")
            hi_of("gate", gl_hi, gl_w)
            for m, dst in enumerate((xk, xv)):
                for n in range(2):
                    j = b0 + 8 + 2 * m + n
                    stream_to(j)
                    wait_full(act, j)
                    run(dst[0:64, 2 * n, :], ps(j)[0:64, :], ACT.Copy)
                    run(dst[64:128, 2 * n, 0:511], ps(j)[0:64, 1:512], ACT.Copy)
                    run(dst[0:64, 2 * n + 1, :], ps(j)[64:128, :], ACT.Copy)
                    read(j, run(dst[64:128, 2 * n + 1, 0:511], ps(j)[64:128, 1:512], ACT.Copy))
            for x, (k, v) in enumerate(((k_s, v_s), (k_w, v_w))):
                for m in range(2):
                    j = b0 + 12 + 6 * x + m
                    stream_to(j)
                    wait_full(act, j)
                    run(k[0:64, 2 * m, :], ps(j)[0:64, :], ACT.Copy)
                    read(j, run(k[64:128, 2 * m + 1, :], ps(j)[64:128, :], ACT.Copy))
                for i in range(TT):
                    stream_to(b0 + 14 + 6 * x + i)
                    copy_out(b0 + 14 + 6 * x + i, v[:, i, :], width=256)
            wait_full(act, b0 + 24)
            read(b0 + 24, run(gates.rearrange("p i g -> p (i g)"), ps(b0 + 24)[:, 0:192], ACT.Sigmoid))
            b0 = base["cmp"]
            for m in range(2):
                act.wait_ge(sem("gelu_arg"), m + 1)
                run(hs, h2, ACT.Sigmoid, scale=1.5957691216057308).then_inc(sem("gelu_sig"), 1)
            wait_full(act, b0 + 2)
            for g in range(4):
                ins = run(k_cmp[(g % 2) * DH:(g % 2) * DH + DH, g // 2, :], ps(b0 + 2)[0:64, g * 32:(g + 1) * 32], ACT.Copy)
            read(b0 + 2, ins)
            for i in range(TT):
                j = b0 + 5 + 5 * i
                act.wait_ge(sem("cmp_shifted"), i + 1)
                run(c_sc[:, i % 2, :], c_sc[:, i % 2, :], ACT.Exp).then_inc(sem("cmp_exp"), 1)
                if i >= 2:
                    wait_full(act, j - 10 + 3)
                copy_out(j + 1, c_pt[:, i % 2, :])
                for x in range(2):
                    copy_out(j + 2 + x, nsa_o[:, i, 512 * x:512 * x + 512])
            join(act)
            attend("nsa", nsa_units())
            for k in range(KT):
                wait_full(act, base["nt"] + k)
                hi_of("ob", ob_hi[:, k, :], ps(base["nt"] + k))
            join(act)
            phase_loads(act, "gain2", L_G2)
            for hf in range(2):
                b0 = base["merge"] + 16 * hf
                if hf:
                    act.wait_ge(sem("merged"), 4)
                for m, dst in enumerate((sig_a, sig_b)):
                    for c in range(4):
                        j = b0 + 4 * m + c
                        stream_to(j)
                        wait_full(act, j)
                        read(j, run(dst[:, c, :], ps(j), ACT.Sigmoid))
                        if hf == 0:
                            hi_of("oa", oa_hi[:, 4 * m + c, :], oa_t[:, 4 * m + c, :])
                for c in range(8):
                    stream_to(b0 + 8 + c)
                    if c >= 4:
                        act.wait_ge(sem("merged"), 4 * hf + c - 3)
                        hi_of("m", m_hi[:, 4 * hf + c - 4, :], m_t[:, 4 * hf + c - 4, :])
                    if hf == 1 and c == 4:
                        wait_full(act, b0 + 11)
                        phase_loads(act, "y2", L_Y2)
            residual("y2", 1, y_tok2)
            join(act)
            root("norm", 2, stat[:, 8:12], stat[:, 4:8])
            norm_hi(2, "ffn_pre")
            join(act)
            phase_loads(act, "y3", L_Y3)
            act.wait_ge(sem("ff_pads"), 1)
            for n in range(11):
                for m in range(4):
                    u = 4 * n + m
                    stream_to(base["ff"] + u)
                    if u >= 4:
                        act.wait_ge(sem("conv_done"), u - 3)
                    copy_out(base["ff"] + u, ff_pad[:, u % 4, 2:514])
                for m in range(2):
                    act.wait_ge(sem("conv_done"), 4 * n + m + 1)
                    if n:
                        act.wait_ge(sem("act_ready"), 2 * n - 1 + m)
                    run(ff_s[:, m, :], ff_c[:, m, :], ACT.Sigmoid).then_inc(sem("ff_sig"), 1)
                if n:
                    for m in (2 * n - 2, 2 * n - 1):
                        act.wait_ge(sem("act_ready"), m + 1)
                        hi_of("act", act_hi[:, m, :], act_t[:, m, :])
            for m in (FF_TILES - 2, FF_TILES - 1):
                act.wait_ge(sem("act_ready"), m + 1)
                hi_of("act", act_hi[:, m, :], act_t[:, m, :])
            residual("y3", 2, y_tok3)
            join(act)

        @block.gpsimd
        def _(pool):
            join = counter()
            pool_step = sem("pool_step")
            steps = [0]

            def after(ins):
                ins.then_inc(pool_step, 1)
                steps[0] += 1
                pool.wait_ge(pool_step, steps[0])

            join(pool)
            join(pool)
            pool.memset(pool_pad[:, :, 0:16], 0.0)
            pool.memset(pool_s[:, :, 0:16], 0.0)
            for c in range(2):
                after(pool.tensor_copy(pool_pad[:, c, 16:528], u_b[:, c, :]))
            have(pool, "start")
            for c in range(2):
                a, b = pool_pad[:, c], pool_s[:, c]
                after(pool.tensor_tensor(b[:, 16:528], a[:, 16:528], a[:, 15:527], ALU.add))
                if c == 0:
                    up = slice(64, 128)
                    after(pool.tensor_tensor(a[up, 16:528], b[up, 16:528], b[up, 14:526], ALU.add))
                    after(pool.tensor_copy(b[up, 16:528], a[up, 16:528]))
                else:
                    after(pool.tensor_tensor(a[:, 16:528], b[:, 16:528], b[:, 14:526], ALU.add))
                    after(pool.tensor_tensor(b[:, 16:528], a[:, 16:528], a[:, 12:524], ALU.add))
                    after(pool.tensor_tensor(a[up, 16:528], b[up, 16:528], b[up, 8:520], ALU.add))
                    after(pool.tensor_copy(b[up, 16:528], a[up, 16:528]))
                after(pool.tensor_tensor(b[:, 16:528], b[:, 16:528], inv_count[:, c, :], ALU.mult))
                pool.tensor_tensor(b[:, 16:528], b[:, 16:528], u_b[:, c, :], ALU.subtract).then_inc(sem("pooled"), 1)
            for n in range(2 * DH):
                pool.wait_ge(sem("hg_scanned"), n + 1)
                if n >= 3:
                    pool.wait_ge(sem("hg_summed"), n - 2)
                pool.tensor_tensor(hg_u[:, n % 3, :], hg_s[:, n % 3, :], q_a[:, n // DH, :],
                                   ALU.mult).then_inc(sem("hg_qs"), 1)
            join(pool)
            for h in range(FOX_HEADS):
                other = slice((1 - h % 2) * DH, (2 - h % 2) * DH)
                pool.memset(k_p[other, h, :], 0.0).then_inc(sem("fox_zeros"), 1)
            join(pool)
            join(pool)
            for q in range(4):
                pool.memset(z_pad[:, :, 0:2], 0.0).then_inc(sem("pads_zero"), 1)
                if q == 0:
                    pool.memset(g2_b[0:96, :], 0.0)
                join(pool)
                have(pool, "rwkv")
                for c in range(TT):
                    wait_read(pool, base["rb", q] + 6 * c + 4)
                    wait_read(pool, base["rb", q] + 6 * c + 5)
                    for h in range(4):
                        wait_read(pool, base["rb", q] + 6 * c + h)
                    blk = over(m_blk, 4)
                    after(pool.tensor_tensor(pw[:, c], low[:, c], blk, ALU.mult))
                    after(pool.tensor_tensor(pwt[:, c], gram[:, c, :, 0:128], blk, ALU.mult))
                    pool.tensor_tensor(invt[:, c], pwt[:, c], over(ident, 4), ALU.add).then_inc(
                        sem("inv_started"), 1)
                for m in range(3):
                    for c in range(TT):
                        wait_full(pool, powers(q, "d", 2, c) if m == 0 else merges(q, "u", m - 1, c))
                        pool.tensor_tensor(pw[:, c], low[:, c], over(m_e[:, m, :], 4), ALU.mult).then_inc(
                            sem("between_ready"), 1)
                join(pool)
                have(pool, "ln", q + 1)
                for n in range(2):
                    wait_read(pool, base["rc", q] + n)
                v16, t16 = (x.rearrange("p c (h v) -> p (c h) v", v=DH) for x in (v_tok, t3_q))
                after(pool.tensor_tensor(t16, v16, along(bonus, DH), ALU.mult))
                after(pool.tensor_tensor(t3_q, t3_q, over(ln_q[:, 1, :], TT), ALU.add))
                after(pool.tensor_tensor(t3_q, t3_q, g_q, ALU.mult))
                pool.tensor_tensor(g_q, g_q, over(ln_q[:, 0, :], TT), ALU.mult).then_inc(sem("gates_ready"), 1)
                join(pool)
            for k in (k_s, k_w):
                for g in range(4):
                    pool.memset(k[(1 - g % 2) * DH:(2 - g % 2) * DH, g, :], 0.0)
            join(pool)
            for h in range(NSA_HEADS):
                if h >= 2:
                    wait_read(pool, base["nsa"]["S", 8 * (h - 1) - 1])
                after(pool.tensor_scalar(tab[:, h % 2, :], dist, 2.0 ** (-8.0 * (h + 1) / NSA_HEADS), None, ALU.mult))
                pool.tensor_tensor(tab[:, h % 2, :], tab[:, h % 2, :], causal, ALU.add).then_inc(sem("slopes_ready"), 1)
            join(pool)
            join(pool)
            join(pool)
            pool.memset(ff_pad[:, :, 0:2], 0.0).then_inc(sem("ff_pads"), 1)
            join(pool)

        @block.vector
        def _(dve):
            join = counter()
            dve_step = sem("dve_step")
            steps = [0]

            def mark(ins):
                ins.then_inc(dve_step, 1)
                steps[0] += 1
                return steps[0]

            def after(step):
                dve.wait_ge(dve_step, step)

            def then(ins):
                after(mark(ins))

            def read(j, ins):
                ins.then_inc(free[j % BANKS], 1)

            def tt(o, a, b, op):
                return dve.tensor_tensor(o, a, b, op)

            def stt(o, a, s, b, op0, op1):
                return dve.scalar_tensor_tensor(o, a, s, b, op0, op1)

            def ts(o, a, s1, s2=None, op0=ALU.mult, op1=None):
                if op1 is None:
                    return dve.tensor_scalar(o, a, s1, None, op0)
                return dve.tensor_scalar(o, a, s1, s2, op0, op1)

            next_piece = [0]

            def stream_to(j):
                while next_piece[0] < min(piece_of[j] + 2, len(pieces)):
                    _, raw, raw_r, hi = pieces[next_piece[0]]
                    next_piece[0] += 1
                    dve.wait_ge(w_hi, next_piece[0])
                    tt(raw_r, raw, hi.bitcast(FP32), ALU.subtract).then_inc(w_lo, 1)

            def lo_of(name, n, o, i, hi):
                dve.wait_ge(sem(name + "_hi"), n + 1)
                return tt(o, i, hi.bitcast(FP32), ALU.subtract)

            def lo_tile(name, n, o, i, hi):
                lo_of(name, n, o[:, n, :], i[:, n, :], hi[:, n, :]).then_inc(sem(name + "_lo"), 1)

            def inverse_root(name, n, ins, o, i):
                ins.then_inc(sem(name + "_ms"), 1)
                dve.wait_ge(sem(name + "_root"), n + 1)
                return dve.reciprocal(o, i)

            def sum_squares(junk, x, n):
                return dve.tensor_tensor_reduce(out=junk, in0=x, in1=x, scale=1.0, scalar=0.0, op0=ALU.mult,
                                                op1=ALU.add, accum_out=stat[:, n:n + 1])

            def norm(n, xn, gain):
                for i in range(TT):
                    m = mark(sum_squares(xn[:, i, :], x_tok[:, i, :], i))
                after(m)
                then(inverse_root("norm", n, ts(stat[:, 4:8], stat[:, 0:4], 1.0 / D, EPS, ALU.mult, ALU.add),
                                  stat[:, 12:16], stat[:, 8:12]))
                for i in range(TT):
                    ins = ts(xn[:, i, :], x_tok[:, i, :], stat[:, 12 + i:13 + i])
                ins.then_inc(sem("norm_scaled"), 1)
                if n == 0:
                    stream_to(base["p1"])
                for k in range(KT):
                    j = base["n%d" % (n + 1)] + k
                    wait_full(dve, j)
                    dve.wait_ge(sem("h_hi"), KT * n + k + 1)
                    read(j, stt(h_lo[:, k, :], ps(j), params(gain, k), h_hi[:, k, :].bitcast(FP32),
                                ALU.mult, ALU.subtract))

            def residual(name, n, y, gain, done):
                junk = 8192 if name == "y1" else 4096
                stream_to(base[name])
                stream_to(base[name] + TT)
                for i in range(TT):
                    for hf in range(2):
                        wait_read(dve, base[name] + 4 * hf + i)
                    m = mark(sum_squares(view(junk + 1024 * i, D), y[:, i, :], i))
                after(m)
                then(inverse_root("post", n, ts(stat[:, 4:8], stat[:, 0:4], 1.0 / D, EPS, ALU.mult, ALU.add),
                                  stat[:, 12:16], stat[:, 8:12]))
                marks = [mark(stt(y[:, i, :], y[:, i, :], stat[:, 12 + i:13 + i], gain, ALU.mult, ALU.mult))
                         for i in range(TT)]
                for i in range(TT):
                    after(marks[i])
                    tt(x_tok[:, i, :], x_tok[:, i, :], y[:, i, :], ALU.add).then_inc(done, 1)

            def attend(name, units, bias, finish):
                order = base[name]
                for s in range(len(units) + LAG_V):
                    if s < len(units):
                        k, att = units[s][1], units[s][4]
                        w = k.shape[1]
                        j = order["S", s]
                        wait_full(dve, j)
                        if s >= 4:
                            wait_full(dve, order["T", s - 4])
                        read(j, dve.tensor_tensor_reduce(
                            out=view(att, 4, T)[:, s % 4, 0:w], in0=ps(j)[:, 0:w], in1=bias(s), scale=1.0,
                            scalar=-3.0e38, op0=ALU.add, op1=ALU.max, accum_out=stat[:, 16 + s % 8:17 + s % 8]))
                        wait_read(dve, j)
                        ts(stat[:, 24 + s % 8:25 + s % 8], stat[:, 16 + s % 8:17 + s % 8], -1.0).then_inc(
                            sem("neg_max"), 1)
                    if s >= LAG_V:
                        u = s - LAG_V
                        j = order["V", u]
                        wait_full(dve, j)
                        then(dve.reciprocal(stat[:, 160:161], stat[:, 152 + u % 8:153 + u % 8]))
                        finish(u, j)

            have(dve, "start")
            dve.wait_ge(x_in, 16 * TT)
            norm(0, norm_1, "pre_norm")
            join(dve)
            m = None
            for n in range(29):
                j = base["p1"] + n
                stream_to(j)
                if n in SILU_NO:
                    s = SILU_NO[n]
                    wait_full(dve, j)
                    dve.wait_ge(sem("silu_sig"), s + 1)
                    read(j, tt(SILU_OUT[n], ps(j), sig[:, s % 2, :], ALU.mult))
                elif n == 2:
                    dve.wait_ge(sem("forget_ready"), 2)
                    ts(f_a, f_a, TINY, None, ALU.max)
            join(dve)
            def key_value(n):
                j = base["hg"] + n
                wait_full(dve, j)
                if n >= 3:
                    dve.wait_ge(sem("hg_scanned"), n - 2)
                read(j, tt(hg_kv[:, n % 3, :], ps(j), k_a[:, n // DH, :], ALU.mult))

            for c in range(2):
                lo_tile("i", c, i_lo, i_a, i_hi)
            key_value(0)
            for n in range(2 * DH):
                if n + 1 < 2 * DH:
                    key_value(n + 1)
                wait_read(dve, base["hg"] + n)
                if n >= 3:
                    dve.wait_ge(sem("hg_qs"), n - 2)
                dve.tensor_tensor_scan(hg_s[:, n % 3, :], f_a[:, n // DH, :], hg_kv[:, n % 3, :], 0.0,
                                       ALU.mult, ALU.add).then_inc(sem("hg_scanned"), 1)
            for c in range(2):
                j = base["hn"] + c
                wait_full(dve, j)
                if c == 0:
                    dve.wait_ge(sem("hg_scanned"), 2 * DH)
                m = ts(hg_kv[:, c, :], ps(j), 1.0 / DH, EPS, ALU.mult, ALU.add)
                read(j, m)
            for c in range(2):
                wait_read(dve, base["hn"] + c)
            then(ts(hg_kv[:, 2, 0:2], hg_kv[:, 0, 0:2], 1.0))
            then(inverse_root("hg", 0, ts(hg_kv[:, 2, 0:2], hg_kv[:, 0, 0:2], 1.0),
                              hg_kv[:, 0:2, :], hg_kv[:, 0:2, :]))
            for c in range(2):
                m = mark(stt(hg_sq[:, c, :], bank[6 + c][:, :], params("hgrn_norm", c), hg_kv[:, c, :],
                             ALU.mult, ALU.mult))
            after(m)
            for c in range(2):
                tt(mix_t[:, c, :], hg_sq[:, c, :], silu_ga[:, c, :], ALU.mult)
            for c in range(2):
                j = base["pool"] + c
                wait_full(dve, j)
                read(j, stt(mix_t[:, 2 + c, :], ps(j), params("pool_scale", c), silu_gb[:, c, :], ALU.mult, ALU.mult))
            join(dve)
            x8, a8, e8, l8, n8 = (v[0:8, :] for v in (fc_x, fc_abs, fc_e, fc_ls, fc_neg))
            stt(a8, x8, -1.0, x8, ALU.mult, ALU.max).then_inc(sem("fox_abs"), 1)
            dve.wait_ge(sem("fox_log"), 1)
            then(stt(l8, x8, 0.0, e8, ALU.min, ALU.subtract))
            then(ts(a8, x8, 0.0, 1.0, ALU.mult, ALU.add))
            dve.tensor_tensor_scan(n8, a8, l8, 0.0, ALU.mult, ALU.subtract).then_inc(sem("fox_decay"), 1)
            for k in range(4):
                lo_tile("mix", k, mix_lo, mix_t, mix_hi)

            def fox_bias(u):
                wait_read(dve, base["fox"]["B", u // TT])
                return fc_tab[:, u // TT, 0:(u % TT + 1) * P]

            def fox_finish(u, j):
                ins = ts(fox_o[:, u % TT, (u // TT) * DH:(u // TT + 1) * DH], ps(j)[:, 0:DH], stat[:, 160:161])
                read(j, ins)
                wait_read(dve, j)

            attend("fox", fox_units(), fox_bias, fox_finish)
            ts(stat[:, 161:162], stat[:, 160:161], 1.0).then_inc(sem("fox_o_ready"), 1)
            for k in range(4):
                j = base["ft"] + k
                wait_full(dve, j)
                read(j, tt(mix_t[:, 4 + k, :], ps(j), silu_gc[:, k, :], ALU.mult))
            for k in range(4, KT):
                lo_tile("mix", k, mix_lo, mix_t, mix_hi)
            have(dve, "y1")
            residual("y1", 0, y_tok1, gain1, sem("x_ready"))
            join(dve)
            norm(1, norm_2, "mix_pre")
            dve.memset(stat[:, 32:33], MID)
            dve.memset(stat[:, 33:34], -MID)
            join(dve)
            have(dve, "rwkv")
            mixes = [0]

            def mix(j, o, mu):
                m = mixes[0]
                mixes[0] += 1
                stream_to(j)
                wait_read(dve, j)
                z = z_pad[:, m % 2, :]
                then(tt(z_d[:, m % 2, :], z[:, 0:512], z[:, 1:513], ALU.subtract))
                stt(o, z_d[:, m % 2, :], mu, z[:, 1:513], ALU.mult, ALU.add).then_inc(sem("mixed"), 1)

            for n, o in enumerate((lo_wa, lo_g1, lo_g2)):
                mix(base["lora"] + n, o, params("mu_lora", n))
            for q in range(4):
                b0 = base["ra", q]
                for n in range(2):
                    mix(b0 + n, r_q[:, n, :], params("mu_rkv", 2 * q + n))
                for n in range(2):
                    mix(b0 + 2 + n, k_q[:, n, :], params("mu_rkv", 8 + 2 * q + n))
                for n in range(2):
                    mix(b0 + 4 + n, v_q[:, n, :], params("mu_rkv", 16 + 2 * q + n))
                dve.wait_ge(sem("mixed"), 3 + 6 * (q + 1))
                for n in range(2):
                    m = mark(ts(kk_q[:, n, :], k_q[:, n, :], params("k_k", 2 * q + n)))
                after(m)
                tt(t1_q, kk_q, kk_q, ALU.mult).then_inc(sem("kk_squares"), 1)
                for n in range(2):
                    wait_read(dve, b0 + 6 + n)
                then(ts(lw_q, lw_q, LOG_DECAY))
                for n in range(2):
                    m = mark(dve.tensor_tensor_scan(b_q[:, n, :], m_reset, lw_q[:, n, :], 0.0, ALU.mult, ALU.add))
                after(m)
                tt(pp_q, b_q, lw_q, ALU.subtract).then_inc(sem("decay_sums"), 1)
                for n in range(2):
                    j = b0 + 10 + n
                    wait_full(dve, j)
                    if n == 1:
                        wait_full(dve, b0 + 11)
                    wait_full(dve, b0 + 11)
                    ins = ts(t1_q[:, n, :], ps(j), 1e-24, None, ALU.max)
                    read(j, ins)
                for n in range(2):
                    wait_read(dve, b0 + 10 + n)
                then(inverse_root("kk", q, ts(z_d[:, 0, 0:2], t1_q[:, 0, 0:2], 1.0), t1_q, t1_q))
                m1 = mark(tt(kk_q, kk_q, t1_q, ALU.mult))
                for n in range(2):
                    wait_read(dve, b0 + 8 + n)
                    m = mark(ts(t2_q[:, n, :], av_q[:, n, :], 1.0, params("k_a", 2 * q + n), ALU.subtract, ALU.mult))
                after(m)
                then(stt(k_q, t2_q, 1.0, k_q, ALU.add, ALU.mult))
                for n in range(2):
                    m = mark(ts(t1_q[:, n, :], r_q[:, n, :], params("r_k", 2 * q + n)))
                after(m)
                tt(t1_q, t1_q, k_q, ALU.mult).then_inc(sem("rk_ready"), 1)
                m = mark(tt(t2_q, kk_q, av_q, ALU.mult))
                dve.wait_ge(sem("decays_ready"), q + 1)
                for n in range(2):
                    stt(a_r[:, n, :, 0, :], kk_q[:, n, :].rearrange("p (c t) -> p c t", c=TT), -1.0,
                        pp_q[:, n, :].rearrange("p (c t) -> p c t", c=TT), ALU.mult, ALU.mult)
                    tt(a_r[:, n, :, 1, :], r_q[:, n, :].rearrange("p (c t) -> p c t", c=TT),
                       pm_q[:, n, :].rearrange("p (c t) -> p c t", c=TT), ALU.mult)
                after(m)
                tt(b_h, t2_q, pi_q, ALU.mult)
                tt(k_h, k_q, pi_q, ALU.mult).then_inc(sem("operands_ready"), 1)
                j = b0 + 12
                wait_full(dve, j)
                read(j, dve.tensor_copy(bonus, ps(j)[:, 0:16]))
                join(dve)
                b0 = base["rb", q]
                for c in range(TT):
                    for h in range(4):
                        j = b0 + 6 * c + h
                        wait_full(dve, j)
                        read(j, tt(gram[:, c, h, :], ps(j), m_gram, ALU.mult))
                    for x in range(2):
                        j = b0 + 6 * c + 4 + x
                        wait_full(dve, j)
                        read(j, tt(low[:, c, x:4:2, :], ps(j)[:, 0:256].rearrange("p (h x) -> p h x", h=2),
                                   over(m_low, 2), ALU.mult))

                for lev in range(3):
                    for c in range(TT):
                        if lev < 2:
                            j = powers(q, "b", lev, c)
                            wait_full(dve, j)
                            read(j, dve.tensor_copy(pwt[:, c], ps(j).rearrange("p (h x) -> p h x", h=4)))
                        j = powers(q, "d", lev, c)
                        wait_full(dve, j)
                        o = invt[:, c].rearrange("p h x -> p (h x)")
                        read(j, tt(o, o, ps(j), ALU.add))
                for m in range(3):
                    for c in range(TT):
                        j = merges(q, "y", m, c)
                        wait_full(dve, j)
                        o = later_half(invt[:, c], m)
                        read(j, tt(o, o, ps(j)[:, 0:256].rearrange("p (h n b) -> p h n b", h=4, b=16 << m), ALU.add))
                join(dve)
                b0 = base["rc", q]

                def center(c):
                    y4 = y_q[:, c, :].rearrange("p (h v) -> p h v", v=DH)
                    s4, ms = stat[:, 40:44], stat[:, 56 + 4 * c:60 + 4 * c]
                    wait_read(dve, b0 + 4 + 4 * c)
                    then(dve.reduce_sum(s4, y4, axis=AX.X))
                    then(ts(s4, s4, -1.0 / DH))
                    then(tt(y4, y4, along(s4, DH), ALU.add))
                    then(tt(sq_c, y_q[:, c, :], y_q[:, c, :], ALU.mult))
                    then(dve.reduce_sum(ms, sq_c.rearrange("p (h v) -> p h v", v=DH), axis=AX.X))
                    ts(ms, ms, 1.0 / DH, 64e-5, ALU.mult, ALU.add).then_inc(sem("gn_ms"), 1)

                def normalize(c):
                    y4 = y_q[:, c, :].rearrange("p (h v) -> p h v", v=DH)
                    scale = stat[:, 72 + 4 * c:76 + 4 * c]
                    dve.wait_ge(sem("gn_root"), TT * q + c + 1)
                    then(dve.reciprocal(scale, stat[:, 56 + 4 * c:60 + 4 * c]))
                    then(tt(y4, y4, along(scale, DH), ALU.mult))
                    dve.wait_ge(sem("gates_ready"), q + 1)
                    then(tt(y_q[:, c, :], y_q[:, c, :], g_q[:, c, :], ALU.mult))
                    return tt(y_q[:, c, :], y_q[:, c, :], t3_q[:, c, :], ALU.add)

                for c in range(TT):
                    j = b0 + 3 + 4 * c
                    wait_full(dve, j)
                    read(j, dve.tensor_copy(sa_b, ps(j)[:, 0:256]))
                    if c:
                        center(c - 1)
                    if c < TT - 1:
                        j += 2
                        wait_full(dve, j)
                        for n in range(2):
                            decay = last_p[:, 4 * n + c:4 * n + c + 1]
                            if c == 0:
                                ins = stt(state[:, n, :], ps(j)[:, n * P:(n + 1) * P], decay, head_ones,
                                          ALU.mult, ALU.mult)
                        if c == 0:
                            ins.then_inc(sem("state_ready"), 1)
                            dve.wait_ge(sem("state_ready"), 3 * q + 1)
                            read(j, ts(stat[:, 34:35], stat[:, 32:33], 1.0))
                        else:
                            read(j, tt(st_tmp, ps(j)[:, 0:256], state.rearrange("p n v -> p (n v)"), ALU.add))
                            wait_read(dve, j)
                            for n in range(2):
                                decay = last_p[:, 4 * n + c:4 * n + c + 1]
                                ins = stt(state[:, n, :], st_tmp[:, n * P:(n + 1) * P], decay, head_ones,
                                          ALU.mult, ALU.mult)
                            ins.then_inc(sem("state_ready"), 1)
                    if c:
                        normalize(c - 1)
                center(TT - 1)
                normalize(TT - 1).then_inc(sem("rwkv_o_ready"), 1)
                join(dve)
            for n in range(24):
                stream_to(base["np"] + n)
                if n == 7:
                    have(dve, "nsa")
                    lo_of("gate", 0, gl_lo, gl_w, gl_hi).then_inc(sem("gate_lo"), 1)
            b0 = base["cmp"]
            for hid in (hid_k, hid_v):
                dve.memset(hid[:, :, 31:32], 0.0)
            for n, hid in enumerate((hid_k, hid_v)):
                j = b0 + n
                wait_full(dve, j)
                then(dve.tensor_copy(hb, ps(j)[:, 128:130]))
                read(j, ts(hx, ps(j)[:, 0:124], hb[:, 0:1], None, ALU.add))
                wait_read(dve, j)
                then(tt(h2, hx, hx, ALU.mult))
                then(ts(h2, h2, 0.044715, 1.0, ALU.mult, ALU.add))
                tt(h2, h2, hx, ALU.mult).then_inc(sem("gelu_arg"), 1)
                dve.wait_ge(sem("gelu_sig"), n + 1)
                ins = tt(hid[:, :, 0:31], hx.rearrange("p (g n) -> p g n", g=4), hs.rearrange("p (g n) -> p g n", g=4),
                         ALU.mult)
                if n == 0:
                    ins.then_inc(sem("hidden_ready"), 1)
                    dve.wait_ge(sem("hidden_ready"), 1)
                else:
                    then(ins)
                    for g in range(4):
                        ins = dve.tensor_copy(hid4[:, g], over(hid[:, g, :], 4))
                    ins.then_inc(sem("hidden_ready"), 1)
            j = b0 + 3
            wait_full(dve, j)
            for g in range(4):
                ins = tt(v_bd[:, g], over(ps(j)[:, g * DH:(g + 1) * DH], 4), along(v_mask, DH), ALU.mult)
            read(j, ins)
            wait_read(dve, base["np"] + 24)
            for i in range(TT):
                j = b0 + 4 + 5 * i
                sc = c_sc[:, i % 2, :]
                s3 = sc.rearrange("p (h n) -> p h n", n=32)
                s4 = sc.rearrange("p (g x n) -> p g x n", x=2, n=P)
                bias4 = c_bias[:, i, :].rearrange("p (g x n) -> p g x n", x=2, n=P)
                if i >= 2:
                    wait_full(dve, j - 10 + 2)
                for x in range(2):
                    wait_full(dve, j + x)
                    read(j + x, tt(s4[:, :, x, :], ps(j + x)[:, 0:256].rearrange("p (g n) -> p g n", g=2),
                                   bias4[:, :, x, :], ALU.add))
                for x in range(2):
                    wait_read(dve, j + x)
                then(dve.reduce_max(stat[:, 104:120], s3, axis=AX.X))
                tt(s3, s3, along(stat[:, 104:120], 32), ALU.subtract).then_inc(sem("cmp_shifted"), 1)
                dve.wait_ge(sem("cmp_exp"), i + 1)
                then(tt(s3, s3, over(c_01[:, i, :], 16), ALU.mult))
                then(dve.reduce_sum(stat[:, 120:136], s3, axis=AX.X))
                then(ts(stat[:, 120:136], stat[:, 120:136], TINY, None, ALU.max))
                then(dve.reciprocal(stat[:, 136:152], stat[:, 120:136]))
                then(tt(stat[:, 136:152], stat[:, 136:152], gates[:, i, :].rearrange("p (h b) -> p h b", b=3)[:, :, 0],
                        ALU.mult))
                tt(s3, s3, along(stat[:, 136:152], 32), ALU.mult).then_inc(sem("cmp_probs"), 1)
            join(dve)
            def nsa_bias(u):
                h, i = u // 8, u // 2 % TT
                dve.wait_ge(sem("slopes_ready"), h + 1)
                return tab[:, h % 2, 384 - P * i:512]

            def nsa_finish(u, j):
                h, i, br = u // 8, u // 2 % TT, 1 + u % 2
                then(tt(stat[:, 162:163], stat[:, 160:161], gates[:, i, 3 * h + br:3 * h + br + 1], ALU.mult))
                o = nsa_o[:, i, h * DH:(h + 1) * DH]
                read(j, stt(o, ps(j)[:, 0:DH], stat[:, 162:163], o, ALU.mult, ALU.add))
                wait_read(dve, j)

            attend("nsa", nsa_units(), nsa_bias, nsa_finish)
            ts(stat[:, 161:162], stat[:, 160:161], 1.0).then_inc(sem("nsa_o_ready"), 1)
            for k in range(KT):
                j = base["nt"] + k
                wait_full(dve, j)
                read(j, lo_of("ob", k, ob_lo[:, k, :], ps(j), ob_hi[:, k, :]))
            join(dve)
            for hf in range(2):
                b0 = base["merge"] + 16 * hf
                for c in range(8):
                    stream_to(b0 + c)
                    if hf == 0:
                        lo_tile("oa", c, oa_lo, oa_t, oa_hi)
                for c in range(4):
                    j = b0 + 8 + c
                    stream_to(j)
                    wait_read(dve, b0 + c)
                    wait_full(dve, j)
                    read(j, tt(m_t[:, 4 * hf + c, :], ps(j), sig_a[:, c, :], ALU.mult))
                for c in range(4):
                    j = b0 + 12 + c
                    stream_to(j)
                    wait_read(dve, b0 + 4 + c)
                    wait_full(dve, j)
                    if 4 * hf + c >= 2:
                        dve.wait_ge(sem("merged"), 4 * hf + c - 1)
                    read(j, tt(m_tmp[:, c % 2, :], ps(j), sig_b[:, c, :], ALU.mult))
                    wait_read(dve, j)
                    wait_read(dve, b0 + 8 + c)
                    m = m_t[:, 4 * hf + c, :]
                    tt(m, m, m_tmp[:, c % 2, :], ALU.add).then_inc(sem("merged"), 1)
                    if 4 * hf + c:
                        lo_tile("m", 4 * hf + c - 1, m_lo, m_t, m_hi)
            lo_tile("m", KT - 1, m_lo, m_t, m_hi)
            have(dve, "y2")
            have(dve, "gain2")
            residual("y2", 1, y_tok2, gain2, sem("x_ready"))
            join(dve)
            norm(2, norm_3, "ffn_pre")
            join(dve)
            for n in range(11):
                for m in range(4):
                    u = 4 * n + m
                    tile = 2 * n + m if m < 2 else FF_TILES + 2 * n + m - 2
                    if n and m >= 2:
                        dve.wait_ge(sem("act_ready"), 2 * n)
                    if n and m < 2:
                        dve.wait_ge(sem("act_ready"), 2 * n)
                    z, o = ff_pad[:, u % 4, :], ff_c[:, m, :]
                    cw = 3 * tile
                    stream_to(base["ff"] + u)
                    wait_read(dve, base["ff"] + u)
                    then(ts(o, z[:, 2:514], params("conv_w", cw + 2), params("conv_b", tile), ALU.mult, ALU.add))
                    then(stt(o, z[:, 1:513], params("conv_w", cw + 1), o, ALU.mult, ALU.add))
                    stt(o, z[:, 0:512], params("conv_w", cw), o, ALU.mult, ALU.add).then_inc(sem("conv_done"), 1)
                for m in range(2):
                    dve.wait_ge(sem("ff_sig"), 2 * n + m + 1)
                    then(tt(ff_c[:, m, :], ff_c[:, m, :], ff_s[:, m, :], ALU.mult))
                    if m == 0:
                        dve.wait_ge(sem("conv_done"), 4 * n + 4)
                    tt(act_t[:, 2 * n + m, :], ff_c[:, m, :], ff_c[:, 2 + m, :], ALU.mult).then_inc(sem("act_ready"), 1)
                if n:
                    for m in (2 * n - 2, 2 * n - 1):
                        lo_tile("act", m, act_lo, act_t, act_hi)
            for m in (FF_TILES - 2, FF_TILES - 1):
                lo_tile("act", m, act_lo, act_t, act_hi)
            have(dve, "y3")
            residual("y3", 2, y_tok3, gain3, sem("result_ready"))
            join(dve)


def _constants():
    import numpy as np

    f = np.float32
    p, t = np.arange(P)[:, None], np.arange(512)[None, :]
    c = t[:, :P]
    same = lambda n: (p // n == c // n)
    stay = np.zeros((P, N_CCOLS), f)
    stay[:, 0:128] = p == c
    stay[:, 128:256] = same(DH)
    stay[:, 256:768] = t - 384 - p
    stay[:, 768:1280] = np.where(t - 384 > p, BIG_NEG, 0.0)
    z_sel = np.zeros((P, 192), f)
    z_sel[:DH, 64] = 1
    z_sel[DH:, 128] = 1
    sel_b = np.zeros((P, DH, P), f)
    for v in range(DH):
        sel_b[v, v, :DH] = 1
        sel_b[DH + v, v, DH:] = 1
    inv_count = np.zeros((P, 2, 512), f)
    for g, w in enumerate((2, 4, 8, 16)):
        inv_count[(g % 2) * DH:(g % 2) * DH + DH, g // 2] = 1.0 / np.minimum(t + 1.0, w)
    sel8 = np.zeros((8, 8, P), f)
    for h in range(8):
        sel8[h, h] = 1
    rwkv = np.zeros((P, 1666), f)
    rwkv[:, 0:512] = np.concatenate([p < c, p <= c, p < c, p <= c], 1)
    rwkv[:, 512:640] = c < p
    rwkv[:, 640:768] = same(16)
    for m, n in enumerate((32, 64, 128)):
        rwkv[:, 768 + P * m:896 + P * m] = same(n) & ~same(n // 2)
    rwkv[:, 1152:1664] = t % P != 0
    rwkv[:DH, 1664] = 1
    rwkv[DH:, 1665] = 1
    n = np.arange(32)
    tok = (np.arange(TT)[None, :, None] * P + np.arange(P)[:, None, None]).astype(f)
    seen = (16 * n + 31 <= tok) & (n < CMP_N)
    slopes = 2.0 ** (-8.0 * np.arange(1, 17) / 16)
    bias = -slopes.astype(f)[None, None, :, None] * (tok - (16 * n + 15.5).astype(f))[:, :, None, :]
    bias = np.where(seen[:, :, None, :], bias, BIG_NEG).astype(f)
    v_mask = (p // 32 == np.arange(4)[None, :]).astype(f)
    return {"c_stay": stay, "c_z_sel": z_sel, "c_sel_b": sel_b, "c_inv_count": inv_count, "c_sel8": sel8,
            "c_rwkv": rwkv, "c_cmp_bias": bias.reshape(P, TT, 512), "c_cmp_01": seen.astype(f),
            "c_v_mask": v_mask}


def _layouts(a):
    import numpy as np

    par = np.zeros((P, N_PCOLS), np.float32)

    def put(name, x, parts=P):
        at, n = PCOLS[name]
        par[0:parts, at:at + n] = x

    def by_tile(v):
        return v.reshape(-1, P).T

    mu = a["rwkv_mu_2"][0]
    put("pre_norm", by_tile(a["pre_norm_g"][0]))
    put("mix_pre", by_tile(a["norm_mix_pre_2"][0]))
    put("ffn_pre", by_tile(a["norm_ffn_pre_2"][0]))
    put("hgrn_norm", by_tile(a["hgrn_norm_g"][0]))
    put("pool_scale", by_tile(a["pool_scale"][0]))
    par[96:104, PCOLS["fox_bias"][0]] = a["fox_f_bias"][0]
    put("mu_rkv", by_tile(mu[:3072]))
    at = PCOLS["mu_lora"][0]
    par[:, at:at + 2] = by_tile(mu[3072:3328])
    par[96:128, at + 2] = mu[3328:]
    for name in ("w0", "a0", "k_k", "k_a"):
        put(name, by_tile(a[f"rwkv_{name}_2"][0]))
    put("r_k", by_tile(a["rwkv_r_k_2"][0].reshape(-1)))
    put("conv_w", a["ffn_conv_w_2"][0].reshape(3, 2 * FF_TILES, P).transpose(2, 1, 0).reshape(P, -1))
    put("conv_b", by_tile(a["ffn_conv_b_2"][0]))
    pool_w = np.zeros((P, 2, P), np.float32)
    for g in range(4):
        s = slice((g % 2) * DH, (g % 2) * DH + DH)
        pool_w[s, g // 2, s] = a["pool_w"][0, g]
    return {"c_par": par, "c_pool_w": pool_w,
            "c_lora_w": np.concatenate([a["rwkv_w2_2"][0], a["rwkv_a2_2"][0]], 0),
            "c_pos_k": a["cmp_pos_k_2"][0].reshape(16, 2, DH).transpose(1, 2, 0).reshape(P, 16),
            "c_pos_v": a["cmp_pos_v_2"][0].reshape(16, 2, DH).transpose(1, 2, 0).reshape(P, 16)}


_WHOLE = ["w_in", "w_out", "w_in_2", "rwkv_g2_2", "cmp_w1_k_2", "cmp_w2_k_2", "cmp_w1_v_2", "cmp_w2_v_2",
          "w_branch_rwkv_2", "w_branch_nsa_2", "w_out_2", "ffn_up_2", "ffn_down_2"]
_ROWS = {"g_post": "post_norm_g", "g_mix_post": "norm_mix_post_2", "g_ffn_post": "norm_ffn_post_2",
         "g_ln_w": "rwkv_ln_w_2", "g_ln_b": "rwkv_ln_b_2"}


def kernel(**inputs):
    import numpy as np
    import concourse.bacc as bacc
    from concourse.bass_utils import run_bass_kernel_spmd

    a = {name: np.asarray(v) for name, v in inputs.items()}
    arrays = {"x": a["x"][0], **{name: a[name][0] for name in _WHOLE}, **_layouts(a), **_constants(),
              **{name: a[src] for name, src in _ROWS.items()}}
    arrays = {name: np.ascontiguousarray(v) for name, v in arrays.items()}
    nc = bacc.Bacc("TRN2", target_bir_lowering=False, num_devices=1)
    d = {name: nc.dram_tensor(f"in_{name}", v.shape, FP32, kind="ExternalInput").ap() for name, v in arrays.items()}
    for name in _ROWS:
        d[name] = d[name].broadcast_to([P, D])
    x_saved = nc.dram_tensor("x_saved", [T, D], FP32).ap()
    out = nc.dram_tensor("out_x", [T, D], FP32, kind="ExternalOutput").ap()
    build_program(nc, d, x_saved, out)
    r = run_bass_kernel_spmd(nc, [{f"in_{name}": v for name, v in arrays.items()}], core_ids=[0])
    return np.asarray(r.results[0]["out_x"]).reshape(1, T, D)
```

```python
import concourse.bass as bass
from concourse import mybir
from contextlib import ExitStack

FP32 = mybir.dt.float32
FP32R = mybir.dt.float32r
ALU = mybir.AluOpType
ACT = mybir.ActivationFunctionType
AX = mybir.AxisListType

P = 128
T = 512
TT = T // P
D = 1024
KT = D // P
DH = 64
EPS = 1e-6
TINY = 1e-30
BIG_NEG = -1e30
BANKS, FEW_BANKS = 8, 6
FOX_HEADS = 8
RWKV_COLS = 3360
NSA_COLS = 2608
NSA_HEADS, NSA_GROUPS = 16, 4
D_FF = 2816
FF_TILES = D_FF // P
CMP_N = 31
LOG_DECAY = -0.6065306597126334
MID = 38.8
ARENA = 43200

PCOLS = {}


def _pack(names):
    at = 0
    for name, n in names:
        PCOLS[name] = (at, n)
        at += n
    return at


RAW_SLOTS = 3
SLOT = 2048
PIECE = 1024
RAW_AT = ARENA
HI_AT = RAW_AT + RAW_SLOTS * SLOT
MEMORY = HI_AT + 2 * PIECE

N_PCOLS = _pack([("pre_norm", KT), ("mix_pre", KT), ("ffn_pre", KT), ("hgrn_norm", 2), ("pool_scale", 2),
                 ("fox_bias", 1), ("mu_rkv", 24), ("mu_lora", 3), ("w0", KT), ("a0", KT), ("k_k", KT),
                 ("k_a", KT), ("r_k", KT), ("conv_w", 3 * 2 * FF_TILES), ("conv_b", 2 * FF_TILES)])
CCOLS = {"ident": (0, 128), "head_ones": (128, 128), "dist": (256, 512), "mask": (768, 512)}
N_CCOLS = 1280
LAG_H = 4
LAG_T, LAG_V = 2, 4


def build_program(nc, d, x_saved, out):
    with ExitStack() as ctx:
        sems = {}

        def sem(name):
            if name not in sems:
                sems[name] = ctx.enter_context(nc.semaphore(name))
            return sems[name]

        def tensor(name, words):
            return ctx.enter_context(nc.sbuf_tensor(name, [P, words], FP32))

        const = tensor("const", N_CCOLS)
        par = tensor("par", N_PCOLS)
        stat = tensor("stat", 256)
        start = (nc.sbuf_base + 31) // 32 * 32
        tensor("memory", MEMORY)
        arena = nc.alloc_sbuf_tensor_at("arena", [P, ARENA], FP32, offset=start)
        bank = [ctx.enter_context(nc.psum_tensor(f"bank{b}", [P, 512], FP32)) for b in range(8)]

        def words(dims):
            n = 1
            for x in dims:
                n *= x
            return n

        def view(at, *dims, of=arena):
            n = words(dims)
            v = of[:, at:at + n]
            if len(dims) == 2:
                v = v.rearrange("p (a b) -> p a b", a=dims[0])
            elif len(dims) == 3:
                v = v.rearrange("p (a b c) -> p a b c", a=dims[0], b=dims[1])
            elif len(dims) == 4:
                v = v.rearrange("p (a b c e) -> p a b c e", a=dims[0], b=dims[1], c=dims[2])
            return v

        def named(name, at, *dims, dtype=FP32R):
            return view(0, *dims, of=nc.alloc_sbuf_tensor_at(name, [P, words(dims)], dtype, offset=start + 4 * at))

        raw_ring, raw_ring_r = (nc.alloc_sbuf_tensor_at(name, [P, RAW_SLOTS * SLOT], dtype, offset=start + 4 * RAW_AT)
                                for name, dtype in (("weights", FP32), ("weights_lo", FP32R)))
        hi_ring = nc.alloc_sbuf_tensor_at("weights_hi", [P, 2 * PIECE], FP32R, offset=start + 4 * HI_AT)

        def params(name, k=0, parts=P):
            at = PCOLS[name][0] + k
            return par[0:parts, at:at + 1]

        def cst(name):
            at, n = CCOLS[name]
            return const[:, at:at + n]

        def over(ap, n):
            return ap.unsqueeze(1).broadcast_to([P, n, ap.shape[1]])

        def along(ap, n):
            return ap.unsqueeze(2).broadcast_to([P, ap.shape[1], n])

        ident, head_ones = cst("ident"), cst("head_ones")
        dist, causal = cst("dist"), cst("mask")

        x_tok = view(0, TT, D)
        h_hi, h_lo = named("h_hi", 4096, KT, T), named("h_lo", 8192, KT, T)
        S0 = 12288
        mix_t = named("mix_t", S0, KT, T, dtype=FP32)
        mix_lo, mix_hi = named("mix_lo", S0, KT, T), named("mix_hi", 4096, KT, T)
        at = S0 + 4096
        pool_pad, pool_s = view(S0, 2, 528), view(S0 + 2048, 2, 528)
        q_a, f_a, k_a, _, silu_ga, u_b, silu_gb = (view(at + 1024 * n, 2, T) for n in range(7))
        i_a = named("i_a", at + 3072, 2, T, dtype=FP32)
        i_lo = named("i_lo", at + 3072, 2, T)
        y_tok1 = view(at, TT, D)
        gain1 = view(at + 4096, D)
        at += 7168
        q_c, k_c, silu_gc, v_c = (view(at + 2048 * n, *((4, T) if n < 3 else (TT, 512))) for n in range(4))
        at += 8192
        sig = view(at, 2, T)
        i_hi = named("i_hi", at, 2, T)
        at += 1024
        fc_x = view(at, T)
        at += 512
        pool_w = view(at, 2, P)
        z_sel = view(at + 256, 192)
        inv_count = view(at + 448, 2, T)
        at += 1472
        hg_u = view(4096, 3, T)
        hg_kv = view(4096 + 1536, 3, T)
        fc_neg, fc_abs, fc_ls = (view(4096 + 3072 + 512 * n, T) for n in range(3))
        fc_e = fc_abs
        hg_s = view(4096 + 4608, 3, T)
        hg_sq = view(4096 + 6144, 2, T)
        norm_1 = view(at, TT, D)
        sel_b, sel_r = named("sel_b", at, DH, P, dtype=FP32), named("sel_r", at, DH, P)
        fox_o = view(at, TT, 512)
        fox_att = at + 2048
        sel8 = view(at + 5632, 8, P)
        k_p = view(S0 + 4096, 8, T)
        fc_tab = view(8192, 8, T)
        at += 8192
        assert at <= ARENA, at
        oa_t = named("oa_t", S0, KT, T, dtype=FP32)
        norm_2 = view(S0 + 16384, TT, D)
        at = S0 + 4096
        lo_wa, lo_g1, lo_g2 = view(at, T), view(at + 512, T), view(at + 1024, T)
        at += 1536
        lora_w, g2_a, g2_b = view(at, D), view(at + 1024, D), view(at + 2048, D)
        at += 3072
        masks_at = at
        m_gram, m_low, m_blk = view(at, 512), view(at + 512, P), view(at + 640, P)
        m_e = view(at + 768, 3, P)
        m_reset, head_sel = view(at + 1152, T), view(at + 1664, 2)
        at += 1666 + 2
        a_r = view(at, 2, TT, 2, P)
        b_h, k_h = view(at + 2048, 2, T), view(at + 3072, 2, T)
        at += 4096
        v_tok, b_tok, k_tok = (view(at + 1024 * n, TT, 256) for n in range(3))
        at += 3072
        bonus, last_p = view(at, 16), view(at + 16, 8)
        state = view(at + 24, 2, P)
        rhs_b, sa_b = view(at + 280, 256), view(at + 536, 256)
        st_tmp = view(at + 792, 256)
        at += 1048
        gram = view(at, TT, 4, 512)
        inv, invt = (view(at + 8192 + 2048 * n, TT, 4, P) for n in range(2))
        low, pw = view(0, TT, 4, P), view(2048, TT, 4, P)
        pwt = gram[:, :, :, 0:P]
        r_q, k_q, v_q, lw_q, b_q, pm_q, pi_q, pp_q, av_q, kk_q, t1_q, t2_q = (
            view(1024 * n if n < 4 else at + 1024 * (n - 4), 2, T) for n in range(12))
        z_pad = view(at + 8192, 2, 514)
        z_d = view(at + 8192 + 1028, 2, T)
        y_q, g_q, t3_q = (view(1024 * n, TT, 256) for n in range(3))
        ln_q = view(3072, 2, 256)
        sq_c = view(3584, 256)
        at = S0 + 4096
        q_n = view(at, KT, T)
        ob_hi, ob_lo = named("ob_hi", at, KT, T), named("ob_lo", at + 4096, KT, T)
        at += 4096
        k_s, k_w = view(at, 4, T), view(at + 2048, 4, T)
        v_s, v_w = view(at + 4096, TT, 256), view(at + 5120, TT, 256)
        at += 6144
        xk, xv = view(at, 4, T), view(at + 2048, 4, T)
        nsa_att = at
        at += 4096
        gates, gl_w = view(at, TT, 48), named("gate_w", at + 192, KT, 48, dtype=FP32)
        gl_hi, gl_lo = named("gate_w_hi", at + 576, KT, 48), named("gate_w_lo", at + 192, KT, 48)
        at += 960
        w1k, w1v = view(at, 16, P), view(at + 2048, 16, P)
        tab = view(at, 2, T)
        at += 4096
        w2k, w2v, pos_k, pos_v = view(at, DH), view(at + 64, DH), view(at + 128, 16), view(at + 144, 16)
        at += 160
        hb, hx, h2, hid_k, hid_v = (view(at, 2), view(at + 2, 124), view(at + 126, 124),
                                    view(at + 250, 4, 32), view(at + 378, 4, 32))
        hs = view(at + 506, 124)
        at += 630
        hid4 = view(at, 4, 4, 32)
        k_cmp = view(at + 512, 2, 32)
        at += 576
        v_bd = view(at, 4, 4, DH)
        at += 1024
        c_bias, c_01, v_mask = view(at, TT, 16 * 32), view(at + 2048, TT, 32), view(at + 2176, 4)
        at += 2180
        c_sc, c_pt = view(at, 2, 512), view(at + 1024, 2, 512)
        at += 2048
        assert at <= ARENA, at
        nsa_o = view(0, TT, D)
        oa_hi, oa_lo = named("oa_hi", 0, KT, T), named("oa_lo", S0, KT, T)
        at = S0 + 12288
        sig_a, sig_b = view(at, 4, T), view(at + 2048, 4, T)
        m_t = named("m_t", at + 4096, KT, T, dtype=FP32)
        m_lo, m_hi = named("m_lo", at + 4096, KT, T), named("m_hi", at + 8192, KT, T)
        m_tmp = view(at + 12288, 2, T)
        y_tok2 = view(at + 13312, TT, D)
        gain2 = view(at + 17408, D)
        act_t = named("act_t", S0 + FF_TILES * T, FF_TILES, T, dtype=FP32)
        act_hi, act_lo = named("act_hi", S0, FF_TILES, T), named("act_lo", S0 + FF_TILES * T, FF_TILES, T)
        norm_3 = view(S0, TT, D)
        at = S0 + 2 * FF_TILES * T
        ff_pad = view(at, 4, 514)
        ff_c = named("ff_c", at + 2056, 4, T, dtype=FP32)
        ff_s = named("ff_s", at + 2056 + 2048, 2, T, dtype=FP32)
        gain3 = view(at + 2056 + 3072, D)
        y_tok3 = view(8192, TT, D)

        base = {}
        total = [0]

        def jobs(name, n):
            base[name] = total[0]
            total[0] += n

        def attention_jobs(name, units, tables=False):
            order = {}
            for s in range(units + LAG_V):
                for h in table_heads(s) if tables else ():
                    order["B", h] = total[0]
                    total[0] += 1
                for kind, u in (("S", s), ("T", s - LAG_T), ("V", s - LAG_V)):
                    if 0 <= u < units:
                        order[kind, u] = total[0]
                        total[0] += 1
            base[name] = order

        def table_heads(s):
            return [0, 1] if s == 0 else [s // TT + 1] if s % TT == 0 and s // TT + 1 < FOX_HEADS else []

        jobs("n1", KT)
        jobs("p1", 29)
        jobs("hg", 2 * DH)
        jobs("hn", 2)
        jobs("pool", 2)
        first_of_all_banks = total[0]
        attention_jobs("fox", FOX_HEADS * TT, True)
        jobs("ft", 4)
        jobs("y1", 8)
        jobs("n2", KT)
        jobs("lora", 3)
        for q in range(4):
            jobs(("ra", q), 19)
            jobs(("rb", q), 92)
            jobs(("rc", q), 19)
        for name, n in (("kcvc", 4), ("q", 8), ("gates", 1), ("hidden", 2), ("ks", 2), ("blocks", 2),
                        (("cs", 0), 2), ("vs", 4), (("cv", 0), 3), (("cs", 1), 2), ("kw", 2), (("cv", 1), 3),
                        (("cs", 2), 2), ("vw", 4), (("cv", 2), 3), (("cs", 3), 2), (("cv", 3), 3)):
            jobs(name, n)
        attention_jobs("nsa", NSA_HEADS * TT * 2)
        jobs("nt", KT)
        jobs("merge", 32)
        jobs("y2", 8)
        jobs("n3", KT)
        jobs("ff", 44)
        jobs("y3", 8)

        RA = {"decay": (0, 1), "a": (2, 3), "k": (4, 5), "r": (6, 9), "kk": (7, 8), "v": (10, 11), "bonus": (12,),
              "tb": (13, 14), "tk": (15, 16), "tv": (17, 18)}

        def ra(q, kind, n=0):
            return base["ra", q] + RA[kind][n]

        def powers(q, kind, lev, c):
            b1 = base["rb", q] + 24 + 12 * lev
            return b1 + {"a": c, "b": 4 + 2 * c, "d": (5 + 2 * c) if lev < 2 else 4 + c}[kind]

        def merges(q, kind, m, c):
            b1 = base["rb", q] + 60 + 12 * m
            return base["rb", q] + 56 + c if m < 0 else b1 + {"u": 0, "y": 4, "x": 8}[kind] + c

        def later_half(t, m):
            return t.rearrange("p h (n two b) -> p h n two b", two=2, b=16 << m)[:, :, :, 1, :]

        full = [sem(f"bank_full{b}") for b in range(BANKS)]
        free = [sem(f"bank_free{b}") for b in range(BANKS)]

        def bank_use(j):
            if j < first_of_all_banks:
                return j % FEW_BANKS, j // FEW_BANKS
            b, n = (j - first_of_all_banks) % BANKS, (j - first_of_all_banks) // BANKS
            return b, n + ((first_of_all_banks - b + FEW_BANKS - 1) // FEW_BANKS if b < FEW_BANKS else 0)

        def ps(j):
            return bank[bank_use(j)[0]][:, :]

        def wait_full(eng, j):
            b, n = bank_use(j)
            eng.wait_ge(full[b], n + 1)

        def wait_read(eng, j):
            b, n = bank_use(j)
            eng.wait_ge(free[b], n + 1)

        def claim(pe, j):
            b, n = bank_use(j)
            if n:
                pe.wait_ge(free[b], n)

        def cols(w, a, b):
            return w.rearrange("(k p) c -> p k c", p=P)[:, :, a:b]

        uses = []
        pieces = []
        released = []
        piece_of = {}
        token_reads = [0]

        def add_use(loads, k, width, cuts, releases):
            n = len(uses)
            at = (n % RAW_SLOTS) * SLOT
            raw, raw_r = view(at, k, width, of=raw_ring), view(at, k, width, of=raw_ring_r)
            uses.append([(raw[:, :, a:a + src.shape[2]], src) for a, src in loads])
            for (ks, cs), (how, value) in zip(cuts, releases):
                p = len(pieces)
                nk, nc_ = ks.stop - ks.start, cs.stop - cs.start
                hi = view((p % 2) * PIECE, nk, nc_, of=hi_ring)
                pieces.append((n, raw[:, ks, cs], raw_r[:, ks, cs], hi))
                released.append((how, value))
                if how == "job":
                    piece_of[value] = p

        def channels(job, *loads, apart=1):
            width = sum(src.shape[2] for _, src in loads)
            cuts = [(slice(0, KT), slice(a, min(a + P, width))) for a in range(0, width, P)]
            add_use(loads, KT, width, cuts, [("job", job + apart * n) for n in range(len(cuts))])

        def tokens(job, w, a, width, rows=D):
            per_piece = PIECE // width
            k = 0
            while k < rows // P:
                nk = min(2 * per_piece, rows // P - k)
                src = w[k * P:(k + nk) * P, a:a + width].rearrange("(k p) c -> p k c", p=P)
                cuts = [(slice(x, x + per_piece), slice(0, width)) for x in range(0, nk, per_piece)]
                last = k + nk == rows // P
                ends = []
                for n in range(len(cuts)):
                    if last and n == len(cuts) - 1:
                        ends.append(("job", job + TT - 1))
                    else:
                        token_reads[0] += 1
                        ends.append(("read", token_reads[0]))
                add_use([(0, src)], nk, width, cuts, ends)
                k += nk
            for i in range(TT - 1):
                piece_of[job + i] = piece_of[job + TT - 1]

        w1, w2 = d["w_in"], d["w_in_2"]
        b0 = base["p1"]
        for n in range(10):
            channels(b0 + 2 * n, (0, cols(w1, 256 * n, 256 * n + 256)))
        tokens(b0 + 20, w1, 2560, 512)
        for n in range(2):
            channels(b0 + 24 + 2 * n, (0, cols(w1, 3072 + 256 * n, 3328 + 256 * n)))
        channels(b0 + 28, (0, cols(w1, 3592 - 104, 3592)))
        for hf in range(2):
            tokens(base["y1"] + 4 * hf, d["w_out"], 512 * hf, 512)
        channels(base["lora"], (0, cols(w2, 3072, 3328)))
        channels(base["lora"] + 2, (0, cols(w2, RWKV_COLS - P, RWKV_COLS)))
        for q in range(4):
            for m, kind in ((1, "k"), (0, "r"), (2, "v")):
                channels(ra(q, kind), (0, cols(w2, 1024 * m + 256 * q, 1024 * m + 256 * q + 256)),
                         apart=ra(q, kind, 1) - ra(q, kind))
        nb = RWKV_COLS
        for n in range(2):
            channels(base["kcvc"] + 2 * n, (0, cols(w2, nb + 1024 + 256 * n, nb + 1280 + 256 * n)))
        for n in range(4):
            loads = []
            for x in range(2):
                for half in range(2):
                    a = nb + (2 * (n // 2) + half) * 256 + (2 * (n % 2) + x) * DH
                    loads.append((x * P + half * DH, cols(w2, a, a + DH)))
            channels(base["q"] + 2 * n, *loads)
        channels(base["ks"], (0, cols(w2, nb + 1536, nb + 1792)))
        tokens(base["vs"], w2, nb + 1792, 256)
        channels(base["kw"], (0, cols(w2, nb + 2048, nb + 2304)))
        tokens(base["vw"], w2, nb + 2304, 256)
        zg = RWKV_COLS + NSA_COLS
        for hf in range(2):
            for m, (w, a) in enumerate(((w2, zg), (w2, zg + D), (d["w_branch_rwkv_2"], 0), (d["w_branch_nsa_2"], 0))):
                for n in range(2):
                    c0 = a + 512 * hf + 256 * n
                    channels(base["merge"] + 16 * hf + 4 * m + 2 * n, (0, cols(w, c0, c0 + 256)))
        for hf in range(2):
            tokens(base["y2"] + 4 * hf, d["w_out_2"], 512 * hf, 512)
        for n in range(11):
            for m in range(2):
                channels(base["ff"] + 4 * n + 2 * m,
                         (0, cols(d["ffn_up_2"], D_FF * m + 256 * n, D_FF * m + 256 * n + 256)))
        for hf in range(2):
            tokens(base["y3"] + 4 * hf, d["ffn_down_2"], 512 * hf, 512, rows=D_FF)

        loaded_at = []
        for n, loads in enumerate(uses):
            loaded_at.append(16 * len(loads) + (loaded_at[n - RAW_SLOTS] if n >= RAW_SLOTS else 0))
        w_loaded = [sem(f"w_loaded{n}") for n in range(RAW_SLOTS)]
        w_hi, w_lo, w_read = sem("w_hi"), sem("w_lo"), sem("w_read")

        def wait_released(eng, p):
            how, value = released[p]
            if how == "job":
                wait_full(eng, value)
            else:
                eng.wait_ge(w_read, value)

        phase_done = sem("phase_done")

        def counter():
            count = [0]

            def join(eng):
                count[0] += 1
                eng.drain().then_inc(phase_done, 1)
                eng.wait_ge(phase_done, 4 * count[0])
            return join

        x_in, x_out = [sem(f"x_in{i}") for i in range(TT)], sem("x_out")
        load_total = {}

        def phase_loads(act, name, pairs):
            for dst, src in pairs:
                act.dma_start(dst, src).then_inc(sem("loaded_" + name), 16)

        def plan_loads(name, pairs):
            load_total[name] = 16 * len(pairs)
            return pairs

        def have(eng, name, times=1):
            eng.wait_ge(sem("loaded_" + name), load_total[name] * times)

        L_START = plan_loads("start", [(const[:, :], d["c_stay"]), (par[:, :], d["c_par"]),
                                       (pool_w, d["c_pool_w"]),
                                       (z_sel, d["c_z_sel"]), (inv_count, d["c_inv_count"])])
        L_SEL = plan_loads("sel", [(sel_b, d["c_sel_b"])])
        L_FOX = plan_loads("fox", [(sel8[0:8], d["c_sel8"])])
        L_Y1 = plan_loads("y1", [(gain1, d["g_post"])])
        L_RW = plan_loads("rwkv", [(lora_w, d["c_lora_w"]), (g2_a, d["rwkv_g2_2"][0:128, :]),
                                   (g2_b[96:128], d["rwkv_g2_2"][128:160, :]),
                                   (view(masks_at, 1666), d["c_rwkv"])])
        L_LN = [plan_loads("ln", [(ln_q[:, 0, :], d["g_ln_w"][:, 256 * q:256 * q + 256]),
                                       (ln_q[:, 1, :], d["g_ln_b"][:, 256 * q:256 * q + 256])])
                for q in range(4)]
        L_NSA = plan_loads("nsa", [(gl_w, cols(w2, RWKV_COLS + 2560, RWKV_COLS + 2608)),
                                   (w1k, d["cmp_w1_k_2"].rearrange("(j p) m -> p j m", p=P)),
                                   (w1v, d["cmp_w1_v_2"].rearrange("(j p) m -> p j m", p=P)),
                                   (w2k, d["cmp_w2_k_2"]), (w2v, d["cmp_w2_v_2"]),
                                   (pos_k, d["c_pos_k"]), (pos_v, d["c_pos_v"]),
                                   (c_bias, d["c_cmp_bias"]), (c_01, d["c_cmp_01"]), (v_mask, d["c_v_mask"])])
        L_Y2 = plan_loads("y2", [(x_tok, x_saved.rearrange("(i p) c -> p i c", p=P))])
        L_G2 = plan_loads("gain2", [(gain2, d["g_mix_post"])])
        L_Y3 = plan_loads("y3", [(gain3, d["g_ffn_post"])])

        SILU = ([(n, q_a[:, n, :]) for n in (0, 1)] + [(6 + n, silu_ga[:, n, :]) for n in (0, 1)]
                + [(10 + n, silu_gb[:, n, :]) for n in (0, 1)] + [(24 + n, silu_gc[:, n, :]) for n in range(4)])
        SILU_NO = {n: s for s, (n, _) in enumerate(SILU)}
        SILU_OUT = dict(SILU)

        def nsa_place(h):
            g, hg = h // 4, h % 4
            return slice((g % 2) * DH, (g % 2) * DH + DH), (g // 2) * 4 + hg

        def fox_units():
            units = []
            for h in range(FOX_HEADS):
                tile = h // 2
                for i in range(TT):
                    w = (i + 1) * P
                    units.append((q_c[:, tile, i * P:(i + 1) * P], k_p[:, h, 0:w], (ident, causal[:, 384:512]),
                                  [v_c[:, x, h * DH:(h + 1) * DH] for x in range(i + 1)], fox_att))
            return units

        def nsa_units():
            units = []
            for h in range(NSA_HEADS):
                half, tile = nsa_place(h)
                g = h // 4
                for i in range(TT):
                    w = (i + 1) * P
                    for k, v in ((k_s, v_s), (k_w, v_w)):
                        units.append((q_n[:, tile, i * P:(i + 1) * P], k[:, g, 0:w], None,
                                      [v[:, x, g * DH:(g + 1) * DH] for x in range(i + 1)], nsa_att))
            return units

        ATT = {"fox": 0, "nsa": FOX_HEADS * TT}

        block = ctx.enter_context(nc.Block())

        @block.sync
        def _(sp):
            for i in (0, 2, 1, 3):
                sp.dma_start(x_tok[:, i, :], d["x"][i * P:(i + 1) * P, :]).then_inc(x_in[i], 16)
            for n, loads in enumerate(uses):
                if n >= RAW_SLOTS:
                    wait_released(sp, [p for p in range(len(pieces)) if pieces[p][0] == n - RAW_SLOTS][-1])
                for dst, src in loads:
                    sp.dma_start(dst, src).then_inc(w_loaded[n % RAW_SLOTS], 16)
            for i in range(TT):
                sp.wait_ge(sem("result_ready"), i + 1)
                sp.dma_start(out[i * P:(i + 1) * P, :], x_tok[:, i, :]).then_inc(sem("result_out"), 16)
            sp.wait_ge(sem("result_out"), 16 * TT)

        @block.tensor
        def _(pe):
            join = counter()

            def mm(o, w, x, first=True, last=True):
                return pe.matmul(o, w, x, start=first, stop=last)

            def fill(j, ins):
                ins.then_inc(full[bank_use(j)[0]], 1)

            def transposes(j, tiles, width=P):
                claim(pe, j)
                for i, t in enumerate(tiles):
                    ins = pe.transpose(ps(j)[:, i * P:(i + 1) * P], t, ident)
                fill(j, ins)

            def mm3(o, w, x, first, last):
                mm(o, w[0], x[0], first, False)
                mm(o, w[0], x[1], False, False)
                return mm(o, w[1], x[0], False, last)

            taken = [0]

            def take_piece():
                _, _, lo, hi = pieces[taken[0]]
                taken[0] += 1
                pe.wait_ge(w_lo, taken[0])
                return hi, lo

            def to_channels(j, x):
                w = take_piece()
                claim(pe, j)
                for k in range(KT):
                    ins = mm3(ps(j)[0:w[0].shape[2], :], [v[:, k, :] for v in w], [v[:, k, :] for v in x],
                              k == 0, k == KT - 1)
                fill(j, ins)

            def to_tokens(j0, x, width, ready=None):
                k0, kt = 0, x[0].shape[1]
                while k0 < kt:
                    w = take_piece()
                    k1 = k0 + w[0].shape[1]
                    if ready:
                        pe.wait_ge(sem(ready), k1)
                    for i in range(TT):
                        if k0 == 0:
                            claim(pe, j0 + i)
                        for k in range(k0, k1):
                            ins = mm3(ps(j0 + i)[:, 0:width], [v[:, k, i * P:(i + 1) * P] for v in x],
                                      [v[:, k - k0, :] for v in w], k == 0, k == kt - 1)
                        if k1 == kt:
                            fill(j0 + i, ins)
                    if k1 < kt:
                        ins.then_inc(w_read, 1)
                    k0 = k1

            def norm(n, xn):
                pe.wait_ge(sem("norm_scaled"), n + 1)
                pe.wait_ge(sem("norm_scaled_act"), n + 1)
                for k in range(KT):
                    transposes(base["n%d" % (n + 1)] + k, [xn[:, i, k * P:(k + 1) * P] for i in range(TT)])

            def attend(name, units):
                order = base[name]
                off = ATT[name]
                for s in range(len(units) + LAG_V):
                    for h in table_heads(s) if name == "fox" else ():
                        claim(pe, order["B", h])
                        fill(order["B", h], mm(ps(order["B", h]), sel8[0:8, h, :], fc_neg[0:8, :]))
                    if name == "fox" and s % TT == 0 and s < len(units):
                        pe.wait_ge(sem("fox_zeros"), s // TT + 1)
                        pe.wait_ge(sem("fox_keys"), s // TT + 1)
                    if s < len(units):
                        q, k, extra, _, att = units[s]
                        j = order["S", s]
                        claim(pe, j)
                        w = k.shape[1]
                        ins = mm(ps(j)[:, 0:w], q, k, True, extra is None)
                        if extra is not None:
                            ins = mm(ps(j)[:, w - P:w], extra[0], extra[1], False, True)
                        fill(j, ins)
                    if 0 <= s - LAG_T < len(units):
                        u = s - LAG_T
                        _, k, _, _, att = units[u]
                        pe.wait_ge(sem("probs_ready"), off + u + 1)
                        prob = view(att, 4, T)[:, u % 4, :]
                        transposes(order["T", u], [prob[:, x * P:(x + 1) * P] for x in range(k.shape[1] // P)])
                    if 0 <= s - LAG_V:
                        u = s - LAG_V
                        _, k, _, vals, att = units[u]
                        j = order["V", u]
                        wait_read(pe, order["T", u])
                        claim(pe, j)
                        pt = view(att + 2048, 3, T)[:, u % 3, :]
                        for x, v in enumerate(vals):
                            ins = mm(ps(j)[:, 0:DH], pt[:, x * P:(x + 1) * P], v, x == 0, x == len(vals) - 1)
                        fill(j, ins)

            def project_out(name, x, ready):
                for hf in range(2):
                    to_tokens(base[name] + 4 * hf, x, 512, ready)

            h_both = (h_hi, h_lo)

            have(pe, "start")
            norm(0, norm_1)
            join(pe)
            for n in range(29):
                if n == 20:
                    to_tokens(base["p1"] + n, h_both, 512)
                elif n < 20 or n >= 24:
                    to_channels(base["p1"] + n, h_both)
            join(pe)
            pe.wait_ge(sem("i_lo"), 2)
            for n in range(2 * DH + LAG_H):
                if n < 2 * DH:
                    j = base["hg"] + n
                    claim(pe, j)
                    mm(ps(j), sel_r[:, n % DH, :], i_hi[:, n // DH, :], True, False)
                    fill(j, mm(ps(j), sel_r[:, n % DH, :], i_lo[:, n // DH, :], False, True))
                if n >= LAG_H:
                    m = n - LAG_H
                    pe.wait_ge(sem("hg_qs"), m + 1)
                    v = m % DH
                    mm(bank[6 + m // DH][:, :], z_sel[:, 64 - v:192 - v], hg_u[:, m % 3, :],
                       v == 0, v == DH - 1).then_inc(sem("hg_summed"), 1)
            for c in range(2):
                j = base["hn"] + c
                pe.wait_ge(sem("hg_squares"), c + 1)
                claim(pe, j)
                fill(j, mm(ps(j), head_ones, hg_sq[:, c, :]))
            for c in range(2):
                j = base["pool"] + c
                pe.wait_ge(sem("pooled"), c + 1)
                claim(pe, j)
                fill(j, mm(ps(j), pool_w[:, c, :], pool_s[:, c, 16:528]))
            join(pe)
            have(pe, "fox")
            pe.wait_ge(sem("fox_decay"), 1)
            attend("fox", fox_units())
            pe.wait_ge(sem("fox_o_ready"), 1)
            for k in range(4):
                transposes(base["ft"] + k, [fox_o[:, i, k * P:(k + 1) * P] for i in range(TT)])
            project_out("y1", (mix_hi, mix_lo), "mix_lo")
            join(pe)
            norm(1, norm_2)
            join(pe)
            for n in range(3):
                to_channels(base["lora"] + n, h_both)
            have(pe, "rwkv")
            pe.wait_ge(sem("lora_ready"), 1)
            for q in range(4):
                for n in range(2):
                    j = ra(q, "decay", n)
                    c0 = (2 * q + n) * P
                    claim(pe, j)
                    fill(j, mm(ps(j), lora_w[0:64, c0:c0 + P], lo_wa[0:64, :]))
                for n in range(2):
                    j = ra(q, "a", n)
                    c0 = (2 * q + n) * P
                    claim(pe, j)
                    fill(j, mm(ps(j), lora_w[64:128, c0:c0 + P], lo_wa[64:128, :]))
                for n in range(2):
                    to_channels(ra(q, "k", n), h_both)
                to_channels(ra(q, "r"), h_both)
                pe.wait_ge(sem("kk_squares"), q + 1)
                for n in range(2):
                    j = ra(q, "kk", n)
                    claim(pe, j)
                    fill(j, mm(ps(j), head_ones, t1_q[:, n, :]))
                to_channels(ra(q, "r", 1), h_both)
                for n in range(2):
                    to_channels(ra(q, "v", n), h_both)
                pe.wait_ge(sem("rk_ready"), q + 1)
                j = ra(q, "bonus")
                claim(pe, j)
                for c in range(TT):
                    for n in range(2):
                        ins = mm(ps(j)[:, 4 * c + 2 * n:4 * c + 2 * n + 2], t1_q[:, n, c * P:(c + 1) * P], head_sel)
                fill(j, ins)
                pe.wait_ge(sem("operands_ready"), q + 1)
                for kind, src in (("tb", b_h), ("tk", k_h), ("tv", v_q)):
                    if kind == "tv":
                        pe.wait_ge(sem("mixed"), 3 + 6 * (q + 1))
                    for n in range(2):
                        transposes(ra(q, kind, n), [src[:, n, c * P:(c + 1) * P] for c in range(TT)])
                join(pe)
                b0 = base["rb", q]
                for c in range(TT):
                    for h in range(4):
                        j = b0 + 6 * c + h
                        half, n = slice((h % 2) * DH, (h % 2) * DH + DH), h // 2
                        tok = slice(c * P, (c + 1) * P)
                        claim(pe, j)
                        ar = a_r[half, n, c, :, :].rearrange("p a b -> p (a b)")
                        mm(ps(j)[:, 0:256], b_h[half, n, tok], ar)
                        fill(j, mm(ps(j)[:, 256:512], k_h[half, n, tok], ar))
                    for x in range(2):
                        j = b0 + 6 * c + 4 + x
                        half = slice(x * DH, x * DH + DH)
                        claim(pe, j)
                        for n in range(2):
                            ins = mm(ps(j)[:, n * P:(n + 1) * P], a_r[half, n, c, 0, :], b_h[half, n, tok])
                        fill(j, ins)

                def four(j, w, x, n=P):
                    claim(pe, j)
                    for h in range(4):
                        ins = mm(ps(j)[:, h * n:(h + 1) * n], w[:, h, :], x[:, h])
                    fill(j, ins)

                for lev in range(3):
                    for c in range(TT):
                        if lev == 0:
                            pe.wait_ge(sem("inv_started"), 4 * q + c + 1)
                        else:
                            wait_read(pe, powers(q, "b", lev - 1, c))
                        four(powers(q, "a", lev, c), pwt[:, c], pw[:, c])
                    for c in range(TT):
                        wait_read(pe, powers(q, "a", lev, c))
                        if lev < 2:
                            transposes(powers(q, "b", lev, c), [pw[:, c, h, :] for h in range(4)])
                        if lev:
                            wait_read(pe, powers(q, "d", lev - 1, c))
                        four(powers(q, "d", lev, c), pw[:, c], invt[:, c])
                for c in range(TT):
                    wait_read(pe, powers(q, "d", 2, c))
                    transposes(merges(q, "x", -1, c), [invt[:, c, h, :] for h in range(4)])
                for m in range(3):
                    for c in range(TT):
                        pe.wait_ge(sem("between_ready"), 12 * q + 4 * m + c + 1)
                        if m:
                            wait_read(pe, merges(q, "y", m - 1, c))
                        four(merges(q, "u", m, c), pw[:, c], later_half(invt[:, c], m), 64)
                    for c in range(TT):
                        wait_read(pe, merges(q, "u", m, c))
                        wait_read(pe, merges(q, "x", m - 1, c))
                        four(merges(q, "y", m, c), inv[:, c], pwt[:, c, :, 0:64], 64)
                    if m < 2:
                        for c in range(TT):
                            wait_read(pe, merges(q, "y", m, c))
                            transposes(merges(q, "x", m, c), [invt[:, c, h, :] for h in range(4)])
                join(pe)
                b0 = base["rc", q]
                for n in range(2):
                    j = b0 + n
                    claim(pe, j)
                    for c in range(2):
                        tok = slice((2 * n + c) * P, (2 * n + c + 1) * P)
                        mm(ps(j)[:, c * 256:(c + 1) * 256], lo_g1[:, tok], g2_a[:, 256 * q:256 * q + 256], True, False)
                        ins = mm(ps(j)[:, c * 256:(c + 1) * 256], lo_g2[:, tok],
                                 g2_b[:, 256 * q:256 * q + 256], False, True)
                    fill(j, ins)
                for c in range(TT):
                    j = b0 + 2 + 4 * c
                    if c:
                        pe.wait_ge(sem("state_ready"), 3 * q + c)
                    claim(pe, j)
                    for n in range(2):
                        if c:
                            mm(ps(j)[:, n * P:(n + 1) * P], a_r[:, n, c, 0, :], state[:, n, :], True, False)
                        for h in (2 * n, 2 * n + 1):
                            ins = mm(ps(j)[:, h * DH:(h + 1) * DH], gram[:, c, h, 256:384],
                                     v_tok[:, c, h * DH:(h + 1) * DH], c == 0, c == 0 or h % 2 == 1)
                    fill(j, ins)
                    wait_read(pe, j)
                    j += 1
                    claim(pe, j)
                    for h in range(4):
                        ins = mm(ps(j)[:, h * DH:(h + 1) * DH], invt[:, c, h, :], rhs_b[:, h * DH:(h + 1) * DH])
                    fill(j, ins)
                    wait_read(pe, j)
                    j += 1
                    claim(pe, j)
                    for n in range(2):
                        if c:
                            mm(ps(j)[:, n * P:(n + 1) * P], a_r[:, n, c, 1, :], state[:, n, :], True, False)
                        for h in (2 * n, 2 * n + 1):
                            hv = slice(h * DH, (h + 1) * DH)
                            mm(ps(j)[:, hv], gram[:, c, h, 128:256], sa_b[:, hv], c == 0, False)
                            ins = mm(ps(j)[:, hv], gram[:, c, h, 384:512], v_tok[:, c, hv], False,
                                     c == 0 or h % 2 == 1)
                    fill(j, ins)
                    if c < TT - 1:
                        j += 1
                        claim(pe, j)
                        for n in range(2):
                            ch = slice(n * P, (n + 1) * P)
                            mm(ps(j)[:, ch], b_tok[:, c, ch], sa_b[:, ch], True, False)
                            ins = mm(ps(j)[:, ch], k_tok[:, c, ch], v_tok[:, c, ch], False, True)
                        fill(j, ins)
                pe.wait_ge(sem("rwkv_o_ready"), q + 1)
                for n in range(2):
                    transposes(b0 + 17 + n, [y_q[:, c, n * P:(n + 1) * P] for c in range(TT)])
                join(pe)
            for n in range(4):
                to_channels(base["kcvc"] + n, h_both)
            for n in range(8):
                to_channels(base["q"] + n, h_both)
            have(pe, "nsa")
            pe.wait_ge(sem("gate_lo"), 1)
            j = base["gates"]
            claim(pe, j)
            for i in range(TT):
                for k in range(KT):
                    ins = mm3(ps(j)[:, 48 * i:48 * i + 48], [v[:, k, i * P:(i + 1) * P] for v in h_both],
                              (gl_hi[:, k, :], gl_lo[:, k, :]), k == 0, k == KT - 1)
            fill(j, ins)
            for m, (w1, x, pos) in enumerate(((w1k, xk, pos_k), (w1v, xv, pos_v))):
                j = base["hidden"] + m
                for n in range(2):
                    wait_read(pe, base["kcvc"] + 2 * m + n)
                claim(pe, j)
                for t in range(16):
                    mm(ps(j)[:, 0:124], w1[:, t, :], x[:, :, 2 * t:2 * t + 16 * CMP_N - 15:16], t == 0, t == 15)
                for t in range(16):
                    ins = mm(ps(j)[:, 128:130], w1[:, t, :], pos[:, t:t + 1].broadcast_to([P, 2]), t == 0, t == 15)
                fill(j, ins)
            for n in range(2):
                to_channels(base["ks"] + n, h_both)
            j = base["blocks"]
            pe.wait_ge(sem("hidden_ready"), 1)
            claim(pe, j)
            fill(j, mm(ps(j)[0:64, 0:128], w2k, hid_k.rearrange("p g n -> p (g n)")))
            pe.wait_ge(sem("hidden_ready"), 2)
            claim(pe, j + 1)
            for g in range(4):
                ins = mm(ps(j + 1)[:, g * DH:(g + 1) * DH], hid4[:, g].rearrange("p h n -> p (h n)"), w2v)
            fill(j + 1, ins)
            for n in range(8):
                wait_read(pe, base["q"] + n)
            wait_read(pe, base["blocks"])
            wait_read(pe, base["blocks"] + 1)

            def block_scores(i):
                for x in range(2):
                    j = base["cs", i] + x
                    claim(pe, j)
                    for n in range(8):
                        half, tile = nsa_place((n // 4) * 8 + x * 4 + n % 4)
                        ins = mm(ps(j)[:, n * 32:(n + 1) * 32], q_n[half, tile, i * P:(i + 1) * P],
                                 k_cmp[half, n // 4, :])
                    fill(j, ins)

            def block_values(i):
                j = base["cv", i]
                pe.wait_ge(sem("cmp_probs"), i + 1)
                transposes(j, [c_sc[:, i % 2, x * P:(x + 1) * P] for x in range(4)])
                wait_read(pe, j)
                for x in range(2):
                    claim(pe, j + 1 + x)
                    for g in (2 * x, 2 * x + 1):
                        ins = mm(ps(j + 1 + x)[:, (g % 2) * 256:(g % 2) * 256 + 256],
                                 c_pt[:, i % 2, g * P:(g + 1) * P], v_bd[:, g].rearrange("p h n -> p (h n)"))
                    fill(j + 1 + x, ins)

            block_scores(0)
            to_tokens(base["vs"], h_both, 256)
            block_values(0)
            block_scores(1)
            for n in range(2):
                to_channels(base["kw"] + n, h_both)
            block_values(1)
            block_scores(2)
            to_tokens(base["vw"], h_both, 256)
            block_values(2)
            block_scores(3)
            block_values(3)
            join(pe)
            attend("nsa", nsa_units())
            pe.wait_ge(sem("nsa_o_ready"), 1)
            for k in range(KT):
                transposes(base["nt"] + k, [nsa_o[:, i, k * P:(k + 1) * P] for i in range(TT)])
            join(pe)
            for hf in range(2):
                for m, x in enumerate((h_both, h_both, (oa_hi, oa_lo), (ob_hi, ob_lo))):
                    if hf == 0 and m == 2:
                        pe.wait_ge(sem("oa_lo"), KT)
                    for c in range(4):
                        to_channels(base["merge"] + 16 * hf + 4 * m + c, x)
            project_out("y2", (m_hi, m_lo), "m_lo")
            join(pe)
            norm(2, norm_3)
            join(pe)
            for n in range(4 * 11):
                to_channels(base["ff"] + n, h_both)
            project_out("y3", (act_hi, act_lo), "act_lo")
            join(pe)


        @block.scalar
        def _(act):
            join = counter()
            act_step = sem("act_step")
            steps = [0]

            def mark(ins):
                ins.then_inc(act_step, 1)
                steps[0] += 1
                return steps[0]

            def run(o, i, f, **kw):
                return act.activation(o, i, f, **kw)

            def read(j, ins):
                ins.then_inc(free[bank_use(j)[0]], 1)

            def copy_out(j, o, scale=1.0, width=512, parts=slice(0, P)):
                wait_full(act, j)
                read(j, run(o, ps(j)[parts, 0:width], ACT.Copy, scale=scale))

            next_piece = [0]

            def stream_to(j):
                while next_piece[0] < min(piece_of[j] + 2, len(pieces)):
                    p = next_piece[0]
                    next_piece[0] += 1
                    n, raw, _, hi = pieces[p]
                    act.wait_ge(w_loaded[n % RAW_SLOTS], loaded_at[n])
                    if p >= 2:
                        wait_released(act, p - 2)
                    run(hi, raw, ACT.Copy).then_inc(w_hi, 1)

            def hi_of(name, o, i):
                run(o, i, ACT.Copy).then_inc(sem(name + "_hi"), 1)

            def norm_hi(n, gain):
                for k in range(KT):
                    j = base["n%d" % (n + 1)] + k
                    wait_full(act, j)
                    run(h_hi[:, k, :], ps(j), ACT.Copy, scale=params(gain, k)).then_inc(sem("h_hi"), 1)

            def norm_tiles(n, xn):
                for i in (2, 3):
                    if n == 0:
                        act.wait_ge(x_in[i], 16)
                    ins = run(xn[:, i, :], x_tok[:, i, :], ACT.Square, accum_out=stat[:, i:i + 1])
                ins.then_inc(sem("norm_squares"), 1)
                root("norm", n, stat[:, 8:12], stat[:, 4:8])
                act.wait_ge(sem("norm_rms"), n + 1)
                for i in (2, 3):
                    ins = run(xn[:, i, :], x_tok[:, i, :], ACT.Copy, scale=stat[:, 12 + i:13 + i])
                ins.then_inc(sem("norm_scaled_act"), 1)

            def root(name, n, o, i):
                act.wait_ge(sem(name + "_ms"), n + 1)
                run(o, i, ACT.Sqrt).then_inc(sem(name + "_root"), 1)

            def attend(name, units):
                order = base[name]
                off = ATT[name]
                for s in range(len(units) + LAG_T):
                    for h in table_heads(s) if name == "fox" else ():
                        copy_out(order["B", h], fc_tab[:, h, :])
                    if s < len(units):
                        k, att = units[s][1], units[s][4]
                        w = k.shape[1]
                        act.wait_ge(sem("neg_max"), off + s + 1)
                        prob = view(att, 4, T)[:, s % 4, 0:w]
                        run(prob, prob, ACT.Exp, bias=stat[:, 24 + s % 8:25 + s % 8],
                            accum_out=stat[:, 152 + s % 8:153 + s % 8]).then_inc(sem("probs_ready"), 1)
                    if s >= LAG_T:
                        u = s - LAG_T
                        k, att = units[u][1], units[u][4]
                        if u >= 3:
                            wait_full(act, order["V", u - 3])
                        copy_out(order["T", u], view(att + 2048, 3, T)[:, u % 3, 0:k.shape[1]],
                                 width=k.shape[1])

            phase_loads(act, "start", L_START)
            norm_tiles(0, norm_1)
            stream_to(base["p1"])
            norm_hi(0, "pre_norm")
            join(act)
            phase_loads(act, "sel", L_SEL)
            for n in range(29):
                j = base["p1"] + n
                stream_to(j)
                if n in SILU_NO:
                    s = SILU_NO[n]
                    if s >= 2:
                        wait_read(act, base["p1"] + SILU[s - 2][0])
                    wait_full(act, j)
                    run(sig[:, s % 2, :], ps(j), ACT.Sigmoid).then_inc(sem("silu_sig"), 1)
                elif n in (2, 3):
                    wait_full(act, j)
                    run(f_a[:, n - 2, :], ps(j), ACT.Sigmoid).then_inc(sem("forget_ready"), 1)
                    read(j, run(k_a[:, n - 2, :], ps(j), ACT.Sigmoid, scale=-1.0))
                elif n in (4, 5):
                    copy_out(j, i_a[:, n - 4, :])
                elif n in (8, 9):
                    copy_out(j, u_b[:, n - 8, :])
                elif n in range(12, 16):
                    copy_out(j, q_c[:, n - 12, :], scale=DH ** -0.5)
                elif n in range(16, 20):
                    copy_out(j, k_c[:, n - 16, :])
                elif n == 28:
                    wait_full(act, j)
                    read(j, run(fc_x[0:8, :], ps(j)[96:104, :], ACT.Identity, bias=params("fox_bias")[96:104]))
                else:
                    copy_out(j, v_c[:, n - 20, :])
                if 8 <= n < 24:
                    have(act, "sel")
                    run(sel_r[:, 4 * n - 32:4 * n - 28, :], sel_b[:, 4 * n - 32:4 * n - 28, :], ACT.Copy)
            join(act)
            for c in range(2):
                hi_of("i", i_hi[:, c, :], i_a[:, c, :])
            act.wait_ge(sem("fox_abs"), 1)
            m = mark(run(fc_e[0:8, :], fc_abs[0:8, :], ACT.Exp, scale=-1.0))
            act.wait_ge(act_step, m)
            run(fc_e[0:8, :], fc_e[0:8, :], ACT.Ln, bias=1.0).then_inc(sem("fox_log"), 1)
            for c in range(2):
                act.wait_ge(sem("hg_summed"), DH * (c + 1))
                run(hg_sq[:, c, :], bank[6 + c][:, :], ACT.Square).then_inc(sem("hg_squares"), 1)
            root("hg", 0, hg_kv[:, 0:2, :], hg_kv[:, 0:2, :])
            join(act)
            phase_loads(act, "fox", L_FOX)
            phase_loads(act, "y1", L_Y1)
            for h in range(FOX_HEADS):
                half = slice((h % 2) * DH, (h % 2) * DH + DH)
                run(k_p[half, h, :], k_c[half, h // 2, :], ACT.Copy).then_inc(sem("fox_keys"), 1)
                if h % 2:
                    hi_of("mix", mix_hi[:, h // 2, :], mix_t[:, h // 2, :])
            attend("fox", fox_units())
            for k in range(4):
                wait_read(act, base["ft"] + k)
                hi_of("mix", mix_hi[:, 4 + k, :], mix_t[:, 4 + k, :])

            def residual(name, n, y):
                for hf in range(2):
                    for i in range(TT):
                        stream_to(base[name] + 4 * hf + i)
                        copy_out(base[name] + 4 * hf + i, y[:, i, hf * 512:(hf + 1) * 512])
                root("post", n, stat[:, 8:12], stat[:, 4:8])

            residual("y1", 0, y_tok1)
            join(act)
            act.dma_start(x_saved.rearrange("(i p) c -> p i c", p=P), x_tok).then_inc(x_out, 16)
            phase_loads(act, "rwkv", L_RW)
            norm_tiles(1, norm_2)
            norm_hi(1, "mix_pre")
            act.wait_ge(x_out, 16)
            join(act)
            mixes = [0]

            def to_mix(j):
                m = mixes[0]
                mixes[0] += 1
                if m >= 2:
                    act.wait_ge(sem("mixed"), m - 1)
                stream_to(j)
                copy_out(j, z_pad[:, m % 2, 1:513])

            act.wait_ge(sem("pads_zero"), 1)
            for n in range(3):
                to_mix(base["lora"] + n)
            act.wait_ge(sem("mixed"), 3)
            run(lo_wa[0:64, :], lo_wa[0:64, :], ACT.Tanh)
            run(lo_g1, lo_g1, ACT.Sigmoid)
            run(lo_g2, lo_g2, ACT.Sigmoid).then_inc(sem("lora_ready"), 1)
            for q in range(4):
                stream_to(ra(q, "k"))
                for n in range(2):
                    j = ra(q, "decay", n)
                    wait_full(act, j)
                    read(j, run(lw_q[:, n, :], ps(j), ACT.Sigmoid, bias=params("w0", 2 * q + n)))
                for n in range(2):
                    j = ra(q, "a", n)
                    wait_full(act, j)
                    read(j, run(av_q[:, n, :], ps(j), ACT.Sigmoid, bias=params("a0", 2 * q + n)))
                act.wait_ge(sem("decay_sums"), q + 1)
                run(pm_q, b_q, ACT.Exp, bias=stat[:, 32:33])
                run(pp_q, pp_q, ACT.Exp, bias=stat[:, 32:33])
                run(last_p, b_q.rearrange("p n (c t) -> p (n c) t", t=P)[:, :, P - 1], ACT.Exp)
                run(pi_q, b_q, ACT.Exp, bias=stat[:, 33:34], scale=-1.0).then_inc(sem("decays_ready"), 1)
                act.wait_ge(sem("pads_zero"), 1 + q)
                for n in range(2):
                    to_mix(ra(q, "k", n))
                to_mix(ra(q, "r"))
                stream_to(ra(q, "r", 1))
                root("kk", q, t1_q, t1_q)
                to_mix(ra(q, "r", 1))
                for n in range(2):
                    to_mix(ra(q, "v", n))
                for kind, dst in (("tb", b_tok), ("tk", k_tok), ("tv", v_tok)):
                    for n in range(2):
                        j = ra(q, kind, n)
                        wait_full(act, j)
                        read(j, run(dst[:, :, n * P:(n + 1) * P],
                                    ps(j).rearrange("p (c x) -> p c x", c=TT), ACT.Copy))
                join(act)
                b0 = base["rb", q]

                def to_heads(j, o, n=P):
                    wait_full(act, j)
                    read(j, run(o, ps(j)[:, 0:4 * n].rearrange("p (h x) -> p h x", h=4), ACT.Copy))

                for lev in range(3):
                    for c in range(TT):
                        to_heads(powers(q, "a", lev, c), pw[:, c])
                for m in range(3):
                    for c in range(TT):
                        to_heads(merges(q, "x", m - 1, c), inv[:, c])
                    for c in range(TT):
                        to_heads(merges(q, "u", m, c), pwt[:, c, :, 0:64], 64)
                join(act)
                phase_loads(act, "ln", L_LN[q])
                b0 = base["rc", q]
                for n in range(2):
                    copy_out(b0 + n, g_q[:, 2 * n:2 * n + 2, :].rearrange("p c x -> p (c x)"))
                for c in range(TT + 1):
                    if c < TT:
                        copy_out(b0 + 2 + 4 * c, rhs_b, width=256)
                    if c:
                        root("gn", TT * q + c - 1, stat[:, 52 + 4 * c:56 + 4 * c], stat[:, 52 + 4 * c:56 + 4 * c])
                    if c < TT:
                        copy_out(b0 + 4 + 4 * c, y_q[:, c, :], width=256)
                for n in range(2):
                    copy_out(b0 + 17 + n, oa_t[:, 2 * q + n, :])
                join(act)
            phase_loads(act, "nsa", L_NSA)
            for m, dst in enumerate((xk, xv)):
                for n in range(2):
                    j = base["kcvc"] + 2 * m + n
                    stream_to(j)
                    wait_full(act, j)
                    run(dst[0:64, 2 * n, :], ps(j)[0:64, :], ACT.Copy)
                    run(dst[64:128, 2 * n, 0:511], ps(j)[0:64, 1:512], ACT.Copy)
                    run(dst[0:64, 2 * n + 1, :], ps(j)[64:128, :], ACT.Copy)
                    read(j, run(dst[64:128, 2 * n + 1, 0:511], ps(j)[64:128, 1:512], ACT.Copy))
            for n in range(8):
                stream_to(base["q"] + n)
                if n == 6:
                    have(act, "nsa")
                    hi_of("gate", gl_hi, gl_w)
                copy_out(base["q"] + n, q_n[:, n, :], scale=DH ** -0.5)
            j = base["gates"]
            wait_full(act, j)
            read(j, run(gates.rearrange("p i g -> p (i g)"), ps(j)[:, 0:192], ACT.Sigmoid))

            def keys_out(name, k):
                for m in range(2):
                    j = base[name] + m
                    stream_to(j)
                    wait_full(act, j)
                    run(k[0:64, 2 * m, :], ps(j)[0:64, :], ACT.Copy)
                    read(j, run(k[64:128, 2 * m + 1, :], ps(j)[64:128, :], ACT.Copy))

            def block_exp(i):
                act.wait_ge(sem("cmp_shifted"), i + 1)
                run(c_sc[:, i % 2, :], c_sc[:, i % 2, :], ACT.Exp).then_inc(sem("cmp_exp"), 1)

            def block_out(i):
                if i >= 2:
                    wait_full(act, base["cv", i - 2] + 2)
                copy_out(base["cv", i], c_pt[:, i % 2, :])
                for x in range(2):
                    copy_out(base["cv", i] + 1 + x, nsa_o[:, i, 512 * x:512 * x + 512])

            stream_to(base["ks"])
            for m in range(2):
                act.wait_ge(sem("gelu_arg"), m + 1)
                run(hs, h2, ACT.Sigmoid, scale=1.5957691216057308).then_inc(sem("gelu_sig"), 1)
            keys_out("ks", k_s)
            j = base["blocks"]
            wait_full(act, j)
            for g in range(4):
                ins = run(k_cmp[(g % 2) * DH:(g % 2) * DH + DH, g // 2, :], ps(j)[0:64, g * 32:(g + 1) * 32], ACT.Copy)
            read(j, ins)
            stream_to(base["vs"])
            block_exp(0)
            for i in range(TT):
                copy_out(base["vs"] + i, v_s[:, i, :], width=256)
            block_out(0)
            stream_to(base["kw"])
            block_exp(1)
            keys_out("kw", k_w)
            block_out(1)
            stream_to(base["vw"])
            block_exp(2)
            for i in range(TT):
                copy_out(base["vw"] + i, v_w[:, i, :], width=256)
            block_out(2)
            block_exp(3)
            block_out(3)
            join(act)
            attend("nsa", nsa_units())
            for k in range(KT):
                wait_full(act, base["nt"] + k)
                hi_of("ob", ob_hi[:, k, :], ps(base["nt"] + k))
            join(act)
            phase_loads(act, "gain2", L_G2)
            for hf in range(2):
                b0 = base["merge"] + 16 * hf
                if hf:
                    act.wait_ge(sem("merged"), 4)
                for m, dst in enumerate((sig_a, sig_b)):
                    for c in range(4):
                        j = b0 + 4 * m + c
                        stream_to(j)
                        wait_full(act, j)
                        read(j, run(dst[:, c, :], ps(j), ACT.Sigmoid))
                        if hf == 0:
                            hi_of("oa", oa_hi[:, 4 * m + c, :], oa_t[:, 4 * m + c, :])
                for c in range(8):
                    stream_to(b0 + 8 + c)
                    if c >= 4:
                        act.wait_ge(sem("merged"), 4 * hf + c - 3)
                        hi_of("m", m_hi[:, 4 * hf + c - 4, :], m_t[:, 4 * hf + c - 4, :])
                    if hf == 1 and c == 4:
                        wait_full(act, b0 + 11)
                        phase_loads(act, "y2", L_Y2)
            residual("y2", 1, y_tok2)
            join(act)
            norm_tiles(2, norm_3)
            norm_hi(2, "ffn_pre")
            join(act)
            phase_loads(act, "y3", L_Y3)
            act.wait_ge(sem("ff_pads"), 1)
            for n in range(11):
                for m in range(4):
                    u = 4 * n + m
                    stream_to(base["ff"] + u)
                    if u >= 4:
                        act.wait_ge(sem("conv_done"), u - 3)
                    copy_out(base["ff"] + u, ff_pad[:, u % 4, 2:514])
                if n < 10:
                    stream_to(base["ff"] + 4 * n + 4)
                for m in range(2):
                    act.wait_ge(sem("conv_done"), 4 * n + m + 1)
                    if n:
                        act.wait_ge(sem("act_ready"), 2 * n - 1 + m)
                    run(ff_s[:, m, :], ff_c[:, m, :], ACT.Sigmoid).then_inc(sem("ff_sig"), 1)
                if n:
                    for m in (2 * n - 2, 2 * n - 1):
                        act.wait_ge(sem("act_ready"), m + 1)
                        hi_of("act", act_hi[:, m, :], act_t[:, m, :])
            for m in (FF_TILES - 2, FF_TILES - 1):
                act.wait_ge(sem("act_ready"), m + 1)
                hi_of("act", act_hi[:, m, :], act_t[:, m, :])
            residual("y3", 2, y_tok3)
            join(act)

        @block.gpsimd
        def _(pool):
            join = counter()
            pool_step = sem("pool_step")
            steps = [0]

            def after(ins):
                ins.then_inc(pool_step, 1)
                steps[0] += 1
                pool.wait_ge(pool_step, steps[0])

            def gains(name, n, y, gain):
                for hf in range(2):
                    pool.wait_ge(sem("half_squared"), 2 * n + hf + 1)
                    part = slice(hf * 512, (hf + 1) * 512)
                    for i in range(TT):
                        pool.tensor_tensor(y[:, i, part], y[:, i, part], gain[:, part], ALU.mult).then_inc(
                            sem("gained"), 1)

            join(pool)
            pool.memset(pool_pad[:, :, 0:16], 0.0)
            pool.memset(pool_s[:, :, 0:16], 0.0)
            for c in range(2):
                wait_read(pool, base["p1"] + 8 + c)
                after(pool.tensor_copy(pool_pad[:, c, 16:528], u_b[:, c, :]))
            have(pool, "start")
            for c in range(2):
                a, b = pool_pad[:, c], pool_s[:, c]
                after(pool.tensor_tensor(b[:, 16:528], a[:, 16:528], a[:, 15:527], ALU.add))
                if c == 0:
                    up = slice(64, 128)
                    after(pool.tensor_tensor(a[up, 16:528], b[up, 16:528], b[up, 14:526], ALU.add))
                    after(pool.tensor_copy(b[up, 16:528], a[up, 16:528]))
                else:
                    after(pool.tensor_tensor(a[:, 16:528], b[:, 16:528], b[:, 14:526], ALU.add))
                    after(pool.tensor_tensor(b[:, 16:528], a[:, 16:528], a[:, 12:524], ALU.add))
                    after(pool.tensor_tensor(a[up, 16:528], b[up, 16:528], b[up, 8:520], ALU.add))
                    after(pool.tensor_copy(b[up, 16:528], a[up, 16:528]))
                after(pool.tensor_tensor(b[:, 16:528], b[:, 16:528], inv_count[:, c, :], ALU.mult))
                pool.tensor_tensor(b[:, 16:528], b[:, 16:528], u_b[:, c, :], ALU.subtract).then_inc(sem("pooled"), 1)
            join(pool)
            for n in range(2 * DH):
                pool.wait_ge(sem("hg_scanned"), n + 1)
                if n >= 3:
                    pool.wait_ge(sem("hg_summed"), n - 2)
                pool.tensor_tensor(hg_u[:, n % 3, :], hg_s[:, n % 3, :], q_a[:, n // DH, :],
                                   ALU.mult).then_inc(sem("hg_qs"), 1)
            join(pool)
            for h in range(FOX_HEADS):
                other = slice((1 - h % 2) * DH, (2 - h % 2) * DH)
                pool.memset(k_p[other, h, :], 0.0).then_inc(sem("fox_zeros"), 1)
            have(pool, "y1")
            gains("y1", 0, y_tok1, gain1)
            join(pool)
            join(pool)
            for q in range(4):
                pool.memset(z_pad[:, :, 0:2], 0.0).then_inc(sem("pads_zero"), 1)
                if q == 0:
                    pool.memset(g2_b[0:96, :], 0.0)
                join(pool)
                have(pool, "rwkv")
                for c in range(TT):
                    wait_read(pool, base["rb", q] + 6 * c + 4)
                    wait_read(pool, base["rb", q] + 6 * c + 5)
                    for h in range(4):
                        wait_read(pool, base["rb", q] + 6 * c + h)
                    blk = over(m_blk, 4)
                    after(pool.tensor_tensor(pw[:, c], low[:, c], blk, ALU.mult))
                    after(pool.tensor_tensor(pwt[:, c], gram[:, c, :, 0:128], blk, ALU.mult))
                    pool.tensor_tensor(invt[:, c], pwt[:, c], over(ident, 4), ALU.add).then_inc(
                        sem("inv_started"), 1)
                for m in range(3):
                    for c in range(TT):
                        wait_full(pool, powers(q, "d", 2, c) if m == 0 else merges(q, "u", m - 1, c))
                        pool.tensor_tensor(pw[:, c], low[:, c], over(m_e[:, m, :], 4), ALU.mult).then_inc(
                            sem("between_ready"), 1)
                join(pool)
                have(pool, "ln", q + 1)
                for n in range(2):
                    wait_read(pool, base["rc", q] + n)
                v16, t16 = (x.rearrange("p c (h v) -> p (c h) v", v=DH) for x in (v_tok, t3_q))
                after(pool.tensor_tensor(t16, v16, along(bonus, DH), ALU.mult))
                after(pool.tensor_tensor(t3_q, t3_q, over(ln_q[:, 1, :], TT), ALU.add))
                after(pool.tensor_tensor(t3_q, t3_q, g_q, ALU.mult))
                pool.tensor_tensor(g_q, g_q, over(ln_q[:, 0, :], TT), ALU.mult).then_inc(sem("gates_ready"), 1)
                join(pool)
            for k in (k_s, k_w):
                for g in range(4):
                    pool.memset(k[(1 - g % 2) * DH:(2 - g % 2) * DH, g, :], 0.0)
            join(pool)
            for h in range(NSA_HEADS):
                if h >= 2:
                    wait_read(pool, base["nsa"]["S", 8 * (h - 1) - 1])
                after(pool.tensor_scalar(tab[:, h % 2, :], dist, 2.0 ** (-8.0 * (h + 1) / NSA_HEADS), None, ALU.mult))
                pool.tensor_tensor(tab[:, h % 2, :], tab[:, h % 2, :], causal, ALU.add).then_inc(sem("slopes_ready"), 1)
            join(pool)
            have(pool, "gain2")
            gains("y2", 1, y_tok2, gain2)
            join(pool)
            join(pool)
            pool.memset(ff_pad[:, :, 0:2], 0.0).then_inc(sem("ff_pads"), 1)
            have(pool, "y3")
            gains("y3", 2, y_tok3, gain3)
            join(pool)

        @block.vector
        def _(dve):
            join = counter()
            dve_step = sem("dve_step")
            steps = [0]

            def mark(ins):
                ins.then_inc(dve_step, 1)
                steps[0] += 1
                return steps[0]

            def after(step):
                dve.wait_ge(dve_step, step)

            def then(ins):
                after(mark(ins))

            def read(j, ins):
                ins.then_inc(free[bank_use(j)[0]], 1)

            def tt(o, a, b, op):
                return dve.tensor_tensor(o, a, b, op)

            def stt(o, a, s, b, op0, op1):
                return dve.scalar_tensor_tensor(o, a, s, b, op0, op1)

            def ts(o, a, s1, s2=None, op0=ALU.mult, op1=None):
                if op1 is None:
                    return dve.tensor_scalar(o, a, s1, None, op0)
                return dve.tensor_scalar(o, a, s1, s2, op0, op1)

            next_piece = [0]

            def stream_to(j):
                while next_piece[0] < min(piece_of[j] + 2, len(pieces)):
                    _, raw, raw_r, hi = pieces[next_piece[0]]
                    next_piece[0] += 1
                    dve.wait_ge(w_hi, next_piece[0])
                    tt(raw_r, raw, hi.bitcast(FP32), ALU.subtract).then_inc(w_lo, 1)

            def lo_of(name, n, o, i, hi):
                dve.wait_ge(sem(name + "_hi"), n + 1)
                return tt(o, i, hi.bitcast(FP32), ALU.subtract)

            def lo_tile(name, n, o, i, hi):
                lo_of(name, n, o[:, n, :], i[:, n, :], hi[:, n, :]).then_inc(sem(name + "_lo"), 1)

            def inverse_root(name, n, ins, o, i):
                ins.then_inc(sem(name + "_ms"), 1)
                dve.wait_ge(sem(name + "_root"), n + 1)
                return dve.reciprocal(o, i)

            def sum_squares(junk, x, n):
                return dve.tensor_tensor_reduce(out=junk, in0=x, in1=x, scale=1.0, scalar=0.0, op0=ALU.mult,
                                                op1=ALU.add, accum_out=stat[:, n:n + 1])

            def norm(n, xn, gain):
                for i in range(2):
                    if n == 0:
                        dve.wait_ge(x_in[i], 16)
                    m = mark(sum_squares(xn[:, i, :], x_tok[:, i, :], i))
                after(m)
                dve.wait_ge(sem("norm_squares"), n + 1)
                ts(stat[:, 4:8], stat[:, 0:4], 1.0 / D, EPS, ALU.mult, ALU.add).then_inc(sem("norm_ms"), 1)
                dve.wait_ge(sem("norm_root"), n + 1)
                dve.reciprocal(stat[:, 12:16], stat[:, 8:12]).then_inc(sem("norm_rms"), 1)
                dve.wait_ge(sem("norm_rms"), n + 1)
                for i in range(2):
                    ins = ts(xn[:, i, :], x_tok[:, i, :], stat[:, 12 + i:13 + i])
                ins.then_inc(sem("norm_scaled"), 1)
                if n == 0:
                    stream_to(base["p1"])
                for k in range(KT):
                    j = base["n%d" % (n + 1)] + k
                    wait_full(dve, j)
                    dve.wait_ge(sem("h_hi"), KT * n + k + 1)
                    read(j, stt(h_lo[:, k, :], ps(j), params(gain, k), h_hi[:, k, :].bitcast(FP32),
                                ALU.mult, ALU.subtract))

            def residual(name, n, y, done):
                junk = 8192 if name == "y1" else 4096
                for hf in range(2):
                    stream_to(base[name] + 4 * hf)
                    for i in range(TT):
                        wait_read(dve, base[name] + 4 * hf + i)
                        m = mark(sum_squares(view(junk + 1024 * i + 512 * hf, 512),
                                             y[:, i, hf * 512:(hf + 1) * 512], 168 + 4 * hf + i))
                    after(m)
                    ts(stat[:, 176:177], stat[:, 168:169], 1.0).then_inc(sem("half_squared"), 1)
                then(tt(stat[:, 0:4], stat[:, 168:172], stat[:, 172:176], ALU.add))
                then(inverse_root("post", n, ts(stat[:, 4:8], stat[:, 0:4], 1.0 / D, EPS, ALU.mult, ALU.add),
                                  stat[:, 12:16], stat[:, 8:12]))
                for i in range(TT):
                    dve.wait_ge(sem("gained"), 8 * n + 5 + i)
                    stt(x_tok[:, i, :], y[:, i, :], stat[:, 12 + i:13 + i], x_tok[:, i, :],
                        ALU.mult, ALU.add).then_inc(done, 1)

            def attend(name, units, bias, finish):
                order = base[name]
                for s in range(len(units) + LAG_V):
                    if s < len(units):
                        k, att = units[s][1], units[s][4]
                        w = k.shape[1]
                        j = order["S", s]
                        wait_full(dve, j)
                        if s >= 4:
                            wait_full(dve, order["T", s - 4])
                        read(j, dve.tensor_tensor_reduce(
                            out=view(att, 4, T)[:, s % 4, 0:w], in0=ps(j)[:, 0:w], in1=bias(s), scale=1.0,
                            scalar=-3.0e38, op0=ALU.add, op1=ALU.max, accum_out=stat[:, 16 + s % 8:17 + s % 8]))
                        wait_read(dve, j)
                        ts(stat[:, 24 + s % 8:25 + s % 8], stat[:, 16 + s % 8:17 + s % 8], -1.0).then_inc(
                            sem("neg_max"), 1)
                    if s >= LAG_V:
                        u = s - LAG_V
                        j = order["V", u]
                        wait_full(dve, j)
                        then(dve.reciprocal(stat[:, 160:161], stat[:, 152 + u % 8:153 + u % 8]))
                        finish(u, j)

            have(dve, "start")
            norm(0, norm_1, "pre_norm")
            join(dve)
            m = None
            for n in range(29):
                j = base["p1"] + n
                stream_to(j)
                if n in SILU_NO:
                    s = SILU_NO[n]
                    wait_full(dve, j)
                    dve.wait_ge(sem("silu_sig"), s + 1)
                    read(j, tt(SILU_OUT[n], ps(j), sig[:, s % 2, :], ALU.mult))
                elif n == 2:
                    dve.wait_ge(sem("forget_ready"), 2)
                    ts(f_a, f_a, TINY, None, ALU.max)
            join(dve)
            def key_value(n):
                j = base["hg"] + n
                wait_full(dve, j)
                if n >= 3:
                    dve.wait_ge(sem("hg_scanned"), n - 2)
                read(j, tt(hg_kv[:, n % 3, :], ps(j), k_a[:, n // DH, :], ALU.mult))

            for c in range(2):
                lo_tile("i", c, i_lo, i_a, i_hi)
            x8, a8, e8, l8, n8 = (v[0:8, :] for v in (fc_x, fc_abs, fc_e, fc_ls, fc_neg))
            key_value(0)
            for n in range(2 * DH):
                if n == 4:
                    stt(a8, x8, -1.0, x8, ALU.mult, ALU.max).then_inc(sem("fox_abs"), 1)
                elif n == 12:
                    dve.wait_ge(sem("fox_log"), 1)
                    then(stt(l8, x8, 0.0, e8, ALU.min, ALU.subtract))
                    then(ts(a8, x8, 0.0, 1.0, ALU.mult, ALU.add))
                    dve.tensor_tensor_scan(n8, a8, l8, 0.0, ALU.mult, ALU.subtract).then_inc(sem("fox_decay"), 1)
                if n + 1 < 2 * DH:
                    key_value(n + 1)
                wait_read(dve, base["hg"] + n)
                if n >= 3:
                    dve.wait_ge(sem("hg_qs"), n - 2)
                dve.tensor_tensor_scan(hg_s[:, n % 3, :], f_a[:, n // DH, :], hg_kv[:, n % 3, :], 0.0,
                                       ALU.mult, ALU.add).then_inc(sem("hg_scanned"), 1)
            for c in range(2):
                j = base["hn"] + c
                wait_full(dve, j)
                if c == 0:
                    dve.wait_ge(sem("hg_scanned"), 2 * DH)
                m = ts(hg_kv[:, c, :], ps(j), 1.0 / DH, EPS, ALU.mult, ALU.add)
                read(j, m)
            for c in range(2):
                wait_read(dve, base["hn"] + c)
            then(ts(hg_kv[:, 2, 0:2], hg_kv[:, 0, 0:2], 1.0))
            then(inverse_root("hg", 0, ts(hg_kv[:, 2, 0:2], hg_kv[:, 0, 0:2], 1.0),
                              hg_kv[:, 0:2, :], hg_kv[:, 0:2, :]))
            for c in range(2):
                m = mark(stt(hg_sq[:, c, :], bank[6 + c][:, :], params("hgrn_norm", c), hg_kv[:, c, :],
                             ALU.mult, ALU.mult))
            after(m)
            for c in range(2):
                tt(mix_t[:, c, :], hg_sq[:, c, :], silu_ga[:, c, :], ALU.mult)
            for c in range(2):
                j = base["pool"] + c
                wait_full(dve, j)
                read(j, stt(mix_t[:, 2 + c, :], ps(j), params("pool_scale", c), silu_gb[:, c, :], ALU.mult, ALU.mult))
            join(dve)
            for k in range(4):
                lo_tile("mix", k, mix_lo, mix_t, mix_hi)

            def fox_bias(u):
                wait_read(dve, base["fox"]["B", u // TT])
                return fc_tab[:, u // TT, 0:(u % TT + 1) * P]

            def fox_finish(u, j):
                ins = ts(fox_o[:, u % TT, (u // TT) * DH:(u // TT + 1) * DH], ps(j)[:, 0:DH], stat[:, 160:161])
                read(j, ins)
                wait_read(dve, j)

            attend("fox", fox_units(), fox_bias, fox_finish)
            ts(stat[:, 161:162], stat[:, 160:161], 1.0).then_inc(sem("fox_o_ready"), 1)
            for k in range(4):
                j = base["ft"] + k
                wait_full(dve, j)
                read(j, tt(mix_t[:, 4 + k, :], ps(j), silu_gc[:, k, :], ALU.mult))
            for k in range(4, KT):
                lo_tile("mix", k, mix_lo, mix_t, mix_hi)
            residual("y1", 0, y_tok1, sem("x_ready"))
            join(dve)
            norm(1, norm_2, "mix_pre")
            dve.memset(stat[:, 32:33], MID)
            dve.memset(stat[:, 33:34], -MID)
            join(dve)
            have(dve, "rwkv")
            mixes = [0]

            def mix(j, o, mu):
                m = mixes[0]
                mixes[0] += 1
                stream_to(j)
                wait_read(dve, j)
                z = z_pad[:, m % 2, :]
                then(tt(z_d[:, m % 2, :], z[:, 0:512], z[:, 1:513], ALU.subtract))
                stt(o, z_d[:, m % 2, :], mu, z[:, 1:513], ALU.mult, ALU.add).then_inc(sem("mixed"), 1)

            for n, o in enumerate((lo_wa, lo_g1, lo_g2)):
                mix(base["lora"] + n, o, params("mu_lora", n))
            for q in range(4):
                stream_to(ra(q, "k"))
                for n in range(2):
                    wait_read(dve, ra(q, "decay", n))
                then(ts(lw_q, lw_q, LOG_DECAY))
                for n in range(2):
                    m = mark(dve.tensor_tensor_scan(b_q[:, n, :], m_reset, lw_q[:, n, :], 0.0, ALU.mult, ALU.add))
                after(m)
                tt(pp_q, b_q, lw_q, ALU.subtract).then_inc(sem("decay_sums"), 1)
                for n in range(2):
                    wait_read(dve, ra(q, "a", n))
                    ts(t2_q[:, n, :], av_q[:, n, :], 1.0, params("k_a", 2 * q + n), ALU.subtract, ALU.mult)
                for n in range(2):
                    mix(ra(q, "k", n), k_q[:, n, :], params("mu_rkv", 8 + 2 * q + n))
                dve.wait_ge(sem("mixed"), 3 + 6 * q + 2)
                for n in range(2):
                    m = mark(ts(kk_q[:, n, :], k_q[:, n, :], params("k_k", 2 * q + n)))
                after(m)
                tt(t1_q, kk_q, kk_q, ALU.mult).then_inc(sem("kk_squares"), 1)
                then(stt(k_q, t2_q, 1.0, k_q, ALU.add, ALU.mult))
                mix(ra(q, "r"), r_q[:, 0, :], params("mu_rkv", 2 * q))
                stream_to(ra(q, "r", 1))
                wait_full(dve, ra(q, "kk", 1))
                for n in range(2):
                    j = ra(q, "kk", n)
                    wait_full(dve, j)
                    read(j, ts(t1_q[:, n, :], ps(j), 1e-24, None, ALU.max))
                for n in range(2):
                    wait_read(dve, ra(q, "kk", n))
                then(inverse_root("kk", q, ts(stat[:, 36:38], t1_q[:, 0, 0:2], 1.0), t1_q, t1_q))
                then(tt(kk_q, kk_q, t1_q, ALU.mult))
                mix(ra(q, "r", 1), r_q[:, 1, :], params("mu_rkv", 2 * q + 1))
                dve.wait_ge(sem("mixed"), 3 + 6 * q + 4)
                for n in range(2):
                    m = mark(ts(t1_q[:, n, :], r_q[:, n, :], params("r_k", 2 * q + n)))
                after(m)
                tt(t1_q, t1_q, k_q, ALU.mult).then_inc(sem("rk_ready"), 1)
                then(tt(t2_q, kk_q, av_q, ALU.mult))
                mix(ra(q, "v"), v_q[:, 0, :], params("mu_rkv", 16 + 2 * q))
                stream_to(ra(q, "v", 1))
                dve.wait_ge(sem("decays_ready"), q + 1)
                tt(b_h, t2_q, pi_q, ALU.mult)
                tt(k_h, k_q, pi_q, ALU.mult).then_inc(sem("operands_ready"), 1)
                for n in range(2):
                    stt(a_r[:, n, :, 0, :], kk_q[:, n, :].rearrange("p (c t) -> p c t", c=TT), -1.0,
                        pp_q[:, n, :].rearrange("p (c t) -> p c t", c=TT), ALU.mult, ALU.mult)
                mix(ra(q, "v", 1), v_q[:, 1, :], params("mu_rkv", 17 + 2 * q))
                for n in range(2):
                    tt(a_r[:, n, :, 1, :], r_q[:, n, :].rearrange("p (c t) -> p c t", c=TT),
                       pm_q[:, n, :].rearrange("p (c t) -> p c t", c=TT), ALU.mult)
                j = ra(q, "bonus")
                wait_full(dve, j)
                read(j, dve.tensor_copy(bonus, ps(j)[:, 0:16]))
                join(dve)
                b0 = base["rb", q]
                for c in range(TT):
                    for h in range(4):
                        j = b0 + 6 * c + h
                        wait_full(dve, j)
                        read(j, tt(gram[:, c, h, :], ps(j), m_gram, ALU.mult))
                    for x in range(2):
                        j = b0 + 6 * c + 4 + x
                        wait_full(dve, j)
                        read(j, tt(low[:, c, x:4:2, :], ps(j)[:, 0:256].rearrange("p (h x) -> p h x", h=2),
                                   over(m_low, 2), ALU.mult))

                for lev in range(3):
                    for c in range(TT):
                        if lev < 2:
                            j = powers(q, "b", lev, c)
                            wait_full(dve, j)
                            read(j, dve.tensor_copy(pwt[:, c], ps(j).rearrange("p (h x) -> p h x", h=4)))
                        j = powers(q, "d", lev, c)
                        wait_full(dve, j)
                        o = invt[:, c].rearrange("p h x -> p (h x)")
                        read(j, tt(o, o, ps(j), ALU.add))
                for m in range(3):
                    for c in range(TT):
                        j = merges(q, "y", m, c)
                        wait_full(dve, j)
                        o = later_half(invt[:, c], m)
                        read(j, tt(o, o, ps(j)[:, 0:256].rearrange("p (h n b) -> p h n b", h=4, b=16 << m), ALU.add))
                join(dve)
                b0 = base["rc", q]

                def center(c):
                    y4 = y_q[:, c, :].rearrange("p (h v) -> p h v", v=DH)
                    s4, ms = stat[:, 40:44], stat[:, 56 + 4 * c:60 + 4 * c]
                    wait_read(dve, b0 + 4 + 4 * c)
                    then(dve.reduce_sum(s4, y4, axis=AX.X))
                    then(ts(s4, s4, -1.0 / DH))
                    then(tt(y4, y4, along(s4, DH), ALU.add))
                    then(tt(sq_c, y_q[:, c, :], y_q[:, c, :], ALU.mult))
                    then(dve.reduce_sum(ms, sq_c.rearrange("p (h v) -> p h v", v=DH), axis=AX.X))
                    ts(ms, ms, 1.0 / DH, 64e-5, ALU.mult, ALU.add).then_inc(sem("gn_ms"), 1)

                def normalize(c):
                    y4 = y_q[:, c, :].rearrange("p (h v) -> p h v", v=DH)
                    scale = stat[:, 72 + 4 * c:76 + 4 * c]
                    dve.wait_ge(sem("gn_root"), TT * q + c + 1)
                    then(dve.reciprocal(scale, stat[:, 56 + 4 * c:60 + 4 * c]))
                    then(tt(y4, y4, along(scale, DH), ALU.mult))
                    dve.wait_ge(sem("gates_ready"), q + 1)
                    then(tt(y_q[:, c, :], y_q[:, c, :], g_q[:, c, :], ALU.mult))
                    return tt(y_q[:, c, :], y_q[:, c, :], t3_q[:, c, :], ALU.add)

                for c in range(TT):
                    j = b0 + 3 + 4 * c
                    wait_full(dve, j)
                    read(j, dve.tensor_copy(sa_b, ps(j)[:, 0:256]))
                    if c:
                        center(c - 1)
                    if c < TT - 1:
                        j += 2
                        wait_full(dve, j)
                        for n in range(2):
                            decay = last_p[:, 4 * n + c:4 * n + c + 1]
                            if c == 0:
                                ins = stt(state[:, n, :], ps(j)[:, n * P:(n + 1) * P], decay, head_ones,
                                          ALU.mult, ALU.mult)
                        if c == 0:
                            ins.then_inc(sem("state_ready"), 1)
                            dve.wait_ge(sem("state_ready"), 3 * q + 1)
                            read(j, ts(stat[:, 34:35], stat[:, 32:33], 1.0))
                        else:
                            read(j, tt(st_tmp, ps(j)[:, 0:256], state.rearrange("p n v -> p (n v)"), ALU.add))
                            wait_read(dve, j)
                            for n in range(2):
                                decay = last_p[:, 4 * n + c:4 * n + c + 1]
                                ins = stt(state[:, n, :], st_tmp[:, n * P:(n + 1) * P], decay, head_ones,
                                          ALU.mult, ALU.mult)
                            ins.then_inc(sem("state_ready"), 1)
                    if c:
                        normalize(c - 1)
                center(TT - 1)
                normalize(TT - 1).then_inc(sem("rwkv_o_ready"), 1)
                join(dve)
            for n in range(4):
                stream_to(base["kcvc"] + n)
            for n in range(8):
                stream_to(base["q"] + n)
                if n == 6:
                    have(dve, "nsa")
                    lo_of("gate", 0, gl_lo, gl_w, gl_hi).then_inc(sem("gate_lo"), 1)
            stream_to(base["ks"])
            for hid in (hid_k, hid_v):
                dve.memset(hid[:, :, 31:32], 0.0)
            for n, hid in enumerate((hid_k, hid_v)):
                j = base["hidden"] + n
                wait_full(dve, j)
                then(dve.tensor_copy(hb, ps(j)[:, 128:130]))
                read(j, ts(hx, ps(j)[:, 0:124], hb[:, 0:1], None, ALU.add))
                wait_read(dve, j)
                then(tt(h2, hx, hx, ALU.mult))
                then(ts(h2, h2, 0.044715, 1.0, ALU.mult, ALU.add))
                tt(h2, h2, hx, ALU.mult).then_inc(sem("gelu_arg"), 1)
                dve.wait_ge(sem("gelu_sig"), n + 1)
                ins = tt(hid[:, :, 0:31], hx.rearrange("p (g n) -> p g n", g=4), hs.rearrange("p (g n) -> p g n", g=4),
                         ALU.mult)
                if n == 0:
                    ins.then_inc(sem("hidden_ready"), 1)
                    dve.wait_ge(sem("hidden_ready"), 1)
                else:
                    then(ins)
                    for g in range(4):
                        ins = dve.tensor_copy(hid4[:, g], over(hid[:, g, :], 4))
                    ins.then_inc(sem("hidden_ready"), 1)
            stream_to(base["ks"] + 1)
            j = base["blocks"] + 1
            wait_full(dve, j)
            for g in range(4):
                ins = tt(v_bd[:, g], over(ps(j)[:, g * DH:(g + 1) * DH], 4), along(v_mask, DH), ALU.mult)
            read(j, ins)
            wait_read(dve, base["gates"])
            for i in range(TT):
                for j in ([base["vs"]], [base["kw"]], [base["kw"] + 1, base["vw"]], [])[i]:
                    stream_to(j)
                j = base["cs", i]
                sc = c_sc[:, i % 2, :]
                s3 = sc.rearrange("p (h n) -> p h n", n=32)
                s4 = sc.rearrange("p (g x n) -> p g x n", x=2, n=P)
                bias4 = c_bias[:, i, :].rearrange("p (g x n) -> p g x n", x=2, n=P)
                if i >= 2:
                    wait_full(dve, base["cv", i - 2])
                for x in range(2):
                    wait_full(dve, j + x)
                    read(j + x, tt(s4[:, :, x, :], ps(j + x)[:, 0:256].rearrange("p (g n) -> p g n", g=2),
                                   bias4[:, :, x, :], ALU.add))
                for x in range(2):
                    wait_read(dve, j + x)
                then(dve.reduce_max(stat[:, 104:120], s3, axis=AX.X))
                tt(s3, s3, along(stat[:, 104:120], 32), ALU.subtract).then_inc(sem("cmp_shifted"), 1)
                dve.wait_ge(sem("cmp_exp"), i + 1)
                then(tt(s3, s3, over(c_01[:, i, :], 16), ALU.mult))
                then(dve.reduce_sum(stat[:, 120:136], s3, axis=AX.X))
                then(ts(stat[:, 120:136], stat[:, 120:136], TINY, None, ALU.max))
                then(dve.reciprocal(stat[:, 136:152], stat[:, 120:136]))
                then(tt(stat[:, 136:152], stat[:, 136:152], gates[:, i, :].rearrange("p (h b) -> p h b", b=3)[:, :, 0],
                        ALU.mult))
                tt(s3, s3, along(stat[:, 136:152], 32), ALU.mult).then_inc(sem("cmp_probs"), 1)
            join(dve)
            def nsa_bias(u):
                h, i = u // 8, u // 2 % TT
                dve.wait_ge(sem("slopes_ready"), h + 1)
                return tab[:, h % 2, 384 - P * i:512]

            def nsa_finish(u, j):
                h, i, br = u // 8, u // 2 % TT, 1 + u % 2
                then(tt(stat[:, 162:163], stat[:, 160:161], gates[:, i, 3 * h + br:3 * h + br + 1], ALU.mult))
                o = nsa_o[:, i, h * DH:(h + 1) * DH]
                read(j, stt(o, ps(j)[:, 0:DH], stat[:, 162:163], o, ALU.mult, ALU.add))
                wait_read(dve, j)

            attend("nsa", nsa_units(), nsa_bias, nsa_finish)
            ts(stat[:, 161:162], stat[:, 160:161], 1.0).then_inc(sem("nsa_o_ready"), 1)
            for k in range(KT):
                j = base["nt"] + k
                wait_full(dve, j)
                read(j, lo_of("ob", k, ob_lo[:, k, :], ps(j), ob_hi[:, k, :]))
            join(dve)
            for hf in range(2):
                b0 = base["merge"] + 16 * hf
                for c in range(8):
                    stream_to(b0 + c)
                    if hf == 0:
                        lo_tile("oa", c, oa_lo, oa_t, oa_hi)
                for c in range(4):
                    j = b0 + 8 + c
                    stream_to(j)
                    wait_read(dve, b0 + c)
                    wait_full(dve, j)
                    read(j, tt(m_t[:, 4 * hf + c, :], ps(j), sig_a[:, c, :], ALU.mult))
                for c in range(4):
                    j = b0 + 12 + c
                    stream_to(j)
                    wait_read(dve, b0 + 4 + c)
                    wait_full(dve, j)
                    if 4 * hf + c >= 2:
                        dve.wait_ge(sem("merged"), 4 * hf + c - 1)
                    read(j, tt(m_tmp[:, c % 2, :], ps(j), sig_b[:, c, :], ALU.mult))
                    wait_read(dve, j)
                    wait_read(dve, b0 + 8 + c)
                    m = m_t[:, 4 * hf + c, :]
                    tt(m, m, m_tmp[:, c % 2, :], ALU.add).then_inc(sem("merged"), 1)
                    if 4 * hf + c:
                        lo_tile("m", 4 * hf + c - 1, m_lo, m_t, m_hi)
            lo_tile("m", KT - 1, m_lo, m_t, m_hi)
            have(dve, "y2")
            residual("y2", 1, y_tok2, sem("x_ready"))
            join(dve)
            norm(2, norm_3, "ffn_pre")
            join(dve)
            for n in range(11):
                for m in range(4):
                    u = 4 * n + m
                    tile = 2 * n + m if m < 2 else FF_TILES + 2 * n + m - 2
                    if n and m >= 2:
                        dve.wait_ge(sem("act_ready"), 2 * n)
                    if n and m < 2:
                        dve.wait_ge(sem("act_ready"), 2 * n)
                    z, o = ff_pad[:, u % 4, :], ff_c[:, m, :]
                    cw = 3 * tile
                    stream_to(base["ff"] + u)
                    wait_read(dve, base["ff"] + u)
                    then(ts(o, z[:, 2:514], params("conv_w", cw + 2), params("conv_b", tile), ALU.mult, ALU.add))
                    then(stt(o, z[:, 1:513], params("conv_w", cw + 1), o, ALU.mult, ALU.add))
                    stt(o, z[:, 0:512], params("conv_w", cw), o, ALU.mult, ALU.add).then_inc(sem("conv_done"), 1)
                if n < 10:
                    stream_to(base["ff"] + 4 * n + 4)
                for m in range(2):
                    dve.wait_ge(sem("ff_sig"), 2 * n + m + 1)
                    then(tt(ff_c[:, m, :], ff_c[:, m, :], ff_s[:, m, :], ALU.mult))
                    if m == 0:
                        dve.wait_ge(sem("conv_done"), 4 * n + 4)
                    tt(act_t[:, 2 * n + m, :], ff_c[:, m, :], ff_c[:, 2 + m, :], ALU.mult).then_inc(sem("act_ready"), 1)
                if n:
                    for m in (2 * n - 2, 2 * n - 1):
                        lo_tile("act", m, act_lo, act_t, act_hi)
            for m in (FF_TILES - 2, FF_TILES - 1):
                lo_tile("act", m, act_lo, act_t, act_hi)
            residual("y3", 2, y_tok3, sem("result_ready"))
            join(dve)


def _constants():
    import numpy as np

    f = np.float32
    p, t = np.arange(P)[:, None], np.arange(512)[None, :]
    c = t[:, :P]
    same = lambda n: (p // n == c // n)
    stay = np.zeros((P, N_CCOLS), f)
    stay[:, 0:128] = p == c
    stay[:, 128:256] = same(DH)
    stay[:, 256:768] = t - 384 - p
    stay[:, 768:1280] = np.where(t - 384 > p, BIG_NEG, 0.0)
    z_sel = np.zeros((P, 192), f)
    z_sel[:DH, 64] = 1
    z_sel[DH:, 128] = 1
    sel_b = np.zeros((P, DH, P), f)
    for v in range(DH):
        sel_b[v, v, :DH] = 1
        sel_b[DH + v, v, DH:] = 1
    inv_count = np.zeros((P, 2, 512), f)
    for g, w in enumerate((2, 4, 8, 16)):
        inv_count[(g % 2) * DH:(g % 2) * DH + DH, g // 2] = 1.0 / np.minimum(t + 1.0, w)
    sel8 = np.zeros((8, 8, P), f)
    for h in range(8):
        sel8[h, h] = 1
    rwkv = np.zeros((P, 1666), f)
    rwkv[:, 0:512] = np.concatenate([p < c, p <= c, p < c, p <= c], 1)
    rwkv[:, 512:640] = c < p
    rwkv[:, 640:768] = same(16)
    for m, n in enumerate((32, 64, 128)):
        rwkv[:, 768 + P * m:896 + P * m] = same(n) & ~same(n // 2)
    rwkv[:, 1152:1664] = t % P != 0
    rwkv[:DH, 1664] = 1
    rwkv[DH:, 1665] = 1
    n = np.arange(32)
    tok = (np.arange(TT)[None, :, None] * P + np.arange(P)[:, None, None]).astype(f)
    seen = (16 * n + 31 <= tok) & (n < CMP_N)
    slopes = 2.0 ** (-8.0 * np.arange(1, 17) / 16)
    bias = -slopes.astype(f)[None, None, :, None] * (tok - (16 * n + 15.5).astype(f))[:, :, None, :]
    bias = np.where(seen[:, :, None, :], bias, BIG_NEG).astype(f)
    v_mask = (p // 32 == np.arange(4)[None, :]).astype(f)
    return {"c_stay": stay, "c_z_sel": z_sel, "c_sel_b": sel_b, "c_inv_count": inv_count, "c_sel8": sel8,
            "c_rwkv": rwkv, "c_cmp_bias": bias.reshape(P, TT, 512), "c_cmp_01": seen.astype(f),
            "c_v_mask": v_mask}


def _layouts(a):
    import numpy as np

    par = np.zeros((P, N_PCOLS), np.float32)

    def put(name, x, parts=P):
        at, n = PCOLS[name]
        par[0:parts, at:at + n] = x

    def by_tile(v):
        return v.reshape(-1, P).T

    mu = a["rwkv_mu_2"][0]
    put("pre_norm", by_tile(a["pre_norm_g"][0]))
    put("mix_pre", by_tile(a["norm_mix_pre_2"][0]))
    put("ffn_pre", by_tile(a["norm_ffn_pre_2"][0]))
    put("hgrn_norm", by_tile(a["hgrn_norm_g"][0]))
    put("pool_scale", by_tile(a["pool_scale"][0]))
    par[96:104, PCOLS["fox_bias"][0]] = a["fox_f_bias"][0]
    put("mu_rkv", by_tile(mu[:3072]))
    at = PCOLS["mu_lora"][0]
    par[:, at:at + 2] = by_tile(mu[3072:3328])
    par[96:128, at + 2] = mu[3328:]
    for name in ("w0", "a0", "k_k", "k_a"):
        put(name, by_tile(a[f"rwkv_{name}_2"][0]))
    put("r_k", by_tile(a["rwkv_r_k_2"][0].reshape(-1)))
    put("conv_w", a["ffn_conv_w_2"][0].reshape(3, 2 * FF_TILES, P).transpose(2, 1, 0).reshape(P, -1))
    put("conv_b", by_tile(a["ffn_conv_b_2"][0]))
    pool_w = np.zeros((P, 2, P), np.float32)
    for g in range(4):
        s = slice((g % 2) * DH, (g % 2) * DH + DH)
        pool_w[s, g // 2, s] = a["pool_w"][0, g]
    return {"c_par": par, "c_pool_w": pool_w,
            "c_lora_w": np.concatenate([a["rwkv_w2_2"][0], a["rwkv_a2_2"][0]], 0),
            "c_pos_k": a["cmp_pos_k_2"][0].reshape(16, 2, DH).transpose(1, 2, 0).reshape(P, 16),
            "c_pos_v": a["cmp_pos_v_2"][0].reshape(16, 2, DH).transpose(1, 2, 0).reshape(P, 16)}


_WHOLE = ["w_in", "w_out", "w_in_2", "rwkv_g2_2", "cmp_w1_k_2", "cmp_w2_k_2", "cmp_w1_v_2", "cmp_w2_v_2",
          "w_branch_rwkv_2", "w_branch_nsa_2", "w_out_2", "ffn_up_2", "ffn_down_2"]
_ROWS = {"g_post": "post_norm_g", "g_mix_post": "norm_mix_post_2", "g_ffn_post": "norm_ffn_post_2",
         "g_ln_w": "rwkv_ln_w_2", "g_ln_b": "rwkv_ln_b_2"}


def kernel(**inputs):
    import numpy as np
    import concourse.bacc as bacc
    from concourse.bass_utils import run_bass_kernel_spmd

    a = {name: np.asarray(v) for name, v in inputs.items()}
    arrays = {"x": a["x"][0], **{name: a[name][0] for name in _WHOLE}, **_layouts(a), **_constants(),
              **{name: a[src] for name, src in _ROWS.items()}}
    arrays = {name: np.ascontiguousarray(v) for name, v in arrays.items()}
    nc = bacc.Bacc("TRN2", target_bir_lowering=False, num_devices=1)
    d = {name: nc.dram_tensor(f"in_{name}", v.shape, FP32, kind="ExternalInput").ap() for name, v in arrays.items()}
    for name in _ROWS:
        d[name] = d[name].broadcast_to([P, D])
    x_saved = nc.dram_tensor("x_saved", [T, D], FP32).ap()
    out = nc.dram_tensor("out_x", [T, D], FP32, kind="ExternalOutput").ap()
    build_program(nc, d, x_saved, out)
    r = run_bass_kernel_spmd(nc, [{f"in_{name}": v for name, v in arrays.items()}], core_ids=[0])
    return np.asarray(r.results[0]["out_x"]).reshape(1, T, D)
```
